# Optimizing a Trainium2 kernel written in Bass

```python
import math
import jax, jax.numpy as jnp
from jax import lax
import numpy as np

D_MODEL = 1024
BATCH = 1
SEQ = 256
DEPTH = 1

CHUNK = 64
Q_BLOCK = 128
EPS = 1e-6
DA_HEADS = 8
DA_HEAD_DIM = 64
DA_WIDTH = DA_HEADS * 2 * DA_HEAD_DIM
ROPE_THETA = 10000.0
ML_HEADS = 4
ML_WIDTH = D_MODEL
ML_HEAD_DIM = ML_WIDTH // ML_HEADS
CONV_WIDTH = 4
D_FF = 2816
FFN_RES = 0.5
N_MOD = 9


def rmsnorm(x, g):
    x32 = x.astype(jnp.float32)
    y = x32 * lax.rsqrt(jnp.mean(x32 * x32, axis=-1, keepdims=True) + EPS)
    return (y * g.astype(jnp.float32)).astype(x.dtype)

def modulate(xn, shift, scale):
    return xn * (1.0 + scale[:, None, :]) + shift[:, None, :]

def swiglu(u, w_gate, w_up, w_down):
    return (jax.nn.silu(u @ w_gate) * (u @ w_up)) @ w_down

def rope(t):
    S, Dh = t.shape[1], t.shape[-1]
    inv = ROPE_THETA ** (-jnp.arange(0, Dh, 2, dtype=jnp.float32) / Dh)
    ang = jnp.arange(S, dtype=jnp.float32)[:, None] * inv[None, :]
    cos = jnp.cos(ang)[None, :, None, None, :].astype(t.dtype)
    sin = jnp.sin(ang)[None, :, None, None, :].astype(t.dtype)
    t1, t2 = jnp.split(t, 2, axis=-1)
    return jnp.concatenate([t1 * cos - t2 * sin, t1 * sin + t2 * cos], axis=-1)

def diff_attention(q, k, v, lam, g_subln, lambda_init):
    B, S, H, _, Dh = q.shape
    scale = Dh ** -0.5
    q = rope(q)
    k = rope(k)
    nb = S // Q_BLOCK
    qb = jnp.moveaxis(q.reshape(B, nb, Q_BLOCK, H, 2, Dh), 1, 0)
    key_chunk = jnp.arange(S) // CHUNK

    def block(args):
        qi, bi = args
        s = jnp.einsum('bqhcd,bkhcd->bchqk', qi, k,
                       preferred_element_type=jnp.float32) * scale
        q_chunk = (bi * Q_BLOCK + jnp.arange(Q_BLOCK)) // CHUNK
        mask = key_chunk[None, :] <= q_chunk[:, None]
        s = jnp.where(mask, s, -jnp.inf)
        p = jax.nn.softmax(s, axis=-1)
        a = p[:, 0] - lam * p[:, 1]
        return jnp.einsum('bhqk,bkhd->bqhd', a.astype(v.dtype), v)

    o = lax.map(block, (qb, jnp.arange(nb)))
    o = jnp.moveaxis(o, 0, 1).reshape(B, S, H, 2 * Dh)
    o = rmsnorm(o, g_subln) * (1.0 - lambda_init)
    return o.reshape(B, S, H * 2 * Dh)

def causal_conv(x, w, b):
    K, C = w.shape
    y = lax.conv_general_dilated(x, w[:, None, :].astype(x.dtype), window_strides=(1,),
                                 padding=[(K - 1, 0)],
                                 dimension_numbers=('NWC', 'WIO', 'NWC'),
                                 feature_group_count=C)
    return y + b

def mlstm_chunkwise(q, k, v, i_pre, f_pre):
    B, H, S, D = q.shape
    L = CHUNK
    nc = S // L
    out_dtype = v.dtype
    q = q.astype(jnp.float32)
    k = k.astype(jnp.float32) * (D ** -0.5)
    v = v.astype(jnp.float32)
    ig = i_pre.astype(jnp.float32)
    logf = jax.nn.log_sigmoid(f_pre.astype(jnp.float32))

    def to_chunks(t):
        return jnp.moveaxis(t.reshape(B, H, nc, L, *t.shape[3:]), 2, 0)

    tril = jnp.tril(jnp.ones((L, L), dtype=bool))

    def body(carry, inp):
        C, n, m = carry
        qc, kc, vc, ic, fc = inp
        b = jnp.cumsum(fc, axis=-1)
        dmat = jnp.where(tril, b[..., :, None] - b[..., None, :] + ic[..., None, :], -jnp.inf)
        inter = b + m[..., None]
        m_t = jnp.maximum(jnp.max(dmat, axis=-1), inter)
        w = jnp.exp(dmat - m_t[..., None])
        sc = jnp.einsum('bhtd,bhsd->bhts', qc, kc) * w
        w_inter = jnp.exp(inter - m_t)
        num = jnp.einsum('bhts,bhsd->bhtd', sc, vc) + w_inter[..., None] * jnp.einsum('bhtd,bhde->bhte', qc, C)
        den = jnp.sum(sc, axis=-1) + w_inter * jnp.einsum('bhtd,bhd->bht', qc, n)
        h = num / jnp.maximum(jnp.abs(den), jnp.exp(-m_t))[..., None]
        bL = b[..., -1]
        g = bL[..., None] - b + ic
        m_new = jnp.maximum(bL + m, jnp.max(g, axis=-1))
        decay = jnp.exp(bL + m - m_new)
        wk = jnp.exp(g - m_new[..., None])[..., None] * kc
        C_new = decay[..., None, None] * C + jnp.einsum('bhsd,bhse->bhde', wk, vc)
        n_new = decay[..., None] * n + jnp.sum(wk, axis=-2)
        return (C_new, n_new, m_new), h

    init = (jnp.zeros((B, H, D, D), jnp.float32), jnp.zeros((B, H, D), jnp.float32),
            jnp.zeros((B, H), jnp.float32))
    _, hs = lax.scan(body, init, (to_chunks(q), to_chunks(k), to_chunks(v),
                                  to_chunks(ig), to_chunks(logf)))
    hs = jnp.moveaxis(hs, 0, 2).reshape(B, H, S, D)
    return hs.astype(out_dtype)

def mlstm_branch(xm, o_pre, conv_w, conv_b, w_mq, w_mk, w_mv, w_if, b_if, ml_skip, g_mlnorm):
    B, S, _ = xm.shape
    H, Dh = ML_HEADS, ML_HEAD_DIM
    xc = jax.nn.silu(causal_conv(xm, conv_w, conv_b))
    xch = xc.reshape(B, S, H, Dh)
    xmh = xm.reshape(B, S, H, Dh)
    q = jnp.einsum('bshd,hde->bhse', xch, w_mq)
    k = jnp.einsum('bshd,hde->bhse', xch, w_mk)
    v = jnp.einsum('bshd,hde->bhse', xmh, w_mv)
    gates = (jnp.einsum('bhse,heg->bgs', q, w_if[0]) + jnp.einsum('bhse,heg->bgs', k, w_if[1])
             + jnp.einsum('bhse,heg->bgs', v, w_if[2]) + b_if[None, :, None])
    hcell = mlstm_chunkwise(q, k, v, gates[:, :H], gates[:, H:])
    hcell = jnp.swapaxes(hcell, 1, 2)
    hn = rmsnorm(hcell, g_mlnorm.reshape(H, Dh))
    y = (hn + ml_skip.reshape(H, Dh) * xch) * jax.nn.sigmoid(o_pre).reshape(B, S, H, Dh)
    return y.reshape(B, S, H * Dh)

def first_inputs(seed: int = 0) -> dict:
    key = jax.random.key(seed)
    ks = jax.random.split(key, 40)
    L = DEPTH

    def nrm(k, shape, scale):
        return jax.random.normal(k, shape, jnp.float32) * scale

    def gain(k, shape):
        return 1.0 + 0.05 * jax.random.normal(k, shape, jnp.float32)

    in_cols = 3 * DA_WIDTH + 2 * ML_WIDTH + 2 * D_MODEL
    f_bias = jnp.linspace(3.0, 6.0, ML_HEADS, dtype=jnp.float32)
    b_if = jnp.concatenate([nrm(ks[30], (L, ML_HEADS), 0.1),
                            f_bias[None, :] + nrm(ks[31], (L, ML_HEADS), 0.1)], axis=-1)
    return {
        "x": nrm(ks[0], (BATCH, SEQ, D_MODEL), 1.0),
        "c": nrm(ks[1], (BATCH, D_MODEL), 1.0),
        "w_ada": nrm(ks[2], (L, D_MODEL, N_MOD * D_MODEL), D_MODEL ** -0.5),
        "b_ada": nrm(ks[3], (L, N_MOD * D_MODEL), 0.02),
        "g_ff1": gain(ks[4], (L, D_MODEL)),
        "w1_gate": nrm(ks[5], (L, D_MODEL, D_FF), D_MODEL ** -0.5),
        "w1_up": nrm(ks[6], (L, D_MODEL, D_FF), D_MODEL ** -0.5),
        "w1_down": nrm(ks[7], (L, D_FF, D_MODEL), D_FF ** -0.5),
        "g_mix": gain(ks[8], (L, D_MODEL)),
        "w_in": nrm(ks[9], (L, D_MODEL, in_cols), D_MODEL ** -0.5),
        "lambda_q1": nrm(ks[10], (L, DA_HEAD_DIM), 0.1),
        "lambda_k1": nrm(ks[11], (L, DA_HEAD_DIM), 0.1),
        "lambda_q2": nrm(ks[12], (L, DA_HEAD_DIM), 0.1),
        "lambda_k2": nrm(ks[13], (L, DA_HEAD_DIM), 0.1),
        "g_subln": gain(ks[14], (L, 2 * DA_HEAD_DIM)),
        "conv_w": nrm(ks[15], (L, CONV_WIDTH, ML_WIDTH), CONV_WIDTH ** -0.5),
        "conv_b": nrm(ks[16], (L, ML_WIDTH), 0.02),
        "w_mq": nrm(ks[17], (L, ML_HEADS, ML_HEAD_DIM, ML_HEAD_DIM), ML_HEAD_DIM ** -0.5),
        "w_mk": nrm(ks[18], (L, ML_HEADS, ML_HEAD_DIM, ML_HEAD_DIM), ML_HEAD_DIM ** -0.5),
        "w_mv": nrm(ks[19], (L, ML_HEADS, ML_HEAD_DIM, ML_HEAD_DIM), ML_HEAD_DIM ** -0.5),
        "w_if": nrm(ks[20], (L, 3, ML_HEADS, ML_HEAD_DIM, 2 * ML_HEADS), (3 * ML_WIDTH) ** -0.5),
        "b_if": b_if,
        "ml_skip": gain(ks[21], (L, ML_WIDTH)),
        "g_mlnorm": gain(ks[22], (L, ML_WIDTH)),
        "w_proj_a": nrm(ks[23], (L, DA_WIDTH, D_MODEL), DA_WIDTH ** -0.5),
        "w_proj_b": nrm(ks[24], (L, ML_WIDTH, D_MODEL), ML_WIDTH ** -0.5),
        "w_out": nrm(ks[25], (L, D_MODEL, D_MODEL), D_MODEL ** -0.5),
        "g_ff2": gain(ks[26], (L, D_MODEL)),
        "w2_gate": nrm(ks[27], (L, D_MODEL, D_FF), D_MODEL ** -0.5),
        "w2_up": nrm(ks[28], (L, D_MODEL, D_FF), D_MODEL ** -0.5),
        "w2_down": nrm(ks[29], (L, D_FF, D_MODEL), D_FF ** -0.5),
        "g_final": gain(ks[32], (D_MODEL,)),
    }

def first_block(x, c, w_ada, b_ada, g_ff1, w1_gate, w1_up, w1_down, g_mix, w_in,
              lambda_q1, lambda_k1, lambda_q2, lambda_k2, g_subln, conv_w, conv_b,
              w_mq, w_mk, w_mv, w_if, b_if, ml_skip, g_mlnorm, w_proj_a, w_proj_b,
              w_out, g_ff2, w2_gate, w2_up, w2_down, g_final):
    B, S, D = x.shape
    split_idx = list(np.cumsum([DA_WIDTH, DA_WIDTH, DA_WIDTH, ML_WIDTH, ML_WIDTH, D_MODEL])[:])
    h = x
    for l in range(DEPTH):
        lambda_init = 0.8 - 0.6 * math.exp(-0.3 * l)
        mods = jnp.split(jax.nn.silu(c) @ w_ada[l] + b_ada[l], N_MOD, axis=-1)
        sh1, sc1, gt1, sh2, sc2, gt2, sh3, sc3, gt3 = mods

        u = modulate(rmsnorm(h, g_ff1[l]), sh1, sc1)
        h = h + FFN_RES * gt1[:, None, :] * swiglu(u, w1_gate[l], w1_up[l], w1_down[l])

        u = modulate(rmsnorm(h, g_mix[l]), sh2, sc2)
        proj = u @ w_in[l]
        qa, ka, va, xm, o_pre, ga, gb = jnp.split(proj, split_idx, axis=-1)

        lam = (jnp.exp(jnp.sum(lambda_q1[l].astype(jnp.float32) * lambda_k1[l].astype(jnp.float32)))
               - jnp.exp(jnp.sum(lambda_q2[l].astype(jnp.float32) * lambda_k2[l].astype(jnp.float32)))
               + lambda_init)
        ya = diff_attention(qa.reshape(B, S, DA_HEADS, 2, DA_HEAD_DIM),
                            ka.reshape(B, S, DA_HEADS, 2, DA_HEAD_DIM),
                            va.reshape(B, S, DA_HEADS, 2 * DA_HEAD_DIM),
                            lam, g_subln[l], lambda_init)
        yb = mlstm_branch(xm, o_pre, conv_w[l], conv_b[l], w_mq[l], w_mk[l], w_mv[l],
                          w_if[l], b_if[l], ml_skip[l], g_mlnorm[l])
        merged = jax.nn.sigmoid(ga) * (ya @ w_proj_a[l]) + jax.nn.sigmoid(gb) * (yb @ w_proj_b[l])
        h = h + gt2[:, None, :] * (merged @ w_out[l])

        u = modulate(rmsnorm(h, g_ff2[l]), sh3, sc3)
        h = h + FFN_RES * gt3[:, None, :] * swiglu(u, w2_gate[l], w2_up[l], w2_down[l])
    return rmsnorm(h, g_final)


DEPTH_2 = 2

N_A_LAYERS = DEPTH_2 // 2
N_B_LAYERS = DEPTH_2 - N_A_LAYERS
A_HEADS = 8
A_HEAD_DIM = 128
A_WIDTH = A_HEADS * A_HEAD_DIM
A_CONV = 4
A_CHUNK = 64
B_HEADS = 16
B_GROUPS = 2
B_HPG = B_HEADS // B_GROUPS
B_HEAD_DIM = 64
B_WIDTH = B_HEADS * B_HEAD_DIM
N_BRANCH = 3
L_CMP = 32
CMP_STRIDE = 16
CMP_HIDDEN = 256
L_SLC = 64
N_SEL = 16
WINDOW = 512
Q_BLOCK_2 = 64
NUM_BUCKETS = 32
MAX_DISTANCE = 128

NEG_INF = -1e30
SEL_BOOST = 1e9


def rmsnorm_2(x, g):
    xf = x.astype(jnp.float32)
    y = xf * lax.rsqrt(jnp.mean(xf * xf, axis=-1, keepdims=True) + EPS)
    return (y * g.astype(jnp.float32)).astype(x.dtype)

def l2norm(x):
    xf = x.astype(jnp.float32)
    return xf * lax.rsqrt(jnp.sum(xf * xf, axis=-1, keepdims=True) + EPS)

def masked_softmax(logits, mask):
    logits = jnp.where(mask, logits.astype(jnp.float32), NEG_INF)
    m = jnp.max(logits, axis=-1, keepdims=True)
    e = jnp.exp(logits - m) * mask
    return e / jnp.maximum(jnp.sum(e, axis=-1, keepdims=True), 1e-30)

def ada_modulation(c, w, b):
    mod = jax.nn.silu(c) @ w + b
    shift, scale, gate = jnp.split(mod, 3, axis=-1)
    return shift[:, None], scale[:, None], gate[:, None]

def t5_bucket(dist):
    n = jnp.maximum(dist, 0)
    max_exact = NUM_BUCKETS // 2
    nf = jnp.maximum(n, 1).astype(jnp.float32)
    large = max_exact + (jnp.log(nf / max_exact) / math.log(MAX_DISTANCE / max_exact)
                         * (NUM_BUCKETS - max_exact)).astype(jnp.int32)
    large = jnp.minimum(large, NUM_BUCKETS - 1)
    return jnp.where(n < max_exact, n, large)

def causal_depthwise_conv(x, w):
    K = w.shape[0]
    T = x.shape[1]
    xp = jnp.pad(x, ((0, 0), (K - 1, 0), (0, 0)))
    y = xp[:, 0:T] * w[0]
    for k in range(1, K):
        y = y + xp[:, k:k + T] * w[k]
    return y

def chunk_gated_delta_rule(q, k, v, g, beta):
    Bn, T, H, dk = q.shape
    dv = v.shape[-1]
    C = A_CHUNK
    N = T // C

    def chunks(t):
        return t.reshape(Bn, N, C, H, -1).transpose(0, 3, 1, 2, 4)

    q, k, v = chunks(q), chunks(k), chunks(v)
    g = g.reshape(Bn, N, C, H).transpose(0, 3, 1, 2)
    beta = beta.reshape(Bn, N, C, H).transpose(0, 3, 1, 2)
    gc = jnp.cumsum(g, axis=-1)
    incl = np.tril(np.ones((C, C), dtype=bool))
    strict = np.tril(np.ones((C, C), dtype=bool), -1)
    diff = gc[..., :, None] - gc[..., None, :]
    decay = jnp.where(incl, jnp.exp(jnp.where(incl, diff, 0.0)), 0.0)
    kb = k * beta[..., None]
    m = jnp.where(strict, jnp.einsum('bhnid,bhnjd->bhnij', kb, k) * decay, 0.0)
    a_mat = m + jnp.eye(C, dtype=m.dtype)
    rhs = jnp.concatenate([v * beta[..., None], kb * jnp.exp(gc)[..., None]], axis=-1)
    uw = lax.linalg.triangular_solve(a_mat, rhs, left_side=True, lower=True, unit_diagonal=True)
    u, w = uw[..., :dv], uw[..., dv:]
    attn = jnp.einsum('bhnid,bhnjd->bhnij', q, k) * decay
    q_dec = q * jnp.exp(gc)[..., None]
    k_dec = k * jnp.exp(gc[..., -1:] - gc)[..., None]
    g_last = jnp.exp(gc[..., -1])

    def step(S, xs):
        q_n, u_n, w_n, a_n, kd_n, gl_n = xs
        v_new = u_n - jnp.einsum('bhck,bhkv->bhcv', w_n, S)
        o_n = jnp.einsum('bhck,bhkv->bhcv', q_n, S) + jnp.einsum('bhij,bhjv->bhiv', a_n, v_new)
        S = S * gl_n[..., None, None] + jnp.einsum('bhck,bhcv->bhkv', kd_n, v_new)
        return S, o_n

    xs = tuple(jnp.moveaxis(t, 2, 0) for t in (q_dec, u, w, attn, k_dec, g_last))
    S0 = jnp.zeros((Bn, H, dk, dv), jnp.float32)
    _, o = lax.scan(step, S0, xs)
    return o.transpose(1, 0, 3, 2, 4).reshape(Bn, T, H, dv)

def gated_deltanet_layer(h, in_w, conv_w, A_log, dt_bias, onorm_g, out_w):
    Bn, T, _ = h.shape
    proj = h @ in_w
    qkv = jax.nn.silu(causal_depthwise_conv(proj[..., :3 * A_WIDTH], conv_w))
    z = proj[..., 3 * A_WIDTH:4 * A_WIDTH].reshape(Bn, T, A_HEADS, A_HEAD_DIM)
    b = proj[..., 4 * A_WIDTH:4 * A_WIDTH + A_HEADS]
    a = proj[..., 4 * A_WIDTH + A_HEADS:]
    q, k, v = [t.reshape(Bn, T, A_HEADS, A_HEAD_DIM) for t in jnp.split(qkv, 3, axis=-1)]
    q = l2norm(q) * (A_HEAD_DIM ** -0.5)
    k = l2norm(k)
    beta = jax.nn.sigmoid(b.astype(jnp.float32))
    g = -jnp.exp(A_log.astype(jnp.float32)) * jax.nn.softplus(a.astype(jnp.float32) + dt_bias.astype(jnp.float32))
    o = chunk_gated_delta_rule(q, k, v.astype(jnp.float32), g, beta)
    o = rmsnorm_2(o, onorm_g) * jax.nn.silu(z.astype(jnp.float32))
    return o.astype(h.dtype).reshape(Bn, T, A_WIDTH) @ out_w

def nsa_shared_kv(stream, kv_norm_g, kv_w, cmp_pos_k, cmp_pos_v, cmp_k_w1, cmp_k_w2, cmp_v_w1, cmp_v_w2):
    Bn, T, _ = stream.shape
    s = rmsnorm_2(stream, kv_norm_g)
    kv = (s @ kv_w).reshape(Bn, T, 6, B_GROUPS, B_HEAD_DIM).transpose(2, 0, 3, 1, 4)
    n_cmp = (T - L_CMP) // CMP_STRIDE + 1
    idx = np.arange(n_cmp)[:, None] * CMP_STRIDE + np.arange(L_CMP)[None, :]

    def compress(tok, pos, w1, w2):
        blk = tok[:, :, idx] + pos
        return jax.nn.silu(blk.reshape(Bn, B_GROUPS, n_cmp, L_CMP * B_HEAD_DIM) @ w1) @ w2

    k_cmp = compress(kv[0], cmp_pos_k, cmp_k_w1, cmp_k_w2)
    v_cmp = compress(kv[1], cmp_pos_v, cmp_v_w1, cmp_v_w2)
    n_slc = T // L_SLC
    k_slc = kv[2].reshape(Bn, B_GROUPS, n_slc, L_SLC, B_HEAD_DIM)
    v_slc = kv[3].reshape(Bn, B_GROUPS, n_slc, L_SLC, B_HEAD_DIM)
    return k_cmp, v_cmp, k_slc, v_slc, kv[4], kv[5]

def nsa_layer(h, shared, rel_bias, in_w, out_w):
    k_cmp, v_cmp, k_slc, v_slc, k_win, v_win = shared
    Bn, T, _ = h.shape
    proj = h @ in_w
    z = proj[..., B_WIDTH:4 * B_WIDTH].reshape(Bn, T, N_BRANCH, B_HEADS, B_HEAD_DIM)
    gates = jax.nn.sigmoid(proj[..., 4 * B_WIDTH:].astype(jnp.float32)).reshape(Bn, T, N_BRANCH, B_HEADS)
    n_q = T // Q_BLOCK_2
    q = (proj[..., :B_WIDTH] * (B_HEAD_DIM ** -0.5)).reshape(
        Bn, n_q, Q_BLOCK_2, B_GROUPS, B_HPG, B_HEAD_DIM).transpose(1, 0, 3, 4, 2, 5)
    n_cmp = k_cmp.shape[2]
    n_slc = k_slc.shape[2]
    n_sel = min(N_SEL, n_slc)
    cmp_end = jnp.arange(n_cmp) * CMP_STRIDE + (L_CMP - 1)
    cells = np.arange(n_cmp)[:, None] + np.arange(L_CMP // CMP_STRIDE)[None, :]
    overlap = jnp.asarray((cells[:, None, :] // (L_SLC // CMP_STRIDE) == np.arange(n_slc)[None, :, None])
                          .sum(-1).astype(np.float32))
    rb_group = rel_bias.reshape(NUM_BUCKETS, B_GROUPS, B_HPG)
    k_win_p = jnp.pad(k_win, ((0, 0), (0, 0), (WINDOW, 0), (0, 0)))
    v_win_p = jnp.pad(v_win, ((0, 0), (0, 0), (WINDOW, 0), (0, 0)))
    b_idx = jnp.arange(Bn)[:, None, None, None]
    g_idx = jnp.arange(B_GROUPS)[None, :, None, None]
    blk_ids = jnp.arange(n_slc)

    def dense_bias(dist):
        return rel_bias[t5_bucket(dist)].transpose(2, 0, 1).reshape(B_GROUPS, B_HPG, *dist.shape)

    def attend_block(args):
        qb, qi = args
        t = qi * Q_BLOCK_2 + jnp.arange(Q_BLOCK_2)
        d_c = t[:, None] - cmp_end[None, :]
        s_c = jnp.einsum('bghqd,bgcd->bghqc', qb, k_cmp).astype(jnp.float32) + dense_bias(d_c)
        p_c = masked_softmax(s_c, d_c >= 0)
        o_c = jnp.einsum('bghqc,bgcd->bghqd', p_c.astype(v_cmp.dtype), v_cmp)
        imp = jnp.einsum('bghqc,cs->bgqs', p_c, overlap)
        cur = (t // L_SLC)[:, None]
        forced = (blk_ids == 0) | (blk_ids == cur) | (blk_ids == cur - 1)
        imp = jnp.where(forced, SEL_BOOST, jnp.where(blk_ids > cur, -SEL_BOOST, imp))
        _, sel = lax.top_k(imp, n_sel)
        k_sel = k_slc[b_idx, g_idx, sel]
        v_sel = v_slc[b_idx, g_idx, sel]
        d_s = t[:, None, None] - (sel[..., None] * L_SLC + jnp.arange(L_SLC))
        bias_s = jnp.moveaxis(rb_group[t5_bucket(d_s), g_idx[..., None]], -1, 2)
        s_s = jnp.einsum('bghqd,bgqnld->bghqnl', qb, k_sel).astype(jnp.float32) + bias_s
        p_s = masked_softmax(s_s.reshape(Bn, B_GROUPS, B_HPG, Q_BLOCK_2, n_sel * L_SLC),
                             (d_s >= 0).reshape(Bn, B_GROUPS, 1, Q_BLOCK_2, n_sel * L_SLC))
        o_s = jnp.einsum('bghqk,bgqkd->bghqd', p_s.astype(v_sel.dtype),
                         v_sel.reshape(Bn, B_GROUPS, Q_BLOCK_2, n_sel * L_SLC, B_HEAD_DIM))
        q0 = qi * Q_BLOCK_2
        k_w = lax.dynamic_slice_in_dim(k_win_p, q0, WINDOW + Q_BLOCK_2, axis=2)
        v_w = lax.dynamic_slice_in_dim(v_win_p, q0, WINDOW + Q_BLOCK_2, axis=2)
        kpos = q0 - WINDOW + jnp.arange(WINDOW + Q_BLOCK_2)
        d_w = t[:, None] - kpos[None, :]
        mask_w = (d_w >= 0) & (d_w < WINDOW) & (kpos[None, :] >= 0)
        s_w = jnp.einsum('bghqd,bgkd->bghqk', qb, k_w).astype(jnp.float32) + dense_bias(d_w)
        p_w = masked_softmax(s_w, mask_w)
        o_w = jnp.einsum('bghqk,bgkd->bghqd', p_w.astype(v_w.dtype), v_w)
        return jnp.stack([o_c, o_s, o_w], axis=0)

    o = lax.map(attend_block, (q, jnp.arange(n_q)))
    o = o.transpose(2, 0, 5, 1, 3, 4, 6).reshape(Bn, T, N_BRANCH, B_HEADS, B_HEAD_DIM)
    y = jnp.sum(gates[..., None].astype(o.dtype) * o * jax.nn.silu(z), axis=2)
    return y.reshape(Bn, T, B_WIDTH) @ out_w

def second_inputs(seed: int = 0) -> dict:
    key = jax.random.key(seed)
    ks = jax.random.split(key, 24)
    f32 = jnp.float32

    def nrm(k, shape, scale):
        return jax.random.normal(k, shape, f32) * scale

    a_cols = 4 * A_WIDTH + 2 * A_HEADS
    b_cols = 4 * B_WIDTH + N_BRANCH * B_HEADS
    dt = jnp.exp(jax.random.uniform(ks[9], (N_A_LAYERS, A_HEADS), f32, math.log(1e-3), math.log(1e-1)))
    return {
        "x": nrm(ks[0], (BATCH, SEQ, D_MODEL), 1.0),
        "c": nrm(ks[1], (BATCH, D_MODEL), 1.0),
        "rel_bias": nrm(ks[2], (NUM_BUCKETS, B_HEADS), 0.3),
        "ada_w": nrm(ks[3], (DEPTH_2, D_MODEL, 3 * D_MODEL), 0.5 * D_MODEL ** -0.5),
        "ada_b": nrm(ks[4], (DEPTH_2, 3 * D_MODEL), 0.02),
        "norm_g": 1.0 + nrm(ks[5], (DEPTH_2, D_MODEL), 0.02),
        "a_in_w": nrm(ks[6], (N_A_LAYERS, D_MODEL, a_cols), D_MODEL ** -0.5),
        "a_conv_w": nrm(ks[7], (N_A_LAYERS, A_CONV, 3 * A_WIDTH), A_CONV ** -0.5),
        "a_A_log": jnp.log(jax.random.uniform(ks[8], (N_A_LAYERS, A_HEADS), f32, 1.0, 16.0)),
        "a_dt_bias": dt + jnp.log(-jnp.expm1(-dt)),
        "a_onorm_g": 1.0 + nrm(ks[10], (N_A_LAYERS, A_HEAD_DIM), 0.02),
        "a_out_w": nrm(ks[11], (N_A_LAYERS, A_WIDTH, D_MODEL), A_WIDTH ** -0.5),
        "kv_norm_g": 1.0 + nrm(ks[12], (D_MODEL,), 0.02),
        "kv_w": nrm(ks[13], (D_MODEL, 6 * B_GROUPS * B_HEAD_DIM), D_MODEL ** -0.5),
        "cmp_pos_k": nrm(ks[14], (L_CMP, B_HEAD_DIM), 0.1),
        "cmp_pos_v": nrm(ks[15], (L_CMP, B_HEAD_DIM), 0.1),
        "cmp_k_w1": nrm(ks[16], (L_CMP * B_HEAD_DIM, CMP_HIDDEN), (L_CMP * B_HEAD_DIM) ** -0.5),
        "cmp_k_w2": nrm(ks[17], (CMP_HIDDEN, B_HEAD_DIM), CMP_HIDDEN ** -0.5),
        "cmp_v_w1": nrm(ks[18], (L_CMP * B_HEAD_DIM, CMP_HIDDEN), (L_CMP * B_HEAD_DIM) ** -0.5),
        "cmp_v_w2": nrm(ks[19], (CMP_HIDDEN, B_HEAD_DIM), CMP_HIDDEN ** -0.5),
        "b_in_w": nrm(ks[20], (N_B_LAYERS, D_MODEL, b_cols), D_MODEL ** -0.5),
        "b_out_w": nrm(ks[21], (N_B_LAYERS, B_WIDTH, D_MODEL), B_WIDTH ** -0.5),
        "final_g": 1.0 + nrm(ks[22], (D_MODEL,), 0.02),
    }

def second_block(x, c, rel_bias, ada_w, ada_b, norm_g, a_in_w, a_conv_w, a_A_log, a_dt_bias, a_onorm_g, a_out_w,
              kv_norm_g, kv_w, cmp_pos_k, cmp_pos_v, cmp_k_w1, cmp_k_w2, cmp_v_w1, cmp_v_w2,
              b_in_w, b_out_w, final_g):
    shared = None
    for l in range(DEPTH_2):
        shift, scale, gate = ada_modulation(c, ada_w[l], ada_b[l])
        h = rmsnorm_2(x, norm_g[l]) * (1.0 + scale) + shift
        if l < N_A_LAYERS:
            out = gated_deltanet_layer(h, a_in_w[l], a_conv_w[l], a_A_log[l], a_dt_bias[l], a_onorm_g[l], a_out_w[l])
        else:
            j = l - N_A_LAYERS
            out = nsa_layer(h, shared, rel_bias, b_in_w[j], b_out_w[j])
        x = x + gate * out
        if l == N_A_LAYERS - 1:
            shared = nsa_shared_kv(x, kv_norm_g, kv_w, cmp_pos_k, cmp_pos_v, cmp_k_w1, cmp_k_w2, cmp_v_w1, cmp_v_w2)
    return rmsnorm_2(x, final_g)


def setup_inputs(seed=0):
    out = dict(first_inputs(seed))
    for name, value in second_inputs(seed + 1).items():
        if name != "x":
            out[name + "_2"] = value
    return out


def reference(
    x, c, w_ada, b_ada, g_ff1, w1_gate, w1_up, w1_down, g_mix, w_in, lambda_q1, lambda_k1,
    lambda_q2, lambda_k2, g_subln, conv_w, conv_b, w_mq, w_mk, w_mv, w_if, b_if, ml_skip,
    g_mlnorm, w_proj_a, w_proj_b, w_out, g_ff2, w2_gate, w2_up, w2_down, g_final, c_2,
    rel_bias_2, ada_w_2, ada_b_2, norm_g_2, a_in_w_2, a_conv_w_2, a_A_log_2, a_dt_bias_2,
    a_onorm_g_2, a_out_w_2, kv_norm_g_2, kv_w_2, cmp_pos_k_2, cmp_pos_v_2, cmp_k_w1_2,
    cmp_k_w2_2, cmp_v_w1_2, cmp_v_w2_2, b_in_w_2, b_out_w_2, final_g_2,
):
    x = first_block(
        x, c, w_ada, b_ada, g_ff1, w1_gate, w1_up, w1_down, g_mix, w_in, lambda_q1, lambda_k1,
        lambda_q2, lambda_k2, g_subln, conv_w, conv_b, w_mq, w_mk, w_mv, w_if, b_if, ml_skip,
        g_mlnorm, w_proj_a, w_proj_b, w_out, g_ff2, w2_gate, w2_up, w2_down, g_final,
    )
    return second_block(
        x, c_2, rel_bias_2, ada_w_2, ada_b_2, norm_g_2, a_in_w_2, a_conv_w_2, a_A_log_2,
        a_dt_bias_2, a_onorm_g_2, a_out_w_2, kv_norm_g_2, kv_w_2, cmp_pos_k_2, cmp_pos_v_2,
        cmp_k_w1_2, cmp_k_w2_2, cmp_v_w1_2, cmp_v_w2_2, b_in_w_2, b_out_w_2, final_g_2,
    )


_drawn_inputs = setup_inputs


def setup_inputs(seed=0):
    import zlib

    import numpy as np

    out = dict(_drawn_inputs(seed))
    spreads = {}
    factors = {'lambda_q1': 8.0,
     'lambda_q2': 2.896,
     'g_subln': 4.116,
     'conv_b': 7.572,
     'ml_skip': 7.213,
     'g_mlnorm': 6.043,
     'g_ff2': 2.91,
     'rel_bias_2': 5.956,
     'ada_b_2': 3.386,
     'norm_g_2': 8.0,
     'a_onorm_g_2': 8.0,
     'kv_norm_g_2': 8.0,
     'cmp_pos_k_2': 8.0,
     'cmp_pos_v_2': 8.0,
     'cmp_k_w1_2': 4.665,
     'cmp_k_w2_2': 4.783,
     'final_g_2': 2.9}
    for name, (base, spread) in spreads.items():
        noise = np.random.default_rng([zlib.crc32(name.encode()), seed]).standard_normal(out[name].shape)
        drawn = base * np.exp(spread * noise) if base else spread * noise
        out[name] = __import__('jax').numpy.asarray(drawn.astype(out[name].dtype))
    for name, factor in factors.items():
        out[name] = (out[name] * factor).astype(out[name].dtype)
    return out
```

```python
from contextlib import ExitStack

import numpy as np

import concourse.bass as bass
from concourse import mybir

P = 128
T = 256
D = 1024
DFF = 2816
F32 = mybir.dt.float32
ALU = mybir.AluOpType
ACT = mybir.ActivationFunctionType
AX = mybir.AxisListType
NEG = -1e30
EPS = 1e-6
UNIT = 2080
SLOT = 4096
NSLOT = 3

VEC = [("c", 8), ("b_ada", 72), ("g_ff1", 8), ("g_mix", 8), ("g_subln", 1), ("conv_w", 32), ("conv_b", 8),
       ("ml_skip", 8), ("g_mlnorm", 8), ("g_ff2", 8), ("g_final", 8), ("c_2", 8), ("ada_b_2", 48),
       ("norm_g_2", 16), ("a_conv_w_2", 96), ("a_onorm_g_2", 1), ("kv_norm_g_2", 8), ("final_g_2", 8),
       ("cmp_pos_k_2", 16), ("cmp_pos_v_2", 16), ("w_if", 192), ("cmp_k_w2_2", 128), ("cmp_v_w2_2", 128),
       ("b_i", 1), ("b_f", 1), ("a_dt_bias_2", 1), ("a_A_log_2", 1), ("lam", 256), ("rel_bias_2", 16)]
CST = [("ident", 128), ("ones", 128), ("mean", 128), ("rot", 128), ("cos", 256), ("sin", 256), ("mblk", 256),
       ("mtri", 384), ("lvl", 7 * 128), ("selc", 64), ("selr", 8 * 128), ("oh", 384), ("m15", 22)]


def offsets(table):
    out, at = {}, 0
    for name, n in table:
        out[name] = (at, n)
        at += n
    return out, at


VO, VN = offsets(VEC)
CO, CN = offsets(CST)


def constants():
    c = np.zeros((P, CN), np.float32)

    def put(name, a):
        o, n = CO[name]
        a = np.asarray(a, np.float32).reshape(a.shape[0], -1)
        assert a.shape[1] == n, (name, a.shape)
        c[:a.shape[0], o:o + n] = a

    i = np.arange(P)
    put("ident", np.eye(P))
    put("ones", np.ones((P, P)))
    put("mean", np.full((P, P), 1.0 / D))
    rot = np.zeros((P, P))
    for p in range(P):
        d = p % 64
        if d < 32:
            rot[p + 32, p] = -1.0
        else:
            rot[p - 32, p] = 1.0
    put("rot", rot)
    inv = np.float32(10000.0) ** (-np.arange(0, 64, 2, dtype=np.float32) / np.float32(64))
    ang = np.arange(T, dtype=np.float32)[:, None] * inv.astype(np.float32)[None, :]
    put("cos", np.cos(ang).T[i % 32])
    put("sin", np.sin(ang).T[i % 32])
    mblk = np.zeros((P, 256))
    mblk[0:64, 192:256] = NEG
    put("mblk", mblk)
    tri = np.where(i[None, :] >= i[:, None], 0.0, NEG)
    put("mtri", np.concatenate([tri, np.zeros((P, P)), tri], 1))
    lv = np.zeros((P, 7, P))
    for n in range(7):
        b = 1 << n
        bi, bj = i[None, :] // b, i[:, None] // b
        lv[:, n, :] = (bj % 2 == 0) & (bi == bj + 1)
    put("lvl", lv)
    sc = np.zeros((P, 8, 8))
    sr = np.zeros((8, 8, P))
    for h in range(8):
        sc[:, h, h] = 1.0
        sr[h, h, :] = 1.0
    put("selc", sc)
    put("selr", sr)
    delta = 255 - np.arange(384)
    n = np.maximum(delta, 0)
    nf = np.maximum(n, 1).astype(np.float32)
    large = 16 + (np.log(nf / np.float32(16)) / np.float32(np.log(128 / 16)) * np.float32(16)).astype(np.int32)
    bucket = np.where(n < 16, n, np.minimum(large, 31))
    oh = np.zeros((33, 384))
    for j in range(384):
        if delta[j] >= 0:
            oh[bucket[j], j] = 1.0
        else:
            oh[32, j] = NEG
    put("oh", oh)
    m = np.zeros((P, 22))
    for q in range(7):
        m[:, q] = i - 16 * q - 31 >= 0
    for q in range(15):
        m[:, 7 + q] = i + 128 - 16 * q - 31 >= 0
    put("m15", m)
    return c


def vectors(x):
    v = np.zeros((P, VN), np.float32)

    def put(name, a):
        o, n = VO[name]
        a = a.reshape(a.shape[0], -1)
        assert a.shape[1] == n, (name, a.shape)
        v[:a.shape[0], o:o + n] = a

    def cols(a):
        return np.asarray(a).reshape(-1, P).T

    for name in ("c", "b_ada", "g_ff1", "g_mix", "g_subln", "conv_w", "conv_b", "ml_skip", "g_mlnorm", "g_ff2",
                 "g_final", "c_2", "ada_b_2", "norm_g_2", "a_conv_w_2", "a_onorm_g_2", "kv_norm_g_2", "final_g_2",
                 "cmp_pos_k_2", "cmp_pos_v_2"):
        put(name, cols(x[name]))
    for name in ("w_if", "cmp_k_w2_2", "cmp_v_w2_2"):
        a = np.asarray(x[name])
        put(name, a.reshape(-1, P, a.shape[-1]).transpose(1, 0, 2))
    b = np.asarray(x["b_if"]).reshape(8, 1)
    put("b_i", b[0:4])
    put("b_f", b[4:8])
    put("a_dt_bias_2", np.asarray(x["a_dt_bias_2"]).reshape(8, 1))
    put("a_A_log_2", np.asarray(x["a_A_log_2"]).reshape(8, 1))
    lam = np.concatenate([np.asarray(x[k]).reshape(1, 64) for k in ("lambda_q1", "lambda_q2", "lambda_k1", "lambda_k2")], 1)
    put("lam", lam)
    put("rel_bias_2", np.concatenate([np.asarray(x["rel_bias_2"]), np.ones((1, 16), np.float32)], 0))
    return v


class Queue:

    def __init__(self, sem):
        self.sem, self.n, self.items = sem, 0, []

    def __call__(self, fn, *waits, count=True):
        if count:
            self.n += 1
        self.items.append((flat(waits), fn, (self.sem, 1) if count else None))
        return (self.sem, self.n)

    def dma(self, fn, sem, *waits):
        self.items.append((flat(waits), fn, (sem, 16)))

    def emit(self, eng):
        seen = {}
        for waits, fn, inc in self.items:
            need = {}
            for s, v in waits:
                if v > max(seen.get(id(s), 0), need.get(id(s), (s, 0))[1]):
                    need[id(s)] = (s, v)
            for k, (s, v) in need.items():
                eng.wait_ge(s, v)
                seen[k] = v
            ins = fn(eng) if fn is not None else None
            if inc is not None:
                ins.then_inc(*inc)


def flat(x):
    if x is None:
        return []
    if isinstance(x, list) or (isinstance(x, tuple) and not (len(x) == 2 and isinstance(x[1], int))):
        return [y for e in x for y in flat(e)]
    return [x]


class Ring:

    def __init__(self, bufs):
        self.bufs, self.i, self.readers = bufs, -1, [[] for _ in bufs]

    def take(self):
        self.i = (self.i + 1) % len(self.bufs)
        assert self.readers[self.i] is not None, "still in use"
        r, self.readers[self.i] = self.readers[self.i], None
        return self.bufs[self.i], r, self.i

    def give(self, i, *toks):
        self.readers[i] = flat(toks)


def together(*gens):
    gens = list(gens)
    while gens:
        for g in list(gens):
            try:
                next(g)
            except StopIteration:
                gens.remove(g)


def run(gen):
    for _ in gen:
        pass


def build(nc, a, out, scratch):
    ctx = ExitStack()
    with ctx:
        def sb(name, shape):
            return ctx.enter_context(nc.sbuf_tensor(name, shape, F32))

        def sem(name):
            return ctx.enter_context(nc.semaphore(name))

        pe, dve, act, pool, sp = (Queue(sem("s_" + n)) for n in ("pe", "dve", "act", "pool", "sp"))

        vec = sb("vec", [P, VN])
        cst = sb("cst", [P, CN])
        H = sb("H", [P, 8, T])
        U = sb("U", [P, 8, T])
        arena = sb("arena", [P, 10 * UNIT])
        slots = sb("slots", [P, NSLOT, SLOT])
        mods = sb("mods", [P, 72 + 48])
        sm = sb("sm", [P, 192])
        rstd = sb("rstd", [P, T])
        tmpA = sb("tmpA", [P, 3, 512])
        tmpB = sb("tmpB", [P, 3, 512])
        tmpC = sb("tmpC", [P, 2, 512])
        banks = [ctx.enter_context(nc.psum_tensor(f"ps{i}", [P, 512], F32)) for i in range(8)]
        L = Ring([b[:, :] for b in banks[0:3]])
        S = Ring([b[:, :] for b in banks[3:5]])
        X = Ring([b[:, :] for b in banks[5:8]])
        TA = Ring([tmpA[:, i, :] for i in range(3)])
        TB = Ring([tmpB[:, i, :] for i in range(3)])
        TC = Ring([tmpC[:, i, :] for i in range(2)])

        def V(name, r=P):
            o, n = VO[name]
            return vec[0:r, o:o + n]

        def C(name, r=P):
            o, n = CO[name]
            return cst[0:r, o:o + n]

        def B(i, n=2048):
            return arena[:, i * UNIT:i * UNIT + n]

        def B3(i):
            return B(i).rearrange("p (c t) -> p c t", t=T)

        def now():
            return [(q.sem, q.n) for q in (pe, dve, act, pool)]

        ident = C("ident")
        lvl = C("lvl").rearrange("p (n i) -> p n i", n=7)
        selc = C("selc").rearrange("p (h m) -> p h m", h=8)
        selr = C("selr", 8).rearrange("p (h m) -> p h m", h=8)
        mtri = C("mtri")
        mblk = C("mblk")

        s_vec, s_cst = sem("s_vec"), sem("s_cst")
        s_x = sem("s_x")
        sp.dma(lambda e: e.dma_start(vec[:, :], a["vec"]), s_vec)
        sp.dma(lambda e: e.dma_start(cst[:, :], a["cst"]), s_cst)
        vec_in, cst_in = (s_vec, 16), (s_cst, 16)
        sp.dma(lambda e: e.dma_start(H[:, :, :], a["xT"].rearrange("(c p) t -> p c t", p=P)), s_x)
        x_in = (s_x, 16)

        s_slot = [sem(f"s_slot{i}") for i in range(NSLOT)]
        slot_n = [0] * NSLOT
        ring = Ring([slots[:, i, :] for i in range(NSLOT)])

        def load(*parts):
            buf, readers, i = ring.take()
            views = []
            for off, src in parts:
                kc, n = src.shape[0] // P, src.shape[1]
                v = buf[:, off:off + kc * n].rearrange("p (k n) -> p k n", n=n)
                s = src.rearrange("(k p) n -> p k n", p=P)
                sp.dma(lambda e, v=v, s=s: e.dma_start(v, s), s_slot[i], readers)
                slot_n[i] += 16
                views.append(v)
            return views, (s_slot[i], slot_n[i]), i

        def mm(out_, lhsT, rhs, *waits, start=True, stop=True, count=False):
            return pe(lambda e: e.matmul(out_, lhsT, rhs, start=start, stop=stop), *waits, count=count)

        def tr(out_, in_, n, *waits, count=False):
            return pe(lambda e: e.transpose(out_, in_, ident[0:n, 0:n]), *waits, count=count)

        def actv(out_, in_, f, *waits, **kw):
            return act(lambda e: e.activation(out_, in_, f, **kw), *waits)

        def tt(q, out_, i0, i1, op, *waits):
            return q(lambda e: e.tensor_tensor(out_, i0, i1, op), *waits)

        def ts(q, out_, i0, s1, s2, op0, op1, *waits):
            if op1 is None:
                return q(lambda e: e.tensor_scalar(out_, i0, s1, None, op0), *waits)
            return q(lambda e: e.tensor_scalar(out_, i0, s1, s2, op0, op1), *waits)

        def stt(out_, i0, s, i1, op0, op1, *waits):
            return dve(lambda e: e.scalar_tensor_tensor(out=out_, in0=i0, scalar=s, in1=i1, op0=op0, op1=op1), *waits)

        def group(out_, pairs, rdy, waits, count=False):
            tok = None
            for n, (l, r) in enumerate(pairs):
                tok = mm(out_, l, r, rdy[n] if rdy else None, waits if n == 0 else None,
                         start=n == 0, stop=n == len(pairs) - 1, count=count and n == len(pairs) - 1)
            return tok

        cs = sm[:, 0:16]
        t_c = actv(sm[:, 16:24], V("c"), ACT.Tanh, vec_in, scale=0.5)
        t_c = actv(sm[:, 24:32], V("c_2"), ACT.Tanh, scale=0.5)
        t = stt(cs[:, 0:8], sm[:, 16:24], 1.0, V("c"), ALU.add, ALU.mult, t_c)
        t = stt(cs[:, 8:16], sm[:, 24:32], 1.0, V("c_2"), ALU.add, ALU.mult, t_c)
        cs_rdy = ts(dve, cs, cs, 0.5, None, ALU.mult, None, t)
        mod_rdy = {}

        def ada(w, first, blocks, vec0, bias):
            for b0 in range(blocks[0], blocks[1], 4):
                (wv,), arrived, si = load((0, w[:, b0 * P:(b0 + 4) * P]))
                ps, rd, pi = L.take()
                for j in range(4):
                    done = group(ps[:, j:j + 1],
                                 [(wv[:, k, j * P:(j + 1) * P], cs[:, vec0 + k:vec0 + k + 1]) for k in range(8)],
                                 None, [rd, arrived, cs_rdy] if j == 0 else None, count=j == 3)
                ring.give(si, done)
                c0 = first + b0
                tok = tt(dve, mods[:, c0:c0 + 4], ps[:, 0:4], bias[:, b0:b0 + 4], ALU.add, done, vec_in)
                L.give(pi, tok)
                for j in range(4):
                    mod_rdy[c0 + j] = tok
                yield

        def normed(gcol, sc0, sh0, dst, src_rdy, dst_free, tag):
            A = sm[:, 32 + 8 * tag:40 + 8 * tag]
            if sc0 is not None:
                a_rdy = stt(A, mods[:, sc0:sc0 + 8], 1.0, gcol, ALU.add, ALU.mult, mod_rdy[sc0 + 7], now())
            for c2 in range(4):
                tb, rd, bi = TA.take()
                sq = actv(tb[:, :].rearrange("p (c t) -> p c t", t=T), H[:, 2 * c2:2 * c2 + 2, :], ACT.Square, rd,
                          src_rdy[2 * c2:2 * c2 + 2])
                if c2 == 0:
                    ps, rd, pi = X.take()
                for j in range(2):
                    last = mm(ps[:, 0:T], C("mean"), tb[:, j * T:(j + 1) * T], rd if c2 + j == 0 else None, sq, cst_in,
                              start=c2 + j == 0, stop=c2 == 3 and j == 1, count=j == 1)
                TA.give(bi, last)
            sq = actv(rstd[:, :], ps[:, 0:T], ACT.Sqrt, last, eps_rdy, now(), bias=eps)
            X.give(pi, sq)
            r = dve(lambda e: e.reciprocal(rstd[:, :], rstd[:, :]), sq)
            toks = []
            for c in range(8):
                tk = tt(dve, dst[:, c, :], H[:, c, :], rstd[:, :], ALU.mult, r, dst_free if c == 0 else None)
                if sc0 is not None:
                    tk = actv(dst[:, c, :], dst[:, c, :], ACT.Identity, tk, a_rdy, mod_rdy[sh0 + 7],
                              scale=A[:, c:c + 1], bias=mods[:, sh0 + c:sh0 + c + 1])
                toks.append(tk)
            return toks

        s_br = [sem("s_br0"), sem("s_br1")]
        for h in range(16):
            ps, rd, pi = X.take()
            rb = V("rel_bias_2", 33)[:, h:h + 1].to_broadcast([33, P])
            done = mm(ps[:, 0:384], rb, C("oh", 33), rd, vec_in, cst_in, count=True)
            tb, rd, bi = TC.take()
            n = h // 2
            tk = dve(lambda e, tb=tb, ps=ps: e.tensor_copy(tb[:, 0:384], ps[:, 0:384]), done, rd)
            X.give(pi, tk)
            sp.dma(lambda e, h=h, tb=tb: e.dma_start(scratch[h, :, :], tb[:, 0:384]), s_br[h % 2], tk)
            TC.give(bi, (s_br[h % 2], 16 * (n + 1)))

        eps = sm[:, 31:32]
        eps_rdy = dve(lambda e: e.memset(eps, EPS), t)

        def linear(w, c0, cols, rhs, rdy, epi, width=512):
            kc = w.shape[0] // P
            for b in range(0, cols, width):
                if kc * width <= SLOT:
                    (wv,), arrived, si = load((0, w[:, c0 + b:c0 + b + width]))
                    pieces = [(wv, arrived, si, 0, kc)]
                else:
                    hk = kc // 2
                    pieces = []
                    for n in range(2):
                        (wv,), arrived, si = load((0, w[n * hk * P:(n + 1) * hk * P, c0 + b:c0 + b + width]))
                        pieces.append((wv, arrived, si, n * hk, hk))
                for j2 in range(width // 256):
                    ps, rd, pi = L.take()
                    for j in range(2):
                        o = j2 * 256 + j * 128
                        prs, rr = [], []
                        for wv, arrived, si, k0, n in pieces:
                            for k in range(n):
                                prs.append((wv[:, k, o:o + P], rhs[:, k0 + k, :]))
                                rr.append([arrived, rdy[k0 + k]])
                        done = group(ps[:, j * T:(j + 1) * T], prs, rr, rd, count=j == 1)
                    if j2 == width // 256 - 1:
                        for p in pieces:
                            ring.give(p[2], done)
                    L.give(pi, epi((b + j2 * 256) // 256, ps, done))
                    yield

        def ffn(wg, wu, wd, u_rdy, gate0, h_rdy):
            free = now()
            actT = arena[:, 0:22 * T].rearrange("p (c t) -> p c t", t=T)
            rdy = []
            for b in range(11):
                (g_, u_), arrived, si = load((0, wg[:, b * 256:(b + 1) * 256]), (2048, wu[:, b * 256:(b + 1) * 256]))
                for j in range(2):
                    ps, rd, pi = L.take()
                    group(ps[:, 0:T], [(g_[:, k, j * P:(j + 1) * P], U[:, k, :]) for k in range(8)],
                          [[arrived, u_rdy[k]] for k in range(8)], rd)
                    done = group(ps[:, T:2 * T], [(u_[:, k, j * P:(j + 1) * P], U[:, k, :]) for k in range(8)],
                                 None, None, count=True)
                    tb, rd, bi = TB.take()
                    tk = actv(tb[:, 0:T], ps[:, 0:T], ACT.Tanh, done, rd, scale=0.5)
                    tk = stt(tb[:, T:512], tb[:, 0:T], 1.0, ps[:, 0:T], ALU.add, ALU.mult, tk)
                    tk = tt(dve, actT[:, 2 * b + j, :], tb[:, T:512], ps[:, T:512], ALU.mult, tk, free)
                    TB.give(bi, tk)
                    L.give(pi, tk)
                    rdy.append(tk)
                ring.give(si, done)
                yield
            gq = ts(dve, sm[:, 96:104], mods[:, gate0:gate0 + 8], 0.25, None, ALU.mult, None, mod_rdy[gate0 + 7], now())

            def epi(pair, ps, done):
                for j in range(2):
                    c = 2 * pair + j
                    h_rdy[c] = stt(H[:, c, :], ps[:, j * T:(j + 1) * T], sm[:, 96 + c:97 + c], H[:, c, :],
                                   ALU.mult, ALU.add, done, gq, h_rdy[c])
                return h_rdy[c]
            yield from linear(wd, 0, D, actT, rdy, epi, width=256)

        def rows_rsqrt(srcs, rowof, nrow, scale, e, post, dst8, sq_to=None):
            ps, rd, pi = X.take()
            for n, (s, tk) in enumerate(srcs):
                tb, trd, bi = TC.take()
                sq = actv(tb[:, 0:T], s, ACT.Square, trd, tk)
                last = mm(ps[0:8, 0:T], selc[:, rowof[n], :], tb[:, 0:T], rd if n == 0 else None, sq,
                          start=n == 0, stop=n == len(srcs) - 1, count=True)
                TC.give(bi, last)
            tk = ts(dve, dst8, ps[0:8, 0:T], scale / post ** 2, e / post ** 2, ALU.mult, ALU.add, last, now())
            X.give(pi, tk)
            tk = actv(dst8, dst8, ACT.Sqrt, tk)
            return dve(lambda en: en.reciprocal(dst8, dst8), tk)

        run(ada(a["w_ada"], 0, (0, 16), 0, V("b_ada")))
        h_rdy = [x_in] * 8
        u_rdy = normed(V("g_ff1"), 8, 0, U, h_rdy, None, 0)
        together(ffn(a["w1_gate"], a["w1_up"], a["w1_down"], u_rdy, 16, h_rdy), ada(a["w_ada"], 0, (16, 40), 0, V("b_ada")))
        u_rdy = normed(V("g_mix"), 32, 24, U, h_rdy, now(), 1)

        lv = V("lam", 1)
        l1 = tt(dve, tmpA[0:1, 0, 0:128], lv[:, 0:128], lv[:, 128:256], ALU.mult, now())
        l2 = dve(lambda e: e.tensor_reduce(sm[0:1, 106:108], tmpA[0:1, 0, 0:128].rearrange("p (a n) -> p a n", a=2), AX.X, ALU.add), l1)
        TA.give(0, l2)
        l2 = actv(sm[0:1, 106:108], sm[0:1, 106:108], ACT.Exp, l2)
        l2 = stt(sm[0:1, 108:109], sm[0:1, 106:107], -1.0, sm[0:1, 107:108], ALU.mult, ALU.add, l2)
        l2 = ts(dve, sm[0:1, 108:109], sm[0:1, 108:109], -(0.8 - 0.6), None, ALU.add, None, l2)
        ps, rd, pi = X.take()
        l2 = mm(ps[:, 0:1], C("ones", 1), sm[0:1, 108:109], rd, l2, count=True)
        lam_rdy = actv(sm[:, 109:110], ps[:, 0:1], ACT.Copy, l2)
        X.give(pi, lam_rdy)
        nlam = sm[:, 109:110]

        w_in = a["w_in"]
        QR, KR, YA = B3(0), B3(1), B3(3)
        VA = B(2).rearrange("p (i n) -> p i n", i=2)
        qk_rdy = {}
        free0 = now()

        def rope_epi(dst, key):
            def epi(pair, ps, done):
                tb, rd, bi = TA.take()
                raw = actv(tb, ps, ACT.Copy, done, rd)
                p2, rd2, pi2 = X.take()
                rt = mm(p2, C("rot"), tb, raw, rd2, count=True)
                tb2, rd3, bi2 = TB.take()
                cosb = C("cos").unsqueeze(1).to_broadcast([P, 2, T])
                sinb = C("sin").unsqueeze(1).to_broadcast([P, 2, T])
                d3 = dst[:, 2 * pair:2 * pair + 2, :]
                a1 = tt(pool, d3, tb.rearrange("p (c t) -> p c t", t=T), cosb, ALU.mult, raw, free0)
                b1 = tt(dve, tb2.rearrange("p (c t) -> p c t", t=T), p2.rearrange("p (c t) -> p c t", t=T), sinb, ALU.mult, rt, rd3)
                X.give(pi2, b1)
                TA.give(bi, rt, a1)
                s = tt(dve, d3, d3, tb2.rearrange("p (c t) -> p c t", t=T), ALU.add, a1, b1)
                TB.give(bi2, s)
                qk_rdy[(key, 2 * pair)] = qk_rdy[(key, 2 * pair + 1)] = s
                return raw
            return epi

        run(linear(w_in, 0, D, U, u_rdy, rope_epi(QR, "q")))
        run(linear(w_in, D, D, U, u_rdy, rope_epi(KR, "k")))

        def token_major(w, c0, n, src, rdy, i, waits, view=None, arrived=None):
            ps, rd, pi = L.take()
            done = group(ps[:, 0:n], [(src[:, k, i * P:(i + 1) * P], w[:, k, c0:c0 + n]) for k in range(8)],
                         [[arrived, rdy[k]] for k in range(8)], rd, count=True)
            return ps, done, pi

        va_rdy = []
        for b in range(2):
            (wv,), arrived, si = load((0, w_in[:, 2 * D + b * 512:2 * D + (b + 1) * 512]))
            for i in range(2):
                ps, done, pi = token_major(wv, 0, 512, U, u_rdy, i, None, arrived=arrived)
                tk = actv(VA[:, i, b * 512:(b + 1) * 512], ps, ACT.Copy, done, free0)
                L.give(pi, tk)
                va_rdy.append(tk)
            ring.give(si, done)

        EB = sb("EB", [P, 2, 2, 384])
        AB = sb("AB", [P, 2, 384])
        AT = sb("AT", [P, 2, 384])
        eb = Ring([EB[:, i, :, :] for i in range(2)])
        ab = Ring([AB[:, i, :] for i in range(2)])
        at = Ring([AT[:, i, :] for i in range(2)])
        st = sb("st", [P, 2, 24])
        stR = Ring([st[:, i, :] for i in range(2)])
        TILES = [(0, 0, 128, 128), (1, 128, 384, 0)]

        def transposed3(src, waits):
            ps, rd, pi = X.take()
            for n in range(3):
                done = tr(ps[:, n * P:(n + 1) * P], src[:, n * P:(n + 1) * P], P, rd if n == 0 else None, waits, count=n == 2)
            t_, rd, ti = at.take()
            tk = actv(t_, ps[:, 0:384], ACT.Copy, done, rd)
            X.give(pi, tk)
            return t_, tk, ti, done

        def diff_attention():
            ya_rdy = []
            for h in range(8):
                ev, erd, ei = eb.take()
                s_, srd, s_i = stR.take()
                mx = []
                for c in range(2):
                    ps, rd, pi = S.take()
                    q = QR[64 * c:64 * c + 64, h, :]
                    k = KR[64 * c:64 * c + 64, h, :]
                    mm(ps[:, 0:128], q[:, 0:128], k[:, 0:128], rd, qk_rdy[("q", h)], qk_rdy[("k", h)])
                    done = mm(ps[:, 128:384], q[:, 128:256], k[:, 0:256], count=True)
                    for i, a0, a1, m0 in TILES:
                        tk = dve(lambda e, ps=ps, a0=a0, a1=a1, m0=m0, c=c, i=i, ev=ev, s_=s_: e.tensor_tensor_reduce(
                            ev[:, c, a0:a1], ps[:, a0:a1], mblk[:, m0:256], 0.125, NEG, ALU.add, ALU.max,
                            s_[:, 2 * c + i:2 * c + i + 1]), done, erd, srd)
                    S.give(pi, tk)
                    mx.append(tk)
                nm = ts(dve, s_[:, 4:8], s_[:, 0:4], -1.0, None, ALU.mult, None, mx)
                yield
                for c in range(2):
                    for i, a0, a1, m0 in TILES:
                        n = 2 * c + i
                        ex = actv(ev[:, c, a0:a1], ev[:, c, a0:a1], ACT.Exp, nm, bias=s_[:, 4 + n:5 + n],
                                  accum_out=s_[:, 8 + n:9 + n])
                r = dve(lambda e, s_=s_: e.reciprocal(s_[:, 12:16], s_[:, 8:12]), ex)
                r = ts(dve, s_[:, 14:16], s_[:, 14:16], nlam, None, ALU.mult, None, r, lam_rdy)
                a_, ard, ai = ab.take()
                for i, a0, a1, m0 in TILES:
                    tk = ts(dve, a_[:, a0:a1], ev[:, 0, a0:a1], s_[:, 12 + i:13 + i], None, ALU.mult, None, r, ard)
                    tk = stt(a_[:, a0:a1], ev[:, 1, a0:a1], s_[:, 14 + i:15 + i], a_[:, a0:a1], ALU.mult, ALU.add, tk)
                eb.give(ei, tk)
                stR.give(s_i, tk)
                yield
                aT, tk, ti, trd = transposed3(a_, tk)
                ab.give(ai, trd)
                ps, rd, pi = S.take()
                mm(ps[:, 0:T], VA[:, 0, h * P:(h + 1) * P], aT[:, 0:T], rd, tk, va_rdy, start=True, stop=False)
                done = mm(ps[:, 128:T], VA[:, 1, h * P:(h + 1) * P], aT[:, 256:384], start=False, stop=True, count=True)
                at.give(ti, done)
                tk = actv(YA[:, h, :], ps[:, 0:T], ACT.Copy, done, free0)
                S.give(pi, tk)
                ya_rdy.append(tk)
                yield
            r8 = rows[0:8, 0, :]
            rk = rows_rsqrt([(YA[:, h, :], ya_rdy[h]) for h in range(8)], list(range(8)), 8, 1.0 / 128, EPS, 0.8, r8)
            yield
            for h in range(8):
                ps, rd, pi = X.take()
                done = mm(ps[:, 0:T], selr[:, h, :], r8, rd, rk, count=True)
                tk = stt(YA[:, h, :], YA[:, h, :], V("g_subln"), ps[:, 0:T], ALU.mult, ALU.mult, done)
                X.give(pi, tk)
                out_rdy["ya", h] = tk
                if h % 2:
                    yield

        rows = sb("rows", [16, 8, T])
        out_rdy = {}
        XM = arena[:, 4 * UNIT:5 * UNIT].rearrange("p (c t) -> p c t", t=260)
        XC, OP = B3(5), B3(6)
        hw = sb("hw", [P, 40 + 96])
        hw1 = ts(dve, hw[:, 0:40], vec[:, VO["conv_w"][0]:VO["conv_w"][0] + 40], 0.5, None, ALU.mult, None)
        hw2 = ts(dve, hw[:, 40:136], V("a_conv_w_2"), 0.5, None, ALU.mult, None)
        z1 = dve(lambda e: e.memset(XM[:, :, 0:3], 0.0), free0)
        xm_rdy, xc_rdy, op_rdy = [None] * 8, [None] * 8, [None] * 8

        def conv_silu(pad, pad_rdy, w, dst, bias, dwait):
            tb, rd, bi = TB.take()
            y = tb[:, 0:T]
            if bias is None:
                tk = ts(dve, y, pad[:, 0:T], w(0), None, ALU.mult, None, pad_rdy, rd)
            else:
                tk = ts(dve, y, pad[:, 0:T], w(0), bias, ALU.mult, ALU.add, pad_rdy, rd)
            for k in range(1, 4):
                tk = stt(y, pad[:, k:k + T], w(k), y, ALU.mult, ALU.add, tk)
            th = actv(tb[:, T:512], y, ACT.Tanh, tk)
            tk = stt(dst, tb[:, T:512], 1.0, y, ALU.add, ALU.mult, th, dwait)
            TB.give(bi, tk)
            return tk

        def xm_epi(pair, ps, done):
            tk = actv(XM[:, 2 * pair:2 * pair + 2, 3:259], ps.rearrange("p (c t) -> p c t", t=T), ACT.Copy, done, free0)
            for c in (2 * pair, 2 * pair + 1):
                xm_rdy[c] = tk
                xc_rdy[c] = conv_silu(XM[:, c, :], [tk, z1], lambda k, c=c: hw[:, 8 * k + c:8 * k + c + 1], XC[:, c, :],
                                      hw[:, 32 + c:33 + c], hw1)
            return tk

        def tanh_epi(dst, rdy):
            def epi(pair, ps, done):
                tk = actv(dst[:, 2 * pair:2 * pair + 2, :], ps.rearrange("p (c t) -> p c t", t=T), ACT.Tanh, done, scale=0.5)
                rdy[2 * pair] = rdy[2 * pair + 1] = tk
                return tk
            return epi

        def seq(*gens):
            for g in gens:
                yield from g

        together(diff_attention(), seq(linear(w_in, 3 * D, D, U, u_rdy, xm_epi),
                                       linear(w_in, 4 * D, D, U, u_rdy, tanh_epi(OP, op_rdy)),
                                       ada(a["w_ada"], 0, (40, 72), 0, V("b_ada"))))

        MQ, MK, MVT, HC = B3(0), B3(1), B3(2), B3(2)
        MV = B(7).rearrange("p (i n) -> p i n", i=2)
        GA, GB = B3(8), B3(9)
        ga_rdy, gb_rdy = [None] * 8, [None] * 8
        YB = HC
        wif = V("w_if").rearrange("p (t h c g) -> p t h c g", t=3, h=4, c=2)
        gcol = sb("gcol", [P, 2, 20])
        xmv = XM[:, :, 3:259]

        def mlstm():
            free = now()
            (wq, wk), arrived, si = load((0, a["w_mq"]), (2048, a["w_mk"]))
            (wv,), arrived2, si2 = load((0, a["w_mv"]))
            q_r, k_r, vt_r, v_r = {}, {}, {}, {}
            for h in range(4):
                for w, arr, src, rdy, dst, rr in ((wq, arrived, XC, xc_rdy, MQ, q_r), (wk, arrived, XC, xc_rdy, MK, k_r),
                                                  (wv, arrived2, xmv, xm_rdy, MVT, vt_r)):
                    ps, rd, pi = L.take()
                    for e2 in range(2):
                        done = group(ps[:, e2 * T:(e2 + 1) * T],
                                     [(w[:, 2 * h + k, e2 * P:(e2 + 1) * P], src[:, 2 * h + k, :]) for k in range(2)],
                                     [[arr, rdy[2 * h + k]] for k in range(2)], rd, count=e2 == 1)
                    tk = actv(dst[:, 2 * h:2 * h + 2, :], ps.rearrange("p (c t) -> p c t", t=T), ACT.Copy, done, free)
                    L.give(pi, tk)
                    rr[h] = tk
                ps, rd, pi = L.take()
                for i in range(2):
                    done = group(ps[:, i * T:(i + 1) * T],
                                 [(xmv[:, 2 * h + k, i * P:(i + 1) * P], wv[:, 2 * h + k, :]) for k in range(2)],
                                 [[arrived2, xm_rdy[2 * h + k]] for k in range(2)], rd, count=i == 1)
                tk = tt_copy(MV[:, :, h * T:(h + 1) * T], ps.rearrange("p (i n) -> p i n", i=2), done, free)
                L.give(pi, tk)
                v_r[h] = tk
            ring.give(si, done)
            ring.give(si2, done)
            gtok = gcol[:, :, 0:8]
            ps, rd, pi = X.take()
            for i in range(2):
                prs, rr = [], []
                for t3, (buf, r_) in enumerate(((MQ, q_r), (MK, k_r), (MVT, vt_r))):
                    for h in range(4):
                        for c2 in range(2):
                            prs.append((buf[:, 2 * h + c2, i * P:(i + 1) * P], wif[:, t3, h, c2, :]))
                            rr.append(r_[h])
                done = group(ps[:, 8 * i:8 * i + 8], prs, rr, rd, count=i == 1)
            tk = tt_copy(gtok, ps[:, 0:16].rearrange("p (i g) -> p i g", i=2), done, free)
            X.give(pi, tk)
            gates_done = done
            ps, rd, pi = X.take()
            for i in range(2):
                tr(ps[0:4, i * P:(i + 1) * P], gcol[:, i, 0:4], P, rd if i == 0 else None, tk)
            for i in range(2):
                done = tr(ps[0:4, T + i * P:T + (i + 1) * P], gcol[:, i, 4:8], P, count=i == 1)
            R = rows
            ig = ts(dve, R[0:4, 1, :], ps[0:4, 0:T], V("b_i", 4), None, ALU.add, None, done, free)
            fg = ts(dve, R[0:4, 2, :], ps[0:4, T:512], V("b_f", 4), None, ALU.add, None)
            X.give(pi, fg)
            tk = actv(R[0:4, 3, :], R[0:4, 2, :], ACT.Abs, fg)
            tk = actv(R[0:4, 3, :], R[0:4, 3, :], ACT.Exp, tk, scale=-1.0)
            tk = actv(R[0:4, 3, :], R[0:4, 3, :], ACT.Ln, tk, bias=1.0)
            tk = stt(R[0:4, 2, :], R[0:4, 2, :], 0.0, R[0:4, 3, :], ALU.min, ALU.subtract, tk)
            tk = dve(lambda e: e.tensor_tensor_scan(R[0:4, 3, :], one_row[0:4, :], R[0:4, 2, :], 0.0, ALU.mult, ALU.add), tk, one_rdy)
            tk = tt(dve, R[0:4, 1, :], R[0:4, 1, :], R[0:4, 3, :], ALU.subtract, tk, ig)
            tk = dve(lambda e: e.tensor_tensor_scan(R[0:4, 2, :], R[0:4, 1, :], R[0:4, 1, :], 0.0, ALU.max, ALU.max), tk)
            tk2 = stt(R[0:4, 5, :], R[0:4, 3, :], -1.0, R[0:4, 2, :], ALU.mult, ALU.subtract, tk)
            tk2 = actv(R[0:4, 5, :], R[0:4, 5, :], ACT.Exp, tk2)
            tk3 = ts(dve, R[0:4, 4, :], R[0:4, 2, :], -1.0, None, ALU.mult, None, tk)
            ps, rd, pi = X.take()
            for i in range(2):
                done = tr(ps[:, 4 * i:4 * i + 4], R[0:4, 1, i * P:(i + 1) * P], 4, rd if i == 0 else None, tk, count=i == 1)
            gs = tt_copy(gcol[:, :, 8:12], ps[:, 0:8].rearrange("p (i g) -> p i g", i=2), done)
            X.give(pi, gs)
            yield
            hc_rdy = [None] * 8
            for h in range(4):
                ps, rd, pi = X.take()
                bc = mm(ps, selr[0:4, h, :], R[0:4, 4:6, :], rd, tk2, tk3, count=True)
                w_, wrd, wi = TA.take()
                xs = tt(dve, w_[:, 0:T], ps[:, 0:T], mtri[:, 0:T], ALU.add, bc, wrd)
                xs = tt(dve, w_[:, T:384], ps[:, 128:T], mtri[:, 256:384], ALU.add)
                em, emrd, emi = TB.take()
                emr = actv(em[:, 0:T], ps[:, T:512], ACT.Copy, bc, xs, emrd)
                X.give(pi, xs, emr)
                actv(w_[:, 0:T], w_[:, 0:T], ACT.Exp, xs, gs, bias=gcol[:, 0, 8 + h:9 + h])
                wr = actv(w_[:, T:384], w_[:, T:384], ACT.Exp, bias=gcol[:, 1, 8 + h:9 + h])
                sp_, rd, si_ = S.take()
                group(sp_[:, 0:T], [(MK[:, 2 * h + c, 0:P], MQ[:, 2 * h + c, :]) for c in range(2)], [[q_r[h], k_r[h]]] * 2, rd)
                done = group(sp_[:, T:384], [(MK[:, 2 * h + c, P:T], MQ[:, 2 * h + c, P:T]) for c in range(2)], None, None, count=True)
                sc_, srd, sci = ab.take()
                sc = stt(sc_, sp_[:, 0:384], 0.0625, w_[:, 0:384], ALU.mult, ALU.mult, wr, done, srd)
                TA.give(wi, sc)
                S.give(si_, sc)
                yield
                np_, rd, ni = S.take()
                for e2 in range(2):
                    o = h * T + e2 * P
                    mm(np_[:, e2 * T:(e2 + 1) * T], MV[:, 0, o:o + P], sc_[:, 0:T], rd if e2 == 0 else None, sc, v_r[h], stop=False)
                    num = mm(np_[:, e2 * T + P:(e2 + 1) * T], MV[:, 1, o:o + P], sc_[:, T:384], start=False, count=e2 == 1)
                dp, rd, di = X.take()
                mm(dp[:, 0:T], C("ones"), sc_[:, 0:T], rd, stop=False)
                den = mm(dp[:, P:T], C("ones"), sc_[:, T:384], start=False, count=True)
                ab.give(sci, den)
                dk = actv(em[:, T:512], dp[:, 0:T], ACT.Abs, den)
                X.give(di, dk)
                dk = tt(dve, em[:, 0:T], em[:, 0:T], em[:, T:512], ALU.max, dk, emr)
                dk = dve(lambda e, em=em: e.reciprocal(em[:, 0:T], em[:, 0:T]), dk)
                for e2 in range(2):
                    hk = tt(dve, HC[:, 2 * h + e2, :], np_[:, e2 * T:(e2 + 1) * T], em[:, 0:T], ALU.mult, dk, num, gates_done)
                    hc_rdy[2 * h + e2] = hk
                S.give(ni, hk)
                TB.give(emi, hk)
                yield
            r8 = rows[0:8, 0, :]
            rk = rows_rsqrt([(HC[:, c, :], hc_rdy[c]) for c in range(8)], [c // 2 for c in range(8)], 4, 1.0 / 256, EPS, 1.0, r8)
            hg = ts(dve, sm[:, 112:120], V("g_mlnorm"), 0.5, None, ALU.mult, None)
            hg = ts(dve, sm[:, 120:128], V("ml_skip"), 0.5, None, ALU.mult, None)
            yield
            for h in range(4):
                ps, rd, pi = X.take()
                done = mm(ps[:, 0:T], selr[:, h, :], r8, rd, rk, count=True)
                for e2 in range(2):
                    c = 2 * h + e2
                    tk = stt(HC[:, c, :], HC[:, c, :], sm[:, 112 + c:113 + c], ps[:, 0:T], ALU.mult, ALU.mult, done, hg)
                    tk2 = stt(HC[:, c, :], XC[:, c, :], sm[:, 120 + c:121 + c], HC[:, c, :], ALU.mult, ALU.add, tk, hg)
                    tk3 = stt(HC[:, c, :], OP[:, c, :], 1.0, HC[:, c, :], ALU.add, ALU.mult, tk2, op_rdy[c])
                    out_rdy["yb", c] = tk3
                X.give(pi, tk)
                yield

        def tt_copy(o, i, *waits):
            return dve(lambda e: e.tensor_copy(o, i), *waits)

        one_row = rows[0:8, 7, :]
        one_rdy = dve(lambda e: e.memset(one_row, 1.0))

        together(mlstm(), seq(linear(w_in, 5 * D, D, U, u_rdy, tanh_epi(GA, ga_rdy)),
                              linear(w_in, 6 * D, D, U, u_rdy, tanh_epi(GB, gb_rdy)),
                              ada(a["ada_w1"], 72, (0, 24), 8, V("ada_b_2")[:, 0:24])))

        MG = B3(0)
        mg_rdy = [None] * 8
        freem = now()

        def epi_a(pair, ps, done):
            for j in range(2):
                c = 2 * pair + j
                tk = stt(MG[:, c, :], GA[:, c, :], 1.0, ps[:, j * T:(j + 1) * T], ALU.add, ALU.mult, done, ga_rdy[c], freem)
                mg_rdy[c] = tk
            return tk

        def epi_b(pair, ps, done):
            tb, rd, bi = TB.take()
            for j in range(2):
                c = 2 * pair + j
                tk = stt(tb[:, j * T:(j + 1) * T], GB[:, c, :], 1.0, ps[:, j * T:(j + 1) * T], ALU.add, ALU.mult, done, gb_rdy[c], rd)
            s = tt(pool, MG[:, 2 * pair:2 * pair + 2, :], MG[:, 2 * pair:2 * pair + 2, :], tb.rearrange("p (c t) -> p c t", t=T),
                   ALU.add, tk, mg_rdy[2 * pair + 1])
            TB.give(bi, s)
            mg_rdy[2 * pair] = mg_rdy[2 * pair + 1] = s
            return tk

        run(linear(a["w_proj_a"], 0, D, YA, [out_rdy["ya", c] for c in range(8)], epi_a))
        run(linear(a["w_proj_b"], 0, D, YB, [out_rdy["yb", c] for c in range(8)], epi_b))

        def residual(scale_cols, scale_rdy):
            def epi(pair, ps, done):
                for j in range(2):
                    c = 2 * pair + j
                    h_rdy[c] = stt(H[:, c, :], ps[:, j * T:(j + 1) * T], scale_cols[:, c:c + 1], H[:, c, :],
                                   ALU.mult, ALU.add, done, scale_rdy, h_rdy[c])
                return h_rdy[c]
            return epi

        g2 = ts(dve, sm[:, 128:136], mods[:, 40:48], 0.5, None, ALU.mult, None, mod_rdy[47])
        run(linear(a["w_out"], 0, D, MG, mg_rdy, residual(sm[:, 128:136], g2)))

        u_rdy = normed(V("g_ff2"), 56, 48, U, h_rdy, now(), 2)
        together(ffn(a["w2_gate"], a["w2_up"], a["w2_down"], u_rdy, 64, h_rdy), ada(a["ada_w2"], 96, (0, 24), 8, V("ada_b_2")[:, 24:48]))

        n_rdy = normed(None, None, None, U, h_rdy, now(), 3)
        h_rdy = [ts(dve, H[:, c, :], U[:, c, :], V("g_final")[:, c:c + 1], None, ALU.mult, None, n_rdy[c]) for c in range(8)]

        u_rdy = normed(V("norm_g_2")[:, 0:8], 80, 72, U, h_rdy, now(), 4)
        free = now()
        wa = a["a_in_w_2"]
        R = rows
        gb_ = sb("gb_", [P, 2, 32])
        (wv,), arrived, si = load((0, wa[:, 4096:4112]))
        for i in range(2):
            ps, done, pi = token_major(wv, 0, 16, U, u_rdy, i, None, arrived=arrived)
            tk = tt_copy(gb_[:, i, 0:16], ps[:, 0:16], done)
            L.give(pi, tk)
        ring.give(si, done)
        gtok = tk
        QG, KG, VG, ZG = B3(0), B3(1), B3(2), B3(3)
        cv_rdy = {}
        pads = B(9, 1040).rearrange("p (a b n) -> p a b n", a=2, b=2)
        padr = Ring([pads[:, i, :, :] for i in range(2)])
        z2 = dve(lambda e: e.memset(pads[:, :, :, 0:3], 0.0), free)

        def conv_epi(pair, ps, done):
            pd, rd, di = padr.take()
            cp = actv(pd[:, :, 3:259], ps.rearrange("p (c t) -> p c t", t=T), ACT.Copy, done, rd)
            for j in range(2):
                c = 2 * pair + j
                dst = (QG, KG, VG)[c // 8][:, c % 8, :]
                cv_rdy[c] = conv_silu(pd[:, j, :], [cp, z2], lambda k, c=c: hw[:, 40 + 24 * k + c:41 + 24 * k + c], dst,
                                      None, [free, hw2])
            padr.give(di, cv_rdy[c])
            return cp

        g_tok = {}

        def delta_gates():
            ps, rd, pi = X.take()
            for i in range(2):
                tr(ps[0:8, i * P:(i + 1) * P], gb_[:, i, 0:8], P, rd if i == 0 else None, gtok)
            for i in range(2):
                done = tr(ps[0:8, T + i * P:T + (i + 1) * P], gb_[:, i, 8:16], P, count=i == 1)
            bt0 = actv(R[0:8, 1, :], ps[0:8, 0:T], ACT.Tanh, done, free, scale=0.5)
            bt = ts(dve, R[0:8, 1, :], R[0:8, 1, :], 1.0, 0.5, ALU.add, ALU.mult, bt0)
            ak = ts(dve, R[0:8, 2, :], ps[0:8, T:512], V("a_dt_bias_2", 8), None, ALU.add, None, done, bt0)
            X.give(pi, ak)
            tk = actv(R[0:8, 3, :], R[0:8, 2, :], ACT.Abs, ak)
            tk = actv(R[0:8, 3, :], R[0:8, 3, :], ACT.Exp, tk, scale=-1.0)
            tk = actv(R[0:8, 3, :], R[0:8, 3, :], ACT.Ln, tk, bias=1.0)
            el = actv(sm[0:8, 136:137], V("a_A_log_2", 8), ACT.Exp)
            tk = stt(R[0:8, 2, :], R[0:8, 2, :], 0.0, R[0:8, 3, :], ALU.max, ALU.add, tk)
            tk = ts(dve, R[0:8, 2, :], R[0:8, 2, :], sm[0:8, 136:137], -1.0, ALU.mult, ALU.mult, tk, el)
            gc = dve(lambda e: e.tensor_tensor_scan(R[0:8, 3, :], one_row[0:8, :], R[0:8, 2, :], 0.0, ALU.mult, ALU.add), tk)
            ps, rd, pi = X.take()
            for i in range(2):
                tr(ps[:, 16 * i:16 * i + 8], R[0:8, 1, i * P:(i + 1) * P], 8, rd if i == 0 else None, bt, gc)
                done = tr(ps[:, 16 * i + 8:16 * i + 16], R[0:8, 3, i * P:(i + 1) * P], 8, count=i == 1)
            pv = ps[:, 0:32].rearrange("p (i g) -> p i g", i=2)
            tk = tt_copy(gb_[:, :, 16:24], pv[:, :, 0:8], done)
            tk = ts(dve, gb_[:, :, 24:32], pv[:, :, 8:16], -1.0, None, ALU.mult, None, done)
            X.give(pi, tk)
            g_tok["tok"] = tk
            g_tok["beta"], g_tok["gc"] = bt, gc
            yield

        MT = arena[:, 6 * UNIT:6 * UNIT + 3072].rearrange("p (h n) -> p h n", h=8)
        ATT = arena[:, 6 * UNIT + 3072:6 * UNIT + 6144].rearrange("p (h n) -> p h n", h=8)
        VB = B(4).rearrange("p (h i n) -> p h i n", h=8, i=2)
        DM = B(5).rearrange("p (u n) -> p u n", u=16)
        DT = B(9).rearrange("p (u n) -> p u n", u=16)
        P1 = B(2).rearrange("p (u n) -> p u n", u=16)
        UU = B(1).rearrange("p (h i n) -> p h i n", h=8, i=2)
        OG = B3(0)

        def delta():
            yield from delta_gates()
            r8q, r8k = rows[0:8, 0, :], rows[0:8, 4, :]
            rq = rows_rsqrt([(QG[:, h, :], cv_rdy[h]) for h in range(8)], list(range(8)), 8, 1.0, EPS, 128.0 ** -0.5, r8q)
            rk = rows_rsqrt([(KG[:, h, :], cv_rdy[8 + h]) for h in range(8)], list(range(8)), 8, 1.0, EPS, 1.0, r8k)
            yield
            for h in range(8):
                ps, rd, pi = X.take()
                mm(ps[:, 0:T], selr[:, h, :], r8q, rd, rq)
                done = mm(ps[:, T:512], selr[:, h, :], r8k, rk, count=True)
                qn = tt(dve, QG[:, h, :], QG[:, h, :], ps[:, 0:T], ALU.mult, done)
                kn = tt(dve, KG[:, h, :], KG[:, h, :], ps[:, T:512], ALU.mult, done)
                X.give(pi, kn)
                ps, rd, pi = X.take()
                mm(ps[:, 0:T], selr[:, h, :], R[0:8, 1, :], rd, g_tok["beta"])
                done = mm(ps[:, T:512], selr[:, h, :], R[0:8, 3, :], g_tok["gc"], count=True)
                kb, kbrd, kbi = TA.take()
                kbt = tt(dve, kb[:, 0:T], KG[:, h, :], ps[:, 0:T], ALU.mult, done, kn, kbrd)
                dc, dcrd, dci = TB.take()
                dk = tt(dve, dc[:, 0:T], ps[:, T:512], mtri[:, 0:T], ALU.add, dcrd)
                dk = tt(dve, dc[:, T:384], ps[:, T + P:512], mtri[:, 256:384], ALU.add)
                X.give(pi, dk)
                actv(dc[:, 0:T], dc[:, 0:T], ACT.Exp, dk, g_tok["tok"], bias=gb_[:, 0, 24 + h:25 + h])
                dk = actv(dc[:, T:384], dc[:, T:384], ACT.Exp, bias=gb_[:, 1, 24 + h:25 + h])
                ps, rd, pi = X.take()
                for i in range(2):
                    done = tr(ps[:, i * P:(i + 1) * P], VG[:, h, i * P:(i + 1) * P], P, rd if i == 0 else None,
                              cv_rdy[16 + h], count=i == 1)
                for i in range(2):
                    vb = actv(VB[:, h, i, :], ps[:, i * P:(i + 1) * P], ACT.Copy, done, g_tok["tok"], scale=gb_[:, i, 16 + h:17 + h])
                X.give(pi, vb)
                vb_rdy[h] = vb
                yield
                p1, rd, i1 = S.take()
                mm(p1[:, 0:T], KG[:, h, 0:P], kb[:, 0:T], rd, kbt)
                done = mm(p1[:, T:384], KG[:, h, P:T], kb[:, P:T], count=True)
                TA.give(kbi, done)
                p2, rd, i2 = S.take()
                mm(p2[:, 0:T], KG[:, h, 0:P], QG[:, h, :], rd, qn)
                done2 = mm(p2[:, T:384], KG[:, h, P:T], QG[:, h, P:T], count=True)
                mt = tt(dve, MT[:, h, :], p1[:, 0:384], dc[:, 0:384], ALU.mult, done, dk, free)
                S.give(i1, mt)
                att = tt(dve, ATT[:, h, :], p2[:, 0:384], dc[:, 0:384], ALU.mult, done2)
                S.give(i2, att)
                TB.give(dci, att)
                mt_rdy[h] = att
                yield

        vb_rdy, mt_rdy = {}, {}
        run(linear(wa, 0, 3 * D, U, u_rdy, conv_epi))
        zg_rdy = [None] * 8

        def silu_epi(dst, rdy, w):
            def epi(pair, ps, done):
                tb, rd, bi = TC.take()
                th = actv(tb, ps, ACT.Tanh, done, rd, scale=0.5)
                tk = stt(dst[:, 2 * pair:2 * pair + 2, :], tb.rearrange("p (c t) -> p c t", t=T), 1.0,
                         ps.rearrange("p (c t) -> p c t", t=T), ALU.add, ALU.mult, th, w)
                TC.give(bi, tk)
                rdy[2 * pair] = rdy[2 * pair + 1] = tk
                return tk
            return epi
        together(delta(), linear(wa, 3 * D, D, U, u_rdy, silu_epi(ZG, zg_rdy, free)))

        freei = now()
        d_rdy = {}

        def inverse(g):
            def mt(u):
                h, i = u // 2, u % 2
                return MT[:, h, 256:384] if i else MT[:, h, 0:128]
            us = list(range(4 * g, 4 * g + 4))
            sl = slice(4 * g, 4 * g + 4)
            rdy = [mt_rdy[2 * g], mt_rdy[2 * g + 1]]
            idb = ident.unsqueeze(1).to_broadcast([P, 4, P])
            dk = ek = None
            for n in range(7):
                mkb = lvlN[:, n, :].unsqueeze(1).to_broadcast([P, 4, P])
                ps, rd, pi = XX[g % 2].take()
                for j, u in enumerate(us):
                    done = mm(ps[:, j * P:(j + 1) * P], mt(u), ident if n == 0 else DM[:, u, :], rd if j == 0 else None,
                              rdy, dk, count=j == 3)
                pk = tt(dve, P1[:, sl, :], ps.rearrange("p (u n) -> p u n", u=4), mkb, ALU.mult, done, freei if n == 0 else None)
                XX[g % 2].give(pi, pk)
                yield
                if n == 0:
                    dk = tt(pool, DM[:, sl, :], idb, P1[:, sl, :], ALU.subtract, pk, freei)
                    t1 = None
                    for j, u in enumerate(us):
                        t1 = tt(pool, DT[:, u, :], mt(u), lvl[:, 0, :], ALU.mult, rdy, freei)
                    ek = tt(pool, DT[:, sl, :], idb, DT[:, sl, :], ALU.subtract, t1)
                    continue
                pa, rda, ia = XX[g % 2].take()
                for j, u in enumerate(us):
                    done = mm(pa[:, j * P:(j + 1) * P], DT[:, u, :], P1[:, u, :], rda if j == 0 else None, pk, ek, count=j == 3)
                pb, rdb, ib = XX[g % 2].take()
                for j, u in enumerate(us):
                    done2 = mm(pb[:, j * P:(j + 1) * P], P1[:, u, :], DT[:, u, :], rdb if j == 0 else None, pk, count=j == 3)
                dk = tt(dve, DM[:, sl, :], DM[:, sl, :], pa.rearrange("p (u n) -> p u n", u=4), ALU.subtract, done, dk)
                XX[g % 2].give(ia, dk)
                ek = tt(dve, DT[:, sl, :], DT[:, sl, :], pb.rearrange("p (u n) -> p u n", u=4), ALU.subtract, done2, ek)
                XX[g % 2].give(ib, ek)
                yield
            d_rdy[g] = [dk, ek]

        lvlN = B(1, 896).rearrange("p (n i) -> p n i", n=7)
        bfree = now()
        for n in range(7):
            ps, rd, pi = X.take()
            tk = tr(ps[:, 0:P], lvl[:, n, :], P, rd, count=True)
            lk = tt_copy(lvlN[:, n, :], ps[:, 0:P], tk, bfree)
            X.give(pi, lk)
        freei = now()
        XX = [Ring([b[:, :] for b in banks[0:4]]), Ring([b[:, :] for b in banks[4:8]])]
        for r in XX:
            r.readers = [freei] * 4
        together(inverse(0), inverse(1))
        together(inverse(2), inverse(3))
        after = now()
        for r in (L, S, X):
            r.readers = [after] * len(r.bufs)

        og_rdy = [None] * 8

        def delta_out(h0):
            for h in range(h0, 8, 2):
                u = 2 * h
                ps, rd, pi = X.take()
                done = mm(ps[:, 0:P], DT[:, u, :], VB[:, h, 0, :], rd, vb_rdy[h], after, count=True)
                uk = actv(UU[:, h, 0, :], ps[:, 0:P], ACT.Copy, done, after)
                X.give(pi, uk)
                yield
                ps, rd, pi = X.take()
                done = mm(ps[:, 0:P], MT[:, h, P:T], UU[:, h, 0, :], rd, uk, count=True)
                rk = tt(dve, VB[:, h, 1, :], VB[:, h, 1, :], ps[:, 0:P], ALU.subtract, done)
                X.give(pi, rk)
                yield
                ps, rd, pi = X.take()
                done = mm(ps[:, 0:P], DT[:, u + 1, :], VB[:, h, 1, :], rd, rk, count=True)
                uk = actv(UU[:, h, 1, :], ps[:, 0:P], ACT.Copy, done, after)
                X.give(pi, uk)
                yield
                ps, rd, pi = S.take()
                mm(ps[:, 0:T], UU[:, h, 0, :], ATT[:, h, 0:T], rd, uk, stop=False)
                done = mm(ps[:, P:T], UU[:, h, 1, :], ATT[:, h, T:384], start=False, count=True)
                ok = actv(OG[:, h, :], ps[:, 0:T], ACT.Copy, done, after)
                S.give(pi, ok)
                og_rdy[h] = ok
                yield
        together(delta_out(0), delta_out(1))
        r8 = rows[0:8, 0, :]
        rk = rows_rsqrt([(OG[:, h, :], og_rdy[h]) for h in range(8)], list(range(8)), 8, 1.0 / 128, EPS, 0.5, r8)
        y_rdy = []
        for h in range(8):
            ps, rd, pi = X.take()
            done = mm(ps[:, 0:T], selr[:, h, :], r8, rd, rk, count=True)
            tk = stt(OG[:, h, :], OG[:, h, :], V("a_onorm_g_2"), ps[:, 0:T], ALU.mult, ALU.mult, done)
            X.give(pi, tk)
            y_rdy.append(tt(pool, OG[:, h, :], OG[:, h, :], ZG[:, h, :], ALU.mult, tk, zg_rdy[h]))
        run(linear(a["a_out_w_2"], 0, D, OG, y_rdy, residual(mods[:, 88:96], mod_rdy[95])))

        n_rdy = normed(None, None, None, U, h_rdy, now(), 5)
        SK = B3(0)
        free = now()
        A2 = sm[:, 144:152]
        a2 = stt(A2, mods[:, 104:112], 1.0, V("norm_g_2")[:, 8:16], ALU.add, ALU.mult, mod_rdy[111])
        s_rdy, u_rdy = [], []
        for c in range(8):
            s_rdy.append(actv(SK[:, c, :], U[:, c, :], ACT.Copy, n_rdy[c], free, scale=V("kv_norm_g_2")[:, c:c + 1]))
            u_rdy.append(ts(dve, U[:, c, :], U[:, c, :], A2[:, c:c + 1], mods[:, 96 + c:97 + c], ALU.mult, ALU.add,
                            s_rdy[c], a2, mod_rdy[103]))

        BT = arena[:, 6 * UNIT:6 * UNIT + 4096].rearrange("p (h n) -> p h n", h=16)
        s_bt = sem("s_bt")
        skew = bass.AP(tensor=scratch.tensor, offset=127, ap=[[383, P], [P * 384, 16], [1, T]])
        sp.dma(lambda e: e.dma_start(BT, skew), s_bt, [(s, 16 * n) for s, n in zip(s_br, (8, 8))], free)
        bt_rdy = (s_bt, 16)

        KW = arena[:, 9 * UNIT:9 * UNIT + 1024].rearrange("p (b g t) -> p b g t", b=2, g=2)
        VW = arena[:, 9 * UNIT + 1024:9 * UNIT + 1536].rearrange("p (b i n) -> p b i n", b=2, i=2)
        BLK = arena[:, 8 * UNIT:8 * UNIT + 960].rearrange("p (s m g n) -> p s m g n", s=2, m=16, g=2)
        HK = arena[:, 8 * UNIT + 960:8 * UNIT + 1080].rearrange("p (s c n) -> p s c n", s=2, c=2)
        KC = arena[:, 8 * UNIT + 1080:8 * UNIT + 1110].rearrange("p (g n) -> p g n", g=2)
        VC = arena[0:15, 8 * UNIT + 1110:8 * UNIT + 1110 + 128]
        blk_rdy, kw_rdy, vw_rdy = [], [], []

        def kv_prep():
            (wv,), arrived, si = load((0, a["kv_w_2"][:, 0:512]))
            for j in range(4):
                if j == 3:
                    for i in range(2):
                        ps, done, pi = token_major(wv, 384, 128, SK, s_rdy, i, None, arrived=arrived)
                        tk = tt_copy(VW[:, 0, i, :], ps[:, 0:128], done, free)
                        L.give(pi, tk)
                        vw_rdy.append(tk)
                    yield
                    continue
                ps, rd, pi = L.take()
                done = group(ps[:, 0:T], [(wv[:, k, j * P:(j + 1) * P], SK[:, k, :]) for k in range(8)],
                             [[arrived, s_rdy[k]] for k in range(8)], rd, count=True)
                if j < 2:
                    pos = V(("cmp_pos_k_2", "cmp_pos_v_2")[j])
                    for g in range(2):
                        for par in range(2):
                            src = ps[64 * g:64 * g + 64, :]
                            src = bass.AP(tensor=src.tensor, offset=src.offset + par, ap=[list(src.ap[0]), [2, 16], [16, 15]])
                            tk = tt(dve, BLK[64 * par:64 * par + 64, j, :, g, :], src,
                                    pos[64 * par:64 * par + 64, :].unsqueeze(2).to_broadcast([64, 16, 15]), ALU.add, done, free)
                            blk_rdy.append(tk)
                    L.give(pi, tk)
                else:
                    yield from dup(ps, pi, done, 0)
                yield
            ring.give(si, done)
            (wv,), arrived, si = load((0, a["kv_w_2"][:, 512:768]))
            ps, rd, pi = L.take()
            done = group(ps[:, 0:T], [(wv[:, k, 0:P], SK[:, k, :]) for k in range(8)], [arrived] * 8, rd, count=True)
            yield from dup(ps, pi, done, 1)
            for i in range(2):
                ps, done, pi = token_major(wv, 128, 128, SK, s_rdy, i, None, arrived=arrived)
                tk = tt_copy(VW[:, 1, i, :], ps[:, 0:128], done, free)
                L.give(pi, tk)
                vw_rdy.append(tk)
            ring.give(si, done)
            yield
            for s in range(2):
                w1 = a[("cmp_k_w1_2", "cmp_v_w1_2")[s]]
                (wv,), arrived, si = load((0, w1))
                for c in range(2):
                    ps, rd, pi = L.take()
                    done = group(ps[:, 0:30], [(wv[:, m, c * P:(c + 1) * P], BLK[:, s, m, :, :]) for m in range(16)],
                                 [[arrived, blk_rdy]] * 16, rd, count=True)
                    tb, rd, bi = TC.take()
                    th = actv(tb[:, 0:30], ps[:, 0:30], ACT.Tanh, done, rd, scale=0.5)
                    tk = stt(tb[:, 0:30], tb[:, 0:30], 1.0, ps[:, 0:30], ALU.add, ALU.mult, th)
                    hk = ts(dve, HK[:, s, c, :], tb[:, 0:30], 0.5, None, ALU.mult, None, tk)
                    TC.give(bi, hk)
                    L.give(pi, tk)
                ring.give(si, done)
                ps, rd, pi = X.take()
                if s == 0:
                    w2 = V("cmp_k_w2_2").rearrange("p (c n) -> p c n", c=2)
                    for half in range(2):
                        for c in range(2):
                            done = mm(ps[64 * half:64 * half + 64, 0:30], w2[:, c, :], HK[:, 0, c, :], rd if half + c == 0 else None, hk,
                                      start=c == 0, stop=c == 1, count=half + c == 2)
                    tk = tt_copy(KC, ps[:, 0:30].rearrange("p (g n) -> p g n", g=2), done)
                    cmp_rdy.append(tk)
                else:
                    w2 = V("cmp_v_w2_2").rearrange("p (c n) -> p c n", c=2)
                    for g in range(2):
                        for c in range(2):
                            done = mm(ps[0:15, 64 * g:64 * g + 64], HK[:, 1, c, 15 * g:15 * g + 15], w2[:, c, :], rd if g + c == 0 else None, hk,
                                      start=c == 0, stop=c == 1, count=g + c == 2)
                    tk = tt_copy(VC, ps[0:15, 0:128], done)
                    cmp_rdy.append(tk)
                X.give(pi, tk)
                yield

        cmp_rdy = []

        def dup(ps, pi, done, b):
            for g in range(2):
                for half in range(2):
                    tk = tt_copy(KW[64 * half:64 * half + 64, b, g, :], ps[64 * g:64 * g + 64, 0:T], done, free)
            kw_rdy.append(tk)
            L.give(pi, tk)
            yield

        QN, YN = B3(1), B3(5)
        ZS = [B3(2), B3(3), B3(4)]
        wb = a["b_in_w_2"]
        qn_rdy = [None] * 8
        zs_rdy = [[None] * 8 for _ in range(3)]

        def q_epi(pair, ps, done):
            tk = actv(QN[:, 2 * pair:2 * pair + 2, :], ps.rearrange("p (c t) -> p c t", t=T), ACT.Copy, done, free, scale=0.125)
            qn_rdy[2 * pair] = qn_rdy[2 * pair + 1] = tk
            return tk

        gates = sb("gates", [P, 2, 48])
        g3 = sb("g3", [P, 2, 16, 8])

        def zhalf(hf):
            for b in range(3):
                def epi(pair, ps, done, b=b):
                    return silu_epi(ZS[b], zs_rdy[b], free)(pair + 2 * hf, ps, done)
                yield from linear(wb, D * (1 + b) + 512 * hf, 512, U, u_rdy, epi)

        together(kv_prep(), linear(wb, 0, D, U, u_rdy, q_epi))
        (wv,), arrived, si = load((0, wb[:, 4096:4144]))
        for i in range(2):
            ps, done, pi = token_major(wv, 0, 48, U, u_rdy, i, None, arrived=arrived)
            tk = actv(gates[:, i, :], ps[:, 0:48], ACT.Tanh, done, scale=0.5)
            L.give(pi, tk)
        ring.give(si, done)
        gt_rdy = ts(dve, gates[:, :, :], gates[:, :, :], 1.0, 0.25, ALU.add, ALU.mult, tk)

        CE = sb("CE", [P, 2, 24])
        CT = rows[:, 1:3, :]
        ceR = Ring([CE[:, i, :] for i in range(2)])
        ctR = Ring([CT[:, i, :] for i in range(2)])
        m15 = C("m15")
        y_rdy = [None] * 8

        def nsa(j):
            g = j // 4
            for b in (1, 2, 0):
                op_, ord_, oi = X.take()
                for half in range(2):
                    h = 2 * j + half
                    lo = 64 * half
                    q = QN[lo:lo + 64, j, :]
                    gcl = [gates[:, i, 16 * b + h:16 * b + h + 1] for i in range(2)]
                    s_, srd, s_i = stR.take()
                    ps, rd, pi = S.take()
                    if b:
                        k = KW[lo:lo + 64, b - 1, g, :]
                        mm(ps[:, 0:128], q[:, 0:128], k[:, 0:128], rd, qn_rdy[j], kw_rdy)
                        done = mm(ps[:, 128:384], q[:, 128:256], k[:, 0:256], count=True)
                        ev, erd, ei = eb.take()
                        E = ev[:, 0, :]
                        tiles = [(0, 0, 128, BT[:, h, 128:256]), (1, 128, 384, BT[:, h, :])]
                    else:
                        k = KC[lo:lo + 64, g, :]
                        mm(ps[:, 0:7], q[:, 0:128], k[:, 0:7], rd, qn_rdy[j], cmp_rdy)
                        done = mm(ps[:, 7:22], q[:, 128:256], k[:, 0:15], count=True)
                        ev, erd, ei = ceR.take()
                        E = ev
                        tiles = [(0, 0, 7, BT[:, h, 159:256:16]), (1, 7, 22, BT[:, h, 31:256:16])]
                    for i, a0, a1, bias in tiles:
                        mk = dve(lambda e, E=E, a0=a0, a1=a1, ps=ps, bias=bias, s_=s_, i=i: e.tensor_tensor_reduce(
                            E[:, a0:a1], ps[:, a0:a1], bias, 1.0, -3e38, ALU.add, ALU.max, s_[:, i:i + 1]), done, erd, srd, bt_rdy)
                    S.give(pi, mk)
                    nm = ts(dve, s_[:, 2:4], s_[:, 0:2], -1.0, None, ALU.mult, None, mk)
                    yield
                    for i, a0, a1, bias in tiles:
                        kw = {"accum_out": s_[:, 4 + i:5 + i]} if b else {}
                        ex = actv(E[:, a0:a1], E[:, a0:a1], ACT.Exp, nm, bias=s_[:, 2 + i:3 + i], **kw)
                    if b == 0:
                        for i, a0, a1, bias in tiles:
                            ex = dve(lambda e, E=E, a0=a0, a1=a1, s_=s_, i=i: e.tensor_tensor_reduce(
                                E[:, a0:a1], E[:, a0:a1], m15[:, a0:a1], 1.0, 0.0, ALU.mult, ALU.add, s_[:, 4 + i:5 + i]), ex)
                        ex = ts(dve, s_[:, 4:6], s_[:, 4:6], 1e-30, None, ALU.max, None, ex)
                    rk = dve(lambda e, s_=s_: e.reciprocal(s_[:, 6:8], s_[:, 4:6]), ex)
                    for i, a0, a1, bias in tiles:
                        pk = ts(dve, E[:, a0:a1], E[:, a0:a1], s_[:, 6 + i:7 + i], gcl[i], ALU.mult, ALU.mult, rk, gt_rdy)
                    stR.give(s_i, pk)
                    yield
                    if b:
                        aT, tk, ti, trd = transposed3(E, pk)
                        eb.give(ei, trd)
                        o_ = op_[lo:lo + 64, 0:T]
                        mm(o_, VW[:, b - 1, 0, 64 * g:64 * g + 64], aT[:, 0:T], ord_ if half == 0 else None, tk, vw_rdy, stop=False)
                        od = mm(op_[lo:lo + 64, P:T], VW[:, b - 1, 1, 64 * g:64 * g + 64], aT[:, T:384], start=False, count=True)
                        at.give(ti, od)
                    else:
                        tp, rd, ti = S.take()
                        tr(tp[0:7, 0:128], E[:, 0:7], P, rd, pk)
                        done = tr(tp[0:15, 128:256], E[:, 7:22], P, count=True)
                        ceR.give(ei, done)
                        ct, crd, ci = ctR.take()
                        c1 = actv(ct[0:7, 0:128], tp[0:7, 0:128], ACT.Copy, done, crd)
                        c1 = actv(ct[0:15, 128:256], tp[0:15, 128:256], ACT.Copy)
                        S.give(ti, c1)
                        mm(op_[lo:lo + 64, 0:128], VC[0:7, 64 * g:64 * g + 64], ct[0:7, 0:128], ord_ if half == 0 else None, c1, cmp_rdy)
                        od = mm(op_[lo:lo + 64, 128:256], VC[0:15, 64 * g:64 * g + 64], ct[0:15, 128:256], count=True)
                        ctR.give(ci, od)
                    yield
                zr = zs_rdy[b][j]
                if b == 1:
                    yk = tt(dve, YN[:, j, :], op_[:, 0:T], ZS[b][:, j, :], ALU.mult, od, zr, free)
                    X.give(oi, yk)
                else:
                    tb, rd, bi = TB.take()
                    tk = tt(dve, tb[:, 0:T], op_[:, 0:T], ZS[b][:, j, :], ALU.mult, od, zr, rd)
                    X.give(oi, tk)
                    yk = tt(pool, YN[:, j, :], YN[:, j, :], tb[:, 0:T], ALU.add, tk, yk)
                    TB.give(bi, yk)
            y_rdy[j] = yk

        run(zhalf(0))
        together(seq(nsa(0), nsa(1), nsa(2), nsa(3)), zhalf(1))
        run(seq(nsa(4), nsa(5), nsa(6), nsa(7)))
        run(linear(a["b_out_w_2"], 0, D, YN, y_rdy, residual(mods[:, 112:120], mod_rdy[119])))

        n_rdy = normed(None, None, None, U, h_rdy, now(), 6)
        s_out = sem("s_out")
        for c in range(8):
            tk = ts(dve, U[:, c, :], U[:, c, :], V("final_g_2")[:, c:c + 1], None, ALU.mult, None, n_rdy[c])
            sp.dma(lambda e, c=c: e.dma_start(out[c * P:(c + 1) * P, :], U[:, c, :]), s_out, tk)
        sp.items.append(([(s_out, 128)] + [(s, 128) for s in s_br], None, None))

        block = ctx.enter_context(nc.Block())
        block.sync(lambda e: sp.emit(e))
        block.tensor(lambda e: pe.emit(e))
        block.vector(lambda e: dve.emit(e))
        block.scalar(lambda e: act.emit(e))
        block.gpsimd(lambda e: pool.emit(e))


def kernel(**inputs):
    import concourse.bacc as _bacc
    from concourse.bass_utils import run_bass_kernel_spmd as _run

    nc = _bacc.Bacc("TRN2", target_bir_lowering=False, num_devices=1)
    x = {k: np.asarray(v) for k, v in inputs.items()}
    arrays = {"vec": vectors(x), "cst": constants(), "xT": np.ascontiguousarray(x["x"][0].T),
              "ada_w1": x["ada_w_2"][0], "ada_w2": x["ada_w_2"][1]}
    for n in ("w_ada", "w1_gate", "w1_up", "w1_down", "w_in", "w_proj_a", "w_proj_b", "w_out", "w2_gate", "w2_up",
              "w2_down", "a_in_w_2", "a_out_w_2", "b_in_w_2", "b_out_w_2"):
        arrays[n] = x[n][0]
    for n in ("w_mq", "w_mk", "w_mv"):
        arrays[n] = x[n][0].reshape(1024, 256)
    for n in ("kv_w_2", "cmp_k_w1_2", "cmp_v_w1_2"):
        arrays[n] = x[n]
    feed, aps = {}, {}
    for n, v in arrays.items():
        v = np.ascontiguousarray(v)
        feed[f"in_{n}"] = v
        aps[n] = nc.dram_tensor(f"in_{n}", v.shape, F32, kind="ExternalInput").ap()
    out = nc.dram_tensor("out_T", (D, T), F32, kind="ExternalOutput").ap()
    scratch = nc.dram_tensor("bias_rows", (16, P, 384), F32, kind="Internal").ap()
    build(nc, aps, out, scratch)
    r = _run(nc, [feed], core_ids=[0])
    return np.ascontiguousarray(r.results[0]["out_T"].T)[None]
```

```python
from contextlib import ExitStack

import numpy as np

import concourse.bass as bass
from concourse import mybir

P = 128
T = 256
D = 1024
DFF = 2816
F32 = mybir.dt.float32
ALU = mybir.AluOpType
ACT = mybir.ActivationFunctionType
AX = mybir.AxisListType
NEG = -1e30
EPS = 1e-6
UNIT = 2080
SLOT = 4096
NSLOT = 4

VEC = [("c", 8), ("b_ada", 72), ("g_ff1", 8), ("g_mix", 8), ("g_subln", 1), ("conv_w", 32), ("conv_b", 8),
       ("ml_skip", 8), ("g_mlnorm", 8), ("g_ff2", 8), ("g_final", 8), ("c_2", 8), ("ada_b_2", 48),
       ("norm_g_2", 16), ("a_conv_w_2", 96), ("a_onorm_g_2", 1), ("kv_norm_g_2", 8), ("final_g_2", 8),
       ("cmp_pos_k_2", 16), ("cmp_pos_v_2", 16), ("w_if", 192), ("cmp_k_w2_2", 128), ("cmp_v_w2_2", 128),
       ("b_i", 1), ("b_f", 1), ("a_dt_bias_2", 1), ("a_A_log_2", 1), ("rel_bias_2", 16)]
CST = [("ident", 128), ("ones", 128), ("mblk", 256),
       ("mtri", 384), ("selc", 64), ("selr", 8 * 128), ("m15", 22)]


def offsets(table):
    out, at = {}, 0
    for name, n in table:
        out[name] = (at, n)
        at += n
    return out, at


VO, VN = offsets(VEC)
CO, CN = offsets(CST)


def constants():
    c = np.zeros((P, CN), np.float32)

    def put(name, a):
        o, n = CO[name]
        a = np.asarray(a, np.float32).reshape(a.shape[0], -1)
        assert a.shape[1] == n, (name, a.shape)
        c[:a.shape[0], o:o + n] = a

    i = np.arange(P)
    put("ident", np.eye(P))
    put("ones", np.ones((P, P)))
    rot = np.zeros((P, P))
    for p in range(P):
        d = p % 64
        if d < 32:
            rot[p + 32, p] = -1.0
        else:
            rot[p - 32, p] = 1.0
    inv = np.float32(10000.0) ** (-np.arange(0, 64, 2, dtype=np.float32) / np.float32(64))
    ang = np.arange(T, dtype=np.float32)[:, None] * inv.astype(np.float32)[None, :]
    rope = np.concatenate([rot, np.cos(ang).T[i % 32], np.sin(ang).T[i % 32]], 1).astype(np.float32)
    mblk = np.zeros((P, 256))
    mblk[0:64, 192:256] = NEG
    put("mblk", mblk)
    tri = np.where(i[None, :] >= i[:, None], 0.0, NEG)
    put("mtri", np.concatenate([tri, np.zeros((P, P)), tri], 1))
    lv = np.zeros((P, 7, P))
    for n in range(7):
        b = 1 << n
        bi, bj = i[None, :] // b, i[:, None] // b
        lv[:, n, :] = (bj % 2 == 0) & (bi == bj + 1)
    sc = np.zeros((P, 8, 8))
    sr = np.zeros((8, 8, P))
    for h in range(8):
        sc[:, h, h] = 1.0
        sr[h, h, :] = 1.0
    put("selc", sc)
    put("selr", sr)
    delta = 255 - np.arange(384)
    n = np.maximum(delta, 0)
    nf = np.maximum(n, 1).astype(np.float32)
    large = 16 + (np.log(nf / np.float32(16)) / np.float32(np.log(128 / 16)) * np.float32(16)).astype(np.int32)
    bucket = np.where(n < 16, n, np.minimum(large, 31))
    oh = np.zeros((33, 384))
    for j in range(384):
        if delta[j] >= 0:
            oh[bucket[j], j] = 1.0
        else:
            oh[32, j] = NEG
    m = np.zeros((P, 22))
    for q in range(7):
        m[:, q] = i - 16 * q - 31 >= 0
    for q in range(15):
        m[:, 7 + q] = i + 128 - 16 * q - 31 >= 0
    put("m15", m)
    lvls = np.concatenate([lv, lv.transpose(2, 1, 0)], 1).reshape(P, -1).astype(np.float32)
    return c, lvls, oh.astype(np.float32), rope


def vectors(x):
    v = np.zeros((P, VN), np.float32)

    def put(name, a):
        o, n = VO[name]
        a = a.reshape(a.shape[0], -1)
        assert a.shape[1] == n, (name, a.shape)
        v[:a.shape[0], o:o + n] = a

    def cols(a):
        return np.asarray(a).reshape(-1, P).T

    for name in ("c", "b_ada", "g_ff1", "g_mix", "g_subln", "conv_w", "conv_b", "ml_skip", "g_mlnorm", "g_ff2",
                 "g_final", "c_2", "ada_b_2", "norm_g_2", "a_conv_w_2", "a_onorm_g_2", "kv_norm_g_2", "final_g_2",
                 "cmp_pos_k_2", "cmp_pos_v_2"):
        put(name, cols(x[name]))
    for name in ("w_if", "cmp_k_w2_2", "cmp_v_w2_2"):
        a = np.asarray(x[name])
        put(name, a.reshape(-1, P, a.shape[-1]).transpose(1, 0, 2))
    b = np.asarray(x["b_if"]).reshape(8, 1)
    put("b_i", b[0:4])
    put("b_f", b[4:8])
    put("a_dt_bias_2", np.asarray(x["a_dt_bias_2"]).reshape(8, 1))
    put("a_A_log_2", np.asarray(x["a_A_log_2"]).reshape(8, 1))
    lam = np.concatenate([np.asarray(x[k]).reshape(1, 64) for k in ("lambda_q1", "lambda_q2", "lambda_k1", "lambda_k2")], 1)
    put("rel_bias_2", np.concatenate([np.asarray(x["rel_bias_2"]), np.ones((1, 16), np.float32)], 0))
    return v, lam


class Queue:

    def __init__(self, sem):
        self.sem, self.n, self.items = sem, 0, []

    def __call__(self, fn, *waits, count=True):
        if count:
            self.n += 1
        self.items.append((flat(waits), fn, (self.sem, 1) if count else None))
        return (self.sem, self.n)

    def dma(self, fn, sem, *waits):
        self.items.append((flat(waits), fn, (sem, 16)))

    def emit(self, eng):
        seen = {}
        for waits, fn, inc in self.items:
            need = {}
            for s, v in waits:
                if v > max(seen.get(id(s), 0), need.get(id(s), (s, 0))[1]):
                    need[id(s)] = (s, v)
            for k, (s, v) in need.items():
                eng.wait_ge(s, v)
                seen[k] = v
            ins = fn(eng) if fn is not None else None
            if inc is not None:
                ins.then_inc(*inc)


def flat(x):
    if x is None:
        return []
    if isinstance(x, list) or (isinstance(x, tuple) and not (len(x) == 2 and isinstance(x[1], int))):
        return [y for e in x for y in flat(e)]
    return [x]


class Ring:

    def __init__(self, bufs):
        self.bufs, self.i, self.readers = bufs, -1, [[] for _ in bufs]

    def take(self):
        self.i = (self.i + 1) % len(self.bufs)
        assert self.readers[self.i] is not None, "still in use"
        r, self.readers[self.i] = self.readers[self.i], None
        return self.bufs[self.i], r, self.i

    def give(self, i, *toks):
        self.readers[i] = flat(toks)


def together(*gens):
    gens = list(gens)
    while gens:
        for g in list(gens):
            try:
                next(g)
            except StopIteration:
                gens.remove(g)


def seq(*gens):
    for g in gens:
        yield from g


def beside(main, side, every=1):
    n = 0
    for _ in main:
        n += 1
        if n % every == 0:
            next(side, None)


def run(gen):
    for _ in gen:
        pass


def build(nc, a, out, scratch):
    ctx = ExitStack()
    with ctx:
        def sb(name, shape):
            return ctx.enter_context(nc.sbuf_tensor(name, shape, F32))

        def sem(name):
            return ctx.enter_context(nc.semaphore(name))

        pe, dve, act, pool, sp = (Queue(sem("s_" + n)) for n in ("pe", "dve", "act", "pool", "sp"))

        vec = sb("vec", [P, VN])
        cst = sb("cst", [P, CN])
        H = sb("H", [P, 8, T])
        U = sb("U", [P, 8, T])
        arena = sb("arena", [P, 10 * UNIT])
        slots = sb("slots", [P, NSLOT, SLOT])
        mods = sb("mods", [P, 72 + 48])
        sm = sb("sm", [P, 192])
        rstd = sb("rstd", [P, T])
        tmpA = sb("tmpA", [P, 3, 512])
        tmpB = sb("tmpB", [P, 3, 512])
        tmpC = sb("tmpC", [P, 2, 512])
        banks = [ctx.enter_context(nc.psum_tensor(f"ps{i}", [P, 512], F32)) for i in range(8)]
        L = Ring([b[:, :] for b in banks[0:3]])
        S = Ring([b[:, :] for b in banks[3:5]])
        X = Ring([b[:, :] for b in banks[5:8]])
        TA = Ring([tmpA[:, i, :] for i in range(3)])
        TB = Ring([tmpB[:, i, :] for i in range(3)])
        TC = Ring([tmpC[:, i, :] for i in range(2)])

        def V(name, r=P):
            o, n = VO[name]
            return vec[0:r, o:o + n]

        def C(name, r=P):
            o, n = CO[name]
            return cst[0:r, o:o + n]

        def B(i, n=2048):
            return arena[:, i * UNIT:i * UNIT + n]

        def B3(i):
            return B(i).rearrange("p (c t) -> p c t", t=T)

        def now():
            return [(q.sem, q.n) for q in (pe, dve, act, pool)]

        ident = C("ident")
        selc = C("selc").rearrange("p (h m) -> p h m", h=8)
        selr = C("selr", 8).rearrange("p (h m) -> p h m", h=8)
        mtri = C("mtri")
        mblk = C("mblk")

        s_vec, s_cst = sem("s_vec"), sem("s_cst")
        s_x = sem("s_x")
        sp.dma(lambda e: e.dma_start(vec[:, :], a["vec"]), s_vec)
        act.dma(lambda e: e.dma_start(cst[:, :], a["cst"]), s_cst)
        s_oh, s_lvl, s_rope, s_lam = sem("s_oh"), sem("s_lvl"), sem("s_rope"), sem("s_lam")
        rope = arena[:, 9 * UNIT + 384:9 * UNIT + 1024]
        lamv = arena[0:1, 9 * UNIT + 1024:9 * UNIT + 1280]
        act.dma(lambda e: e.dma_start(rope, a["rope"]), s_rope)
        act.dma(lambda e: e.dma_start(lamv, a["lam"]), s_lam)
        oneh = arena[0:33, 9 * UNIT:9 * UNIT + 384]
        act.dma(lambda e: e.dma_start(oneh, a["oh"]), s_oh)
        vec_in, cst_in = (s_vec, 16), (s_cst, 16)
        act.dma(lambda e: e.dma_start(H[:, :, :], a["xT"].rearrange("(c p) t -> p c t", p=P)), s_x)
        x_in = (s_x, 16)

        s_slot = [sem(f"s_slot{i}") for i in range(NSLOT)]
        slot_n = [0] * NSLOT
        ring = Ring([slots[:, i, :] for i in range(NSLOT)])

        def load(*parts):
            buf, readers, i = ring.take()
            views = []
            for off, src in parts:
                kc, n = src.shape[0] // P, src.shape[1]
                v = buf[:, off:off + kc * n].rearrange("p (k n) -> p k n", n=n)
                s = src.rearrange("(k p) n -> p k n", p=P)
                sp.dma(lambda e, v=v, s=s: e.dma_start(v, s), s_slot[i], readers)
                slot_n[i] += 16
                views.append(v)
            return views, (s_slot[i], slot_n[i]), i

        def mm(out_, lhsT, rhs, *waits, start=True, stop=True, count=False):
            return pe(lambda e: e.matmul(out_, lhsT, rhs, start=start, stop=stop), *waits, count=count)

        def tr(out_, in_, n, *waits, count=False):
            return pe(lambda e: e.transpose(out_, in_, ident[0:n, 0:n]), *waits, count=count)

        def actv(out_, in_, f, *waits, **kw):
            return act(lambda e: e.activation(out_, in_, f, **kw), *waits)

        def tt(q, out_, i0, i1, op, *waits):
            return q(lambda e: e.tensor_tensor(out_, i0, i1, op), *waits)

        def ts(q, out_, i0, s1, s2, op0, op1, *waits):
            if op1 is None:
                return q(lambda e: e.tensor_scalar(out_, i0, s1, None, op0), *waits)
            return q(lambda e: e.tensor_scalar(out_, i0, s1, s2, op0, op1), *waits)

        def stt(out_, i0, s, i1, op0, op1, *waits):
            return dve(lambda e: e.scalar_tensor_tensor(out=out_, in0=i0, scalar=s, in1=i1, op0=op0, op1=op1), *waits)

        def group(out_, pairs, rdy, waits, count=False):
            tok = None
            for n, (l, r) in enumerate(pairs):
                tok = mm(out_, l, r, rdy[n] if rdy else None, waits if n == 0 else None,
                         start=n == 0, stop=n == len(pairs) - 1, count=count and n == len(pairs) - 1)
            return tok

        cs = sm[:, 0:16]
        t_c = actv(sm[:, 16:24], V("c"), ACT.Tanh, vec_in, scale=0.5)
        t_c = actv(sm[:, 24:32], V("c_2"), ACT.Tanh, scale=0.5)
        t = stt(cs[:, 0:8], sm[:, 16:24], 1.0, V("c"), ALU.add, ALU.mult, t_c)
        t = stt(cs[:, 8:16], sm[:, 24:32], 1.0, V("c_2"), ALU.add, ALU.mult, t_c)
        cs_rdy = ts(dve, cs, cs, 0.5, None, ALU.mult, None, t)
        mod_rdy = {}

        def ada(w, first, blocks, vec0, bias):
            for b0 in range(blocks[0], blocks[1], 4):
                (wv,), arrived, si = load((0, w[:, b0 * P:(b0 + 4) * P]))
                acc, rd, ai = TA.take()
                tok = ts(dve, acc, wv[:, 0, :], cs[:, vec0:vec0 + 1], None, ALU.mult, None, rd, arrived, cs_rdy)
                for k in range(1, 8):
                    tok = stt(acc, wv[:, k, :], cs[:, vec0 + k:vec0 + k + 1], acc, ALU.mult, ALU.add, tok)
                ring.give(si, tok)
                yield
                ps, rd, pi = L.take()
                for j in range(4):
                    done = tr(ps[:, j * P:(j + 1) * P], acc[:, j * P:(j + 1) * P], P, rd if j == 0 else None, tok, cst_in,
                              count=j == 3)
                TA.give(ai, done)
                c0 = first + b0
                mc = mods[:, c0:c0 + 4]
                tok = dve(lambda e, mc=mc, ps=ps: e.tensor_reduce(mc, ps.rearrange("p (j n) -> p j n", j=4), AX.X, ALU.add), done)
                L.give(pi, tok)
                tok = tt(dve, mc, mc, bias[:, b0:b0 + 4], ALU.add, tok, vec_in)
                for j in range(4):
                    mod_rdy[c0 + j] = tok

        def ada_both():
            yield from ada(a["ada_w1"], 72, (0, 24), 8, V("ada_b_2")[:, 0:24])
            yield from ada(a["ada_w2"], 96, (0, 24), 8, V("ada_b_2")[:, 24:48])

        def normed(gcol, sc0, sh0, dst, src_rdy, dst_free, tag):
            A = sm[:, 32 + 8 * tag:40 + 8 * tag]
            if sc0 is not None:
                a_rdy = stt(A, mods[:, sc0:sc0 + 8], 1.0, gcol, ALU.add, ALU.mult, mod_rdy[sc0 + 7], now())
            actv(sm[:, 30:31], eps, ACT.Sqrt, eps_rdy)
            for c2 in range(4):
                tb, rd, bi = TA.take()
                sq = actv(tb[:, :].rearrange("p (c t) -> p c t", t=T), H[:, 2 * c2:2 * c2 + 2, :], ACT.Square, rd,
                          src_rdy[2 * c2:2 * c2 + 2])
                if c2 == 0:
                    ps, rd, pi = X.take()
                for j in range(2):
                    last = mm(ps[:, 0:T], C("ones"), tb[:, j * T:(j + 1) * T], rd if c2 + j == 0 else None, sq, cst_in,
                              start=c2 + j == 0, stop=c2 == 3 and j == 1, count=j == 1)
                TA.give(bi, last)
            sq = actv(rstd[:, :], ps[:, 0:T], ACT.Sqrt, last, eps_rdy, now(), bias=eps, scale=1.0 / D)
            X.give(pi, sq)
            r = dve(lambda e: e.reciprocal(rstd[:, :], rstd[:, :]), sq)
            toks = []
            for c in range(8):
                tk = tt(dve, dst[:, c, :], H[:, c, :], rstd[:, :], ALU.mult, r, dst_free if c == 0 else None)
                if sc0 is not None:
                    tk = actv(dst[:, c, :], dst[:, c, :], ACT.Identity, tk, a_rdy, mod_rdy[sh0 + 7],
                              scale=A[:, c:c + 1], bias=mods[:, sh0 + c:sh0 + c + 1])
                toks.append(tk)
            return toks

        eps = sm[:, 31:32]
        eps_rdy = dve(lambda e: e.memset(eps, EPS), t)

        def linear(w, c0, cols, rhs, rdy, epi, width=512):
            kc = w.shape[0] // P
            for b in range(0, cols, width):
                if kc * width <= SLOT:
                    (wv,), arrived, si = load((0, w[:, c0 + b:c0 + b + width]))
                    pieces = [(wv, arrived, si, 0, kc)]
                else:
                    hk = kc // 2
                    pieces = []
                    for n in range(2):
                        (wv,), arrived, si = load((0, w[n * hk * P:(n + 1) * hk * P, c0 + b:c0 + b + width]))
                        pieces.append((wv, arrived, si, n * hk, hk))
                for j2 in range(width // 256):
                    ps, rd, pi = L.take()
                    for j in range(2):
                        o = j2 * 256 + j * 128
                        prs, rr = [], []
                        for wv, arrived, si, k0, n in pieces:
                            for k in range(n):
                                prs.append((wv[:, k, o:o + P], rhs[:, k0 + k, :]))
                                rr.append([arrived, rdy[k0 + k]])
                        done = group(ps[:, j * T:(j + 1) * T], prs, rr, rd, count=j == 1)
                    if j2 == width // 256 - 1:
                        for p in pieces:
                            ring.give(p[2], done)
                    L.give(pi, epi((b + j2 * 256) // 256, ps, done))
                    yield

        def ffn(wg, wu, wd, u_rdy, gate0, h_rdy):
            free = now()
            actT = arena[:, 0:22 * T].rearrange("p (c t) -> p c t", t=T)
            rdy = []
            for b in range(11):
                (g_, u_), arrived, si = load((0, wg[:, b * 256:(b + 1) * 256]), (2048, wu[:, b * 256:(b + 1) * 256]))
                for j in range(2):
                    ps, rd, pi = L.take()
                    group(ps[:, 0:T], [(g_[:, k, j * P:(j + 1) * P], U[:, k, :]) for k in range(8)],
                          [[arrived, u_rdy[k]] for k in range(8)], rd)
                    done = group(ps[:, T:2 * T], [(u_[:, k, j * P:(j + 1) * P], U[:, k, :]) for k in range(8)],
                                 None, None, count=True)
                    tb, rd, bi = TB.take()
                    tk = actv(tb[:, 0:T], ps[:, 0:T], ACT.Tanh, done, rd, scale=0.5)
                    tk = stt(tb[:, T:512], tb[:, 0:T], 1.0, ps[:, 0:T], ALU.add, ALU.mult, tk)
                    tk = tt(dve, actT[:, 2 * b + j, :], tb[:, T:512], ps[:, T:512], ALU.mult, tk, free)
                    TB.give(bi, tk)
                    L.give(pi, tk)
                    rdy.append(tk)
                ring.give(si, done)
                yield
            gq = ts(dve, sm[:, 96:104], mods[:, gate0:gate0 + 8], 0.25, None, ALU.mult, None, mod_rdy[gate0 + 7], now())

            def epi(pair, ps, done):
                for j in range(2):
                    c = 2 * pair + j
                    h_rdy[c] = stt(H[:, c, :], ps[:, j * T:(j + 1) * T], sm[:, 96 + c:97 + c], H[:, c, :],
                                   ALU.mult, ALU.add, done, gq, h_rdy[c])
                return h_rdy[c]
            yield from linear(wd, 0, D, actT, rdy, epi, width=256)

        def rows_rsqrt(srcs, rowof, nrow, scale, e, post, dst8, sq_to=None):
            ps, rd, pi = X.take()
            for n, (s, tk) in enumerate(srcs):
                tb, trd, bi = TC.take()
                sq = actv(tb[:, 0:T], s, ACT.Square, trd, tk)
                last = mm(ps[0:8, 0:T], selc[:, rowof[n], :], tb[:, 0:T], rd if n == 0 else None, sq,
                          start=n == 0, stop=n == len(srcs) - 1, count=True)
                TC.give(bi, last)
            tk = ts(dve, dst8, ps[0:8, 0:T], scale / post ** 2, e / post ** 2, ALU.mult, ALU.add, last, now())
            X.give(pi, tk)
            tk = actv(dst8, dst8, ACT.Sqrt, tk)
            return dve(lambda en: en.reciprocal(dst8, dst8), tk)

        s_br = [sem("s_br0"), sem("s_br1")]

        def bias_rows():
            for h in range(16):
                ps, rd, pi = X.take()
                rb = V("rel_bias_2", 33)[:, h:h + 1].to_broadcast([33, P])
                done = mm(ps[:, 0:384], rb, oneh, rd, vec_in, (s_oh, 16), count=True)
                tb, rd, bi = TC.take()
                tk = dve(lambda e, tb=tb, ps=ps: e.tensor_copy(tb[:, 0:384], ps[:, 0:384]), done, rd)
                X.give(pi, tk)
                pool.dma(lambda e, h=h, tb=tb: e.dma_start(scratch[h, :, :], tb[:, 0:384]), s_br[h % 2], tk)
                TC.give(bi, (s_br[h % 2], 16 * (h // 2 + 1)))
                yield

        run(ada(a["w_ada"], 0, (0, 16), 0, V("b_ada")))
        h_rdy = [x_in] * 8
        u_rdy = normed(V("g_ff1"), 8, 0, U, h_rdy, None, 0)
        ada1 = ada(a["w_ada"], 0, (16, 72), 0, V("b_ada"))
        side = seq(ada1, bias_rows())
        beside(ffn(a["w1_gate"], a["w1_up"], a["w1_down"], u_rdy, 16, h_rdy), side)
        while 71 not in mod_rdy:
            next(side)
        u_rdy = normed(V("g_mix"), 32, 24, U, h_rdy, now(), 1)

        lv = lamv
        l1 = tt(dve, tmpA[0:1, 0, 0:128], lv[:, 0:128], lv[:, 128:256], ALU.mult, now(), (s_lam, 16))
        l2 = dve(lambda e: e.tensor_reduce(sm[0:1, 106:108], tmpA[0:1, 0, 0:128].rearrange("p (a n) -> p a n", a=2), AX.X, ALU.add), l1)
        TA.give(0, l2)
        l2 = actv(sm[0:1, 106:108], sm[0:1, 106:108], ACT.Exp, l2)
        l2 = stt(sm[0:1, 108:109], sm[0:1, 106:107], -1.0, sm[0:1, 107:108], ALU.mult, ALU.add, l2)
        l2 = ts(dve, sm[0:1, 108:109], sm[0:1, 108:109], -(0.8 - 0.6), None, ALU.add, None, l2)
        ps, rd, pi = X.take()
        l2 = mm(ps[:, 0:1], C("ones", 1), sm[0:1, 108:109], rd, l2, count=True)
        lam_rdy = actv(sm[:, 109:110], ps[:, 0:1], ACT.Copy, l2)
        X.give(pi, lam_rdy)
        nlam = sm[:, 109:110]

        w_in = a["w_in"]
        QR, KR, YA = B3(0), B3(1), B3(3)
        VA = B(2).rearrange("p (i n) -> p i n", i=2)
        qk_rdy = {}
        free0 = now()

        def rope_epi(dst, key):
            def epi(pair, ps, done):
                tb, rd, bi = TA.take()
                raw = actv(tb, ps, ACT.Copy, done, rd)
                p2, rd2, pi2 = X.take()
                rt = mm(p2, rope[:, 0:128], tb, raw, rd2, (s_rope, 16), count=True)
                tb2, rd3, bi2 = TB.take()
                cosb = rope[:, 128:384].unsqueeze(1).to_broadcast([P, 2, T])
                sinb = rope[:, 384:640].unsqueeze(1).to_broadcast([P, 2, T])
                d3 = dst[:, 2 * pair:2 * pair + 2, :]
                a1 = tt(pool, d3, tb.rearrange("p (c t) -> p c t", t=T), cosb, ALU.mult, raw, free0, (s_rope, 16))
                b1 = tt(dve, tb2.rearrange("p (c t) -> p c t", t=T), p2.rearrange("p (c t) -> p c t", t=T), sinb, ALU.mult, rt, rd3)
                X.give(pi2, b1)
                TA.give(bi, rt, a1)
                s = tt(dve, d3, d3, tb2.rearrange("p (c t) -> p c t", t=T), ALU.add, a1, b1)
                TB.give(bi2, s)
                qk_rdy[(key, 2 * pair)] = qk_rdy[(key, 2 * pair + 1)] = s
                return raw
            return epi

        beside(linear(w_in, 0, D, U, u_rdy, rope_epi(QR, "q")), side)
        beside(linear(w_in, D, D, U, u_rdy, rope_epi(KR, "k")), side)

        def token_major(w, c0, n, src, rdy, i, waits, view=None, arrived=None):
            ps, rd, pi = L.take()
            done = group(ps[:, 0:n], [(src[:, k, i * P:(i + 1) * P], w[:, k, c0:c0 + n]) for k in range(8)],
                         [[arrived, rdy[k]] for k in range(8)], rd, count=True)
            return ps, done, pi

        va_rdy = []
        for b in range(2):
            (wv,), arrived, si = load((0, w_in[:, 2 * D + b * 512:2 * D + (b + 1) * 512]))
            for i in range(2):
                ps, done, pi = token_major(wv, 0, 512, U, u_rdy, i, None, arrived=arrived)
                tk = actv(VA[:, i, b * 512:(b + 1) * 512], ps, ACT.Copy, done, free0)
                L.give(pi, tk)
                va_rdy.append(tk)
            ring.give(si, done)

        EB = arena[:, 7 * UNIT:7 * UNIT + 3072].rearrange("p (n c k) -> p n c k", n=4, c=2)
        AB = sb("AB", [P, 2, 384])
        AT = sb("AT", [P, 2, 384])
        eb = Ring([EB[:, i, :, :] for i in range(4)])
        ab = Ring([AB[:, i, :] for i in range(2)])
        at = Ring([AT[:, i, :] for i in range(2)])
        st = sb("st", [P, 4, 24])
        stR = Ring([st[:, i, :] for i in range(2)])
        TILES = [(0, 0, 128, 128), (1, 128, 384, 0)]

        def transposed3(src, waits, PT, PA):
            ps, rd, pi = PT.take()
            for n in range(3):
                done = tr(ps[:, n * P:(n + 1) * P], src[:, n * P:(n + 1) * P], P, rd if n == 0 else None, waits, count=n == 2)
            t_, rd, ti = PA.take()
            tk = actv(t_, ps[:, 0:384], ACT.Copy, done, rd)
            PT.give(pi, tk)
            return t_, tk, ti, done

        def diff_attention():
            ya_rdy = []
            for h in range(8):
                ev, erd, ei = eb.take()
                s_, srd, s_i = stR.take()
                mx = []
                for c in range(2):
                    ps, rd, pi = S.take()
                    q = QR[64 * c:64 * c + 64, h, :]
                    k = KR[64 * c:64 * c + 64, h, :]
                    mm(ps[:, 0:128], q[:, 0:128], k[:, 0:128], rd, qk_rdy[("q", h)], qk_rdy[("k", h)])
                    done = mm(ps[:, 128:384], q[:, 128:256], k[:, 0:256], count=True)
                    for i, a0, a1, m0 in TILES:
                        tk = dve(lambda e, ps=ps, a0=a0, a1=a1, m0=m0, c=c, i=i, ev=ev, s_=s_: e.tensor_tensor_reduce(
                            ev[:, c, a0:a1], ps[:, a0:a1], mblk[:, m0:256], 0.125, NEG, ALU.add, ALU.max,
                            s_[:, 2 * c + i:2 * c + i + 1]), done, erd, srd)
                    S.give(pi, tk)
                    mx.append(tk)
                nm = ts(dve, s_[:, 4:8], s_[:, 0:4], -1.0, None, ALU.mult, None, mx)
                yield
                for c in range(2):
                    for i, a0, a1, m0 in TILES:
                        n = 2 * c + i
                        ex = actv(ev[:, c, a0:a1], ev[:, c, a0:a1], ACT.Exp, nm, bias=s_[:, 4 + n:5 + n],
                                  accum_out=s_[:, 8 + n:9 + n])
                r = dve(lambda e, s_=s_: e.reciprocal(s_[:, 12:16], s_[:, 8:12]), ex)
                r = ts(dve, s_[:, 14:16], s_[:, 14:16], nlam, None, ALU.mult, None, r, lam_rdy)
                a_, ard, ai = ab.take()
                for i, a0, a1, m0 in TILES:
                    tk = ts(dve, a_[:, a0:a1], ev[:, 0, a0:a1], s_[:, 12 + i:13 + i], None, ALU.mult, None, r, ard)
                    tk = stt(a_[:, a0:a1], ev[:, 1, a0:a1], s_[:, 14 + i:15 + i], a_[:, a0:a1], ALU.mult, ALU.add, tk)
                eb.give(ei, tk)
                stR.give(s_i, tk)
                yield
                aT, tk, ti, trd = transposed3(a_, tk, X, at)
                ab.give(ai, trd)
                ps, rd, pi = S.take()
                mm(ps[:, 0:T], VA[:, 0, h * P:(h + 1) * P], aT[:, 0:T], rd, tk, va_rdy, start=True, stop=False)
                done = mm(ps[:, 128:T], VA[:, 1, h * P:(h + 1) * P], aT[:, 256:384], start=False, stop=True, count=True)
                at.give(ti, done)
                tk = actv(YA[:, h, :], ps[:, 0:T], ACT.Copy, done, free0)
                S.give(pi, tk)
                ya_rdy.append(tk)
                yield
            r8 = rows[0:8, 0, :]
            rk = rows_rsqrt([(YA[:, h, :], ya_rdy[h]) for h in range(8)], list(range(8)), 8, 1.0 / 128, EPS, 0.8, r8)
            yield
            for h in range(8):
                ps, rd, pi = X.take()
                done = mm(ps[:, 0:T], selr[:, h, :], r8, rd, rk, count=True)
                tk = stt(YA[:, h, :], YA[:, h, :], V("g_subln"), ps[:, 0:T], ALU.mult, ALU.mult, done)
                X.give(pi, tk)
                out_rdy["ya", h] = tk
                if h % 2:
                    yield

        rows = sb("rows", [16, 8, T])
        out_rdy = {}
        XM = arena[:, 4 * UNIT:5 * UNIT].rearrange("p (c t) -> p c t", t=260)
        XC, OP = B3(5), B3(6)
        hw = sb("hw", [P, 40 + 96])
        hw1 = ts(dve, hw[:, 0:40], vec[:, VO["conv_w"][0]:VO["conv_w"][0] + 40], 0.5, None, ALU.mult, None)
        hw2 = ts(dve, hw[:, 40:136], V("a_conv_w_2"), 0.5, None, ALU.mult, None)
        z1 = dve(lambda e: e.memset(XM[:, :, 0:3], 0.0), free0)
        xm_rdy, xc_rdy, op_rdy = [None] * 8, [None] * 8, [None] * 8

        def conv_silu(pad, pad_rdy, w, dst, bias, dwait):
            tb, rd, bi = TB.take()
            y = tb[:, 0:T]
            if bias is None:
                tk = ts(dve, y, pad[:, 0:T], w(0), None, ALU.mult, None, pad_rdy, rd)
            else:
                tk = ts(dve, y, pad[:, 0:T], w(0), bias, ALU.mult, ALU.add, pad_rdy, rd)
            for k in range(1, 4):
                tk = stt(y, pad[:, k:k + T], w(k), y, ALU.mult, ALU.add, tk)
            th = actv(tb[:, T:512], y, ACT.Tanh, tk)
            tk = stt(dst, tb[:, T:512], 1.0, y, ALU.add, ALU.mult, th, dwait)
            TB.give(bi, tk)
            return tk

        def xm_epi(pair, ps, done):
            tk = actv(XM[:, 2 * pair:2 * pair + 2, 3:259], ps.rearrange("p (c t) -> p c t", t=T), ACT.Copy, done, free0)
            for c in (2 * pair, 2 * pair + 1):
                xm_rdy[c] = tk
                xc_rdy[c] = conv_silu(XM[:, c, :], [tk, z1], lambda k, c=c: hw[:, 8 * k + c:8 * k + c + 1], XC[:, c, :],
                                      hw[:, 32 + c:33 + c], hw1)
            return tk

        def tanh_epi(dst, rdy):
            def epi(pair, ps, done):
                tk = actv(dst[:, 2 * pair:2 * pair + 2, :], ps.rearrange("p (c t) -> p c t", t=T), ACT.Tanh, done, scale=0.5)
                rdy[2 * pair] = rdy[2 * pair + 1] = tk
                return tk
            return epi

        together(diff_attention(), seq(side, linear(w_in, 3 * D, D, U, u_rdy, xm_epi),
                                       linear(w_in, 4 * D, D, U, u_rdy, tanh_epi(OP, op_rdy))))

        MQ, MK, MVT, HC = B3(0), B3(1), B3(2), B3(2)
        MV = B(7).rearrange("p (i n) -> p i n", i=2)
        GA, GB = B3(8), B3(9)
        ga_rdy, gb_rdy = [None] * 8, [None] * 8
        YB = HC
        wif = V("w_if").rearrange("p (t h c g) -> p t h c g", t=3, h=4, c=2)
        gcol = sb("gcol", [P, 2, 20])
        xmv = XM[:, :, 3:259]

        def mlstm():
            free = now()
            (wq, wk), arrived, si = load((0, a["w_mq"]), (2048, a["w_mk"]))
            (wv,), arrived2, si2 = load((0, a["w_mv"]))
            q_r, k_r, vt_r, v_r = {}, {}, {}, {}

            def turned(h):
                ps, rd, pi = L.take()
                for n in range(4):
                    e2, i = n // 2, n % 2
                    done = tr(ps[:, n * P:(n + 1) * P], MV[:, i, h * T + e2 * P:h * T + (e2 + 1) * P], P,
                              [rd, v_r[h]] if n == 0 else None, count=n == 3)
                tk = actv(MVT[:, 2 * h:2 * h + 2, :], ps.rearrange("p (c t) -> p c t", t=T), ACT.Copy, done, free)
                L.give(pi, tk)
                vt_r[h] = tk

            for h in range(4):
                for w, arr, src, rdy, dst, rr in ((wq, arrived, XC, xc_rdy, MQ, q_r), (wk, arrived, XC, xc_rdy, MK, k_r)):
                    ps, rd, pi = L.take()
                    for e2 in range(2):
                        done = group(ps[:, e2 * T:(e2 + 1) * T],
                                     [(w[:, 2 * h + k, e2 * P:(e2 + 1) * P], src[:, 2 * h + k, :]) for k in range(2)],
                                     [[arr, rdy[2 * h + k]] for k in range(2)], rd, count=e2 == 1)
                    tk = actv(dst[:, 2 * h:2 * h + 2, :], ps.rearrange("p (c t) -> p c t", t=T), ACT.Copy, done, free)
                    L.give(pi, tk)
                    rr[h] = tk
                ps, rd, pi = L.take()
                for i in range(2):
                    done = group(ps[:, i * T:(i + 1) * T],
                                 [(xmv[:, 2 * h + k, i * P:(i + 1) * P], wv[:, 2 * h + k, :]) for k in range(2)],
                                 [[arrived2, xm_rdy[2 * h + k]] for k in range(2)], rd, count=i == 1)
                tk = tt_copy(MV[:, :, h * T:(h + 1) * T], ps.rearrange("p (i n) -> p i n", i=2), done, free)
                L.give(pi, tk)
                pdone = done
                v_r[h] = tk
                if h:
                    turned(h - 1)
            turned(3)
            ring.give(si, pdone)
            ring.give(si2, pdone)
            R = rows
            ps, rd, pi = X.take()
            prs, rr = [], []
            for t3, (buf, r_) in enumerate(((MQ, q_r), (MK, k_r), (MVT, vt_r))):
                for h in range(4):
                    for c2 in range(2):
                        prs.append((wif[:, t3, h, c2, :], buf[:, 2 * h + c2, :]))
                        rr.append(r_[h])
            gates_done = group(ps[0:8, 0:T], prs, rr, rd, count=True)
            tk = tt_copy(R[0:8, 6, :], ps[0:8, 0:T], gates_done, free)
            X.give(pi, tk)
            ps, rd, pi = X.take()
            for i in range(2):
                done = tr(ps[:, 8 * i:8 * i + 8], R[0:8, 6, i * P:(i + 1) * P], 8, rd if i == 0 else None, tk, count=i == 1)
            tk = tt_copy(gcol[:, :, 0:8], ps[:, 0:16].rearrange("p (i g) -> p i g", i=2), done, free)
            X.give(pi, tk)
            ps, rd, pi = X.take()
            for i in range(2):
                tr(ps[0:4, i * P:(i + 1) * P], gcol[:, i, 0:4], P, rd if i == 0 else None, tk)
            for i in range(2):
                done = tr(ps[0:4, T + i * P:T + (i + 1) * P], gcol[:, i, 4:8], P, count=i == 1)
            ig = ts(dve, R[0:4, 1, :], ps[0:4, 0:T], V("b_i", 4), None, ALU.add, None, done, free)
            fg = ts(dve, R[0:4, 2, :], ps[0:4, T:512], V("b_f", 4), None, ALU.add, None)
            X.give(pi, fg)
            tk = actv(R[0:4, 3, :], R[0:4, 2, :], ACT.Abs, fg)
            tk = actv(R[0:4, 3, :], R[0:4, 3, :], ACT.Exp, tk, scale=-1.0)
            tk = actv(R[0:4, 3, :], R[0:4, 3, :], ACT.Ln, tk, bias=1.0)
            tk = stt(R[0:4, 2, :], R[0:4, 2, :], 0.0, R[0:4, 3, :], ALU.min, ALU.subtract, tk)
            tk = dve(lambda e: e.tensor_tensor_scan(R[0:4, 3, :], one_row[0:4, :], R[0:4, 2, :], 0.0, ALU.mult, ALU.add), tk, one_rdy)
            tk = tt(dve, R[0:4, 1, :], R[0:4, 1, :], R[0:4, 3, :], ALU.subtract, tk, ig)
            tk = dve(lambda e: e.tensor_tensor_scan(R[0:4, 2, :], R[0:4, 1, :], R[0:4, 1, :], 0.0, ALU.max, ALU.max), tk)
            tk2 = stt(R[0:4, 5, :], R[0:4, 3, :], -1.0, R[0:4, 2, :], ALU.mult, ALU.subtract, tk)
            tk2 = actv(R[0:4, 5, :], R[0:4, 5, :], ACT.Exp, tk2)
            tk3 = ts(dve, R[0:4, 4, :], R[0:4, 2, :], -1.0, None, ALU.mult, None, tk)
            ps, rd, pi = X.take()
            for i in range(2):
                done = tr(ps[:, 4 * i:4 * i + 4], R[0:4, 1, i * P:(i + 1) * P], 4, rd if i == 0 else None, tk, count=i == 1)
            gs = tt_copy(gcol[:, :, 8:12], ps[:, 0:8].rearrange("p (i g) -> p i g", i=2), done)
            X.give(pi, gs)
            yield
            hc_rdy = [None] * 8
            for h in range(4):
                ps, rd, pi = X.take()
                bc = mm(ps, selr[0:4, h, :], R[0:4, 4:6, :], rd, tk2, tk3, count=True)
                w_, wrd, wi = TA.take()
                xs = tt(dve, w_[:, 0:T], ps[:, 0:T], mtri[:, 0:T], ALU.add, bc, wrd)
                xs = tt(dve, w_[:, T:384], ps[:, 128:T], mtri[:, 256:384], ALU.add)
                em, emrd, emi = TB.take()
                emr = actv(em[:, 0:T], ps[:, T:512], ACT.Copy, bc, xs, emrd)
                X.give(pi, xs, emr)
                actv(w_[:, 0:T], w_[:, 0:T], ACT.Exp, xs, gs, bias=gcol[:, 0, 8 + h:9 + h])
                wr = actv(w_[:, T:384], w_[:, T:384], ACT.Exp, bias=gcol[:, 1, 8 + h:9 + h])
                sp_, rd, si_ = S.take()
                group(sp_[:, 0:T], [(MK[:, 2 * h + c, 0:P], MQ[:, 2 * h + c, :]) for c in range(2)], [[q_r[h], k_r[h]]] * 2, rd)
                done = group(sp_[:, T:384], [(MK[:, 2 * h + c, P:T], MQ[:, 2 * h + c, P:T]) for c in range(2)], None, None, count=True)
                sc_, srd, sci = ab.take()
                sc = stt(sc_, sp_[:, 0:384], 0.0625, w_[:, 0:384], ALU.mult, ALU.mult, wr, done, srd)
                TA.give(wi, sc)
                S.give(si_, sc)
                yield
                np_, rd, ni = S.take()
                for e2 in range(2):
                    o = h * T + e2 * P
                    mm(np_[:, e2 * T:(e2 + 1) * T], MV[:, 0, o:o + P], sc_[:, 0:T], rd if e2 == 0 else None, sc, v_r[h], stop=False)
                    num = mm(np_[:, e2 * T + P:(e2 + 1) * T], MV[:, 1, o:o + P], sc_[:, T:384], start=False, count=e2 == 1)
                dp, rd, di = X.take()
                mm(dp[:, 0:T], C("ones"), sc_[:, 0:T], rd, stop=False)
                den = mm(dp[:, P:T], C("ones"), sc_[:, T:384], start=False, count=True)
                ab.give(sci, den)
                dk = actv(em[:, T:512], dp[:, 0:T], ACT.Abs, den)
                X.give(di, dk)
                dk = tt(dve, em[:, 0:T], em[:, 0:T], em[:, T:512], ALU.max, dk, emr)
                dk = dve(lambda e, em=em: e.reciprocal(em[:, 0:T], em[:, 0:T]), dk)
                for e2 in range(2):
                    hk = tt(dve, HC[:, 2 * h + e2, :], np_[:, e2 * T:(e2 + 1) * T], em[:, 0:T], ALU.mult, dk, num, gates_done)
                    hc_rdy[2 * h + e2] = hk
                S.give(ni, hk)
                TB.give(emi, hk)
                yield
            r8 = rows[0:8, 0, :]
            rk = rows_rsqrt([(HC[:, c, :], hc_rdy[c]) for c in range(8)], [c // 2 for c in range(8)], 4, 1.0 / 256, EPS, 1.0, r8)
            hg = ts(dve, sm[:, 112:120], V("g_mlnorm"), 0.5, None, ALU.mult, None)
            hg = ts(dve, sm[:, 120:128], V("ml_skip"), 0.5, None, ALU.mult, None)
            yield
            for h in range(4):
                ps, rd, pi = X.take()
                done = mm(ps[:, 0:T], selr[:, h, :], r8, rd, rk, count=True)
                for e2 in range(2):
                    c = 2 * h + e2
                    tk = stt(HC[:, c, :], HC[:, c, :], sm[:, 112 + c:113 + c], ps[:, 0:T], ALU.mult, ALU.mult, done, hg)
                    tk2 = stt(HC[:, c, :], XC[:, c, :], sm[:, 120 + c:121 + c], HC[:, c, :], ALU.mult, ALU.add, tk, hg)
                    tk3 = stt(HC[:, c, :], OP[:, c, :], 1.0, HC[:, c, :], ALU.add, ALU.mult, tk2, op_rdy[c])
                    out_rdy["yb", c] = tk3
                X.give(pi, tk)
                yield

        def tt_copy(o, i, *waits):
            return dve(lambda e: e.tensor_copy(o, i), *waits)

        one_row = rows[0:8, 7, :]
        one_rdy = dve(lambda e: e.memset(one_row, 1.0))

        together(mlstm(), seq(linear(w_in, 5 * D, D, U, u_rdy, tanh_epi(GA, ga_rdy)),
                              linear(w_in, 6 * D, D, U, u_rdy, tanh_epi(GB, gb_rdy))))

        MG = B3(0)
        mg_rdy = [None] * 8
        freem = now()

        def epi_a(pair, ps, done):
            for j in range(2):
                c = 2 * pair + j
                tk = stt(MG[:, c, :], GA[:, c, :], 1.0, ps[:, j * T:(j + 1) * T], ALU.add, ALU.mult, done, ga_rdy[c], freem)
                mg_rdy[c] = tk
            return tk

        def epi_b(pair, ps, done):
            tb, rd, bi = TB.take()
            for j in range(2):
                c = 2 * pair + j
                tk = stt(tb[:, j * T:(j + 1) * T], GB[:, c, :], 1.0, ps[:, j * T:(j + 1) * T], ALU.add, ALU.mult, done, gb_rdy[c], rd)
            s = tt(pool, MG[:, 2 * pair:2 * pair + 2, :], MG[:, 2 * pair:2 * pair + 2, :], tb.rearrange("p (c t) -> p c t", t=T),
                   ALU.add, tk, mg_rdy[2 * pair + 1])
            TB.give(bi, s)
            mg_rdy[2 * pair] = mg_rdy[2 * pair + 1] = s
            return tk

        run(linear(a["w_proj_a"], 0, D, YA, [out_rdy["ya", c] for c in range(8)], epi_a))
        run(linear(a["w_proj_b"], 0, D, YB, [out_rdy["yb", c] for c in range(8)], epi_b))

        def residual(scale_cols, scale_rdy):
            def epi(pair, ps, done):
                for j in range(2):
                    c = 2 * pair + j
                    h_rdy[c] = stt(H[:, c, :], ps[:, j * T:(j + 1) * T], scale_cols[:, c:c + 1], H[:, c, :],
                                   ALU.mult, ALU.add, done, scale_rdy, h_rdy[c])
                return h_rdy[c]
            return epi

        g2 = ts(dve, sm[:, 128:136], mods[:, 40:48], 0.5, None, ALU.mult, None, mod_rdy[47])
        run(linear(a["w_out"], 0, D, MG, mg_rdy, residual(sm[:, 128:136], g2)))

        u_rdy = normed(V("g_ff2"), 56, 48, U, h_rdy, now(), 2)
        ada2 = ada_both()
        beside(ffn(a["w2_gate"], a["w2_up"], a["w2_down"], u_rdy, 64, h_rdy), ada2)
        run(ada2)

        n_rdy = normed(None, None, None, U, h_rdy, now(), 3)
        h_rdy = [ts(dve, H[:, c, :], U[:, c, :], V("g_final")[:, c:c + 1], None, ALU.mult, None, n_rdy[c]) for c in range(8)]

        u_rdy = normed(V("norm_g_2")[:, 0:8], 80, 72, U, h_rdy, now(), 4)
        free = now()
        wa = a["a_in_w_2"]
        R = rows
        gb_ = sb("gb_", [P, 2, 32])
        (wv,), arrived, si = load((0, wa[:, 4096:4112]))
        ps, rd, pi = L.take()
        done = group(ps[0:16, 0:T], [(wv[:, k, :], U[:, k, :]) for k in range(8)], [[arrived, u_rdy[k]] for k in range(8)], rd, count=True)
        ring.give(si, done)
        tk = dve(lambda e, ps=ps: e.tensor_copy(rows[0:16, 5, :], ps[0:16, 0:T]), done, free)
        L.give(pi, tk)
        ps, rd, pi = L.take()
        for i in range(2):
            done = tr(ps[:, 16 * i:16 * i + 16], rows[0:16, 5, i * P:(i + 1) * P], 16, rd if i == 0 else None, tk, count=i == 1)
        gtok = dve(lambda e, ps=ps: e.tensor_copy(gb_[:, :, 0:16], ps[:, 0:32].rearrange("p (i g) -> p i g", i=2)), done)
        L.give(pi, gtok)
        QG, KG, VG, ZG = B3(0), B3(1), B3(2), B3(3)
        cv_rdy = {}
        pads = B(9, 1040).rearrange("p (a b n) -> p a b n", a=2, b=2)
        padr = Ring([pads[:, i, :, :] for i in range(2)])
        z2 = dve(lambda e: e.memset(pads[:, :, :, 0:3], 0.0), free)

        def conv_epi(pair, ps, done):
            pd, rd, di = padr.take()
            cp = actv(pd[:, :, 3:259], ps.rearrange("p (c t) -> p c t", t=T), ACT.Copy, done, rd)
            for j in range(2):
                c = 2 * pair + j
                dst = (QG, KG, VG)[c // 8][:, c % 8, :]
                cv_rdy[c] = conv_silu(pd[:, j, :], [cp, z2], lambda k, c=c: hw[:, 40 + 24 * k + c:41 + 24 * k + c], dst,
                                      None, [free, hw2])
            padr.give(di, cv_rdy[c])
            return cp

        g_tok = {}

        def delta_gates():
            ps, rd, pi = X.take()
            for i in range(2):
                tr(ps[0:8, i * P:(i + 1) * P], gb_[:, i, 0:8], P, rd if i == 0 else None, gtok)
            for i in range(2):
                done = tr(ps[0:8, T + i * P:T + (i + 1) * P], gb_[:, i, 8:16], P, count=i == 1)
            bt0 = actv(R[0:8, 1, :], ps[0:8, 0:T], ACT.Tanh, done, free, scale=0.5)
            bt = ts(dve, R[0:8, 1, :], R[0:8, 1, :], 1.0, 0.5, ALU.add, ALU.mult, bt0)
            ak = ts(dve, R[0:8, 2, :], ps[0:8, T:512], V("a_dt_bias_2", 8), None, ALU.add, None, done, bt0)
            X.give(pi, ak)
            tk = actv(R[0:8, 3, :], R[0:8, 2, :], ACT.Abs, ak)
            tk = actv(R[0:8, 3, :], R[0:8, 3, :], ACT.Exp, tk, scale=-1.0)
            tk = actv(R[0:8, 3, :], R[0:8, 3, :], ACT.Ln, tk, bias=1.0)
            el = actv(sm[0:8, 136:137], V("a_A_log_2", 8), ACT.Exp)
            tk = stt(R[0:8, 2, :], R[0:8, 2, :], 0.0, R[0:8, 3, :], ALU.max, ALU.add, tk)
            tk = ts(dve, R[0:8, 2, :], R[0:8, 2, :], sm[0:8, 136:137], -1.0, ALU.mult, ALU.mult, tk, el)
            gc = dve(lambda e: e.tensor_tensor_scan(R[0:8, 3, :], one_row[0:8, :], R[0:8, 2, :], 0.0, ALU.mult, ALU.add), tk)
            ps, rd, pi = X.take()
            for i in range(2):
                tr(ps[:, 16 * i:16 * i + 8], R[0:8, 1, i * P:(i + 1) * P], 8, rd if i == 0 else None, bt, gc)
                done = tr(ps[:, 16 * i + 8:16 * i + 16], R[0:8, 3, i * P:(i + 1) * P], 8, count=i == 1)
            pv = ps[:, 0:32].rearrange("p (i g) -> p i g", i=2)
            tk = tt_copy(gb_[:, :, 16:24], pv[:, :, 0:8], done)
            tk = ts(dve, gb_[:, :, 24:32], pv[:, :, 8:16], -1.0, None, ALU.mult, None, done)
            X.give(pi, tk)
            g_tok["tok"] = tk
            g_tok["beta"], g_tok["gc"] = bt, gc
            yield

        MT = arena[:, 6 * UNIT:6 * UNIT + 3072].rearrange("p (h n) -> p h n", h=8)
        ATT = arena[:, 6 * UNIT + 3072:6 * UNIT + 6144].rearrange("p (h n) -> p h n", h=8)
        VB = B(4).rearrange("p (h i n) -> p h i n", h=8, i=2)
        DM = B(5).rearrange("p (u n) -> p u n", u=16)
        DT = B(9).rearrange("p (u n) -> p u n", u=16)
        P1 = B(2).rearrange("p (u n) -> p u n", u=16)
        UU = B(1).rearrange("p (h i n) -> p h i n", h=8, i=2)
        OG = B3(0)

        def delta():
            yield from delta_gates()
            r8q, r8k = rows[0:8, 0, :], rows[0:8, 4, :]
            rq = rows_rsqrt([(QG[:, h, :], cv_rdy[h]) for h in range(8)], list(range(8)), 8, 1.0, EPS, 128.0 ** -0.5, r8q)
            rk = rows_rsqrt([(KG[:, h, :], cv_rdy[8 + h]) for h in range(8)], list(range(8)), 8, 1.0, EPS, 1.0, r8k)
            yield
            for h in range(8):
                ps, rd, pi = X.take()
                mm(ps[:, 0:T], selr[:, h, :], r8q, rd, rq)
                done = mm(ps[:, T:512], selr[:, h, :], r8k, rk, count=True)
                qn = tt(dve, QG[:, h, :], QG[:, h, :], ps[:, 0:T], ALU.mult, done)
                kn = tt(dve, KG[:, h, :], KG[:, h, :], ps[:, T:512], ALU.mult, done)
                X.give(pi, kn)
                ps, rd, pi = X.take()
                mm(ps[:, 0:T], selr[:, h, :], R[0:8, 1, :], rd, g_tok["beta"])
                done = mm(ps[:, T:512], selr[:, h, :], R[0:8, 3, :], g_tok["gc"], count=True)
                kb, kbrd, kbi = TA.take()
                kbt = tt(dve, kb[:, 0:T], KG[:, h, :], ps[:, 0:T], ALU.mult, done, kn, kbrd)
                dc, dcrd, dci = TB.take()
                dk = tt(dve, dc[:, 0:T], ps[:, T:512], mtri[:, 0:T], ALU.add, dcrd)
                dk = tt(dve, dc[:, T:384], ps[:, T + P:512], mtri[:, 256:384], ALU.add)
                X.give(pi, dk)
                actv(dc[:, 0:T], dc[:, 0:T], ACT.Exp, dk, g_tok["tok"], bias=gb_[:, 0, 24 + h:25 + h])
                dk = actv(dc[:, T:384], dc[:, T:384], ACT.Exp, bias=gb_[:, 1, 24 + h:25 + h])
                ps, rd, pi = X.take()
                for i in range(2):
                    done = tr(ps[:, i * P:(i + 1) * P], VG[:, h, i * P:(i + 1) * P], P, rd if i == 0 else None,
                              cv_rdy[16 + h], count=i == 1)
                for i in range(2):
                    vb = actv(VB[:, h, i, :], ps[:, i * P:(i + 1) * P], ACT.Copy, done, g_tok["tok"], scale=gb_[:, i, 16 + h:17 + h])
                X.give(pi, vb)
                vb_rdy[h] = vb
                yield
                p1, rd, i1 = S.take()
                mm(p1[:, 0:T], KG[:, h, 0:P], kb[:, 0:T], rd, kbt)
                done = mm(p1[:, T:384], KG[:, h, P:T], kb[:, P:T], count=True)
                TA.give(kbi, done)
                p2, rd, i2 = S.take()
                mm(p2[:, 0:T], KG[:, h, 0:P], QG[:, h, :], rd, qn)
                done2 = mm(p2[:, T:384], KG[:, h, P:T], QG[:, h, P:T], count=True)
                mt = tt(dve, MT[:, h, :], p1[:, 0:384], dc[:, 0:384], ALU.mult, done, dk, free)
                S.give(i1, mt)
                att = tt(dve, ATT[:, h, :], p2[:, 0:384], dc[:, 0:384], ALU.mult, done2)
                S.give(i2, att)
                TB.give(dci, att)
                mt_rdy[h] = att
                yield

        vb_rdy, mt_rdy = {}, {}
        run(linear(wa, 0, 3 * D, U, u_rdy, conv_epi))
        zg_rdy = [None] * 8

        def silu_epi(dst, rdy, w):
            def epi(pair, ps, done):
                tb, rd, bi = TC.take()
                th = actv(tb, ps, ACT.Tanh, done, rd, scale=0.5)
                tk = stt(dst[:, 2 * pair:2 * pair + 2, :], tb.rearrange("p (c t) -> p c t", t=T), 1.0,
                         ps.rearrange("p (c t) -> p c t", t=T), ALU.add, ALU.mult, th, w)
                TC.give(bi, tk)
                rdy[2 * pair] = rdy[2 * pair + 1] = tk
                return tk
            return epi
        together(delta(), linear(wa, 3 * D, D, U, u_rdy, silu_epi(ZG, zg_rdy, free)))

        d_rdy = {}

        def inverse(g):
            def mt(u):
                h, i = u // 2, u % 2
                return MT[:, h, 256:384] if i else MT[:, h, 0:128]
            us = list(range(4 * g, 4 * g + 4))
            sl = slice(4 * g, 4 * g + 4)
            rdy = [mt_rdy[2 * g], mt_rdy[2 * g + 1]]
            idb = ident.unsqueeze(1).to_broadcast([P, 4, P])
            mtv = MT[:, 2 * g:2 * g + 2, :].rearrange("p h (k n) -> p h k n", k=3)[:, :, 0:3:2, :]
            X2 = XX[g]

            def four(ps):
                return ps.rearrange("p (u n) -> p u n", u=4)

            def mask(m):
                return m.unsqueeze(1).to_broadcast([P, 4, P])

            ps, rd, pi = X2.take()
            for j, u in enumerate(us):
                done = tr(ps[:, j * P:(j + 1) * P], mt(u), P, rd if j == 0 else None, rdy, count=j == 3)
            pk = tt(dve, P1[:, sl, :], four(ps), mask(lvlN[:, 0, :]), ALU.mult, done, freei)
            X2.give(pi, pk)
            dk = tt(pool, DM[:, sl, :], idb, P1[:, sl, :], ALU.subtract, pk, freei)
            yield
            ek = None
            for h in range(2):
                ek = tt(pool, DT[:, 4 * g + 2 * h:4 * g + 2 * h + 2, :], mtv[:, h, :, :],
                        lvl[:, 0, :].unsqueeze(1).to_broadcast([P, 2, P]), ALU.mult, rdy, freei)
            ek = tt(pool, DT[:, sl, :], idb, DT[:, sl, :], ALU.subtract, ek)
            for n in range(1, 7):
                ps, rd, pi = X2.take()
                for j, u in enumerate(us):
                    done = mm(ps[:, j * P:(j + 1) * P], mt(u), DM[:, u, :], rd if j == 0 else None, dk, count=j == 3)
                pk = tt(dve, P1[:, sl, :], four(ps), mask(lvlN[:, n, :]), ALU.mult, done)
                X2.give(pi, pk)
                yield
                ps, rd, pi = X2.take()
                for j, u in enumerate(us):
                    done = mm(ps[:, j * P:(j + 1) * P], DT[:, u, :], P1[:, u, :], rd if j == 0 else None, pk, ek, count=j == 3)
                dk = tt(dve, DM[:, sl, :], DM[:, sl, :], four(ps), ALU.subtract, done, dk)
                X2.give(pi, dk)
                yield
                ps, rd, pi = X2.take()
                for j, u in enumerate(us):
                    done = tr(ps[:, j * P:(j + 1) * P], DM[:, u, :], P, rd if j == 0 else None, dk, count=j == 3)
                ek = actv(DT[:, sl, :], four(ps), ACT.Copy, done)
                X2.give(pi, ek)
            d_rdy[g] = [dk, ek]

        lvls = B(1, 1792).rearrange("p (s n i) -> p s n i", s=2, n=7)
        lvl, lvlN = lvls[:, 0, :, :], lvls[:, 1, :, :]
        sp.dma(lambda e: e.dma_start(B(1, 1792), a["lvls"]), s_lvl, now())
        freei = [now(), (s_lvl, 16)]
        XX = [Ring([b[:, :] for b in banks[2 * g:2 * g + 2]]) for g in range(4)]
        for r in XX:
            r.readers = [freei] * 2
        together(*[inverse(g) for g in range(4)])
        after = now()
        for r in (L, S, X):
            r.readers = [after] * len(r.bufs)

        og_rdy = [None] * 8

        def delta_out(h0):
            for h in range(h0, 8, 2):
                u = 2 * h
                ps, rd, pi = X.take()
                done = mm(ps[:, 0:P], DT[:, u, :], VB[:, h, 0, :], rd, vb_rdy[h], after, count=True)
                uk = actv(UU[:, h, 0, :], ps[:, 0:P], ACT.Copy, done, after)
                X.give(pi, uk)
                yield
                ps, rd, pi = X.take()
                done = mm(ps[:, 0:P], MT[:, h, P:T], UU[:, h, 0, :], rd, uk, count=True)
                rk = tt(dve, VB[:, h, 1, :], VB[:, h, 1, :], ps[:, 0:P], ALU.subtract, done)
                X.give(pi, rk)
                yield
                ps, rd, pi = X.take()
                done = mm(ps[:, 0:P], DT[:, u + 1, :], VB[:, h, 1, :], rd, rk, count=True)
                uk = actv(UU[:, h, 1, :], ps[:, 0:P], ACT.Copy, done, after)
                X.give(pi, uk)
                yield
                ps, rd, pi = S.take()
                mm(ps[:, 0:T], UU[:, h, 0, :], ATT[:, h, 0:T], rd, uk, stop=False)
                done = mm(ps[:, P:T], UU[:, h, 1, :], ATT[:, h, T:384], start=False, count=True)
                ok = actv(OG[:, h, :], ps[:, 0:T], ACT.Copy, done, after)
                S.give(pi, ok)
                og_rdy[h] = ok
                yield
        together(delta_out(0), delta_out(1))
        r8 = rows[0:8, 0, :]
        rk = rows_rsqrt([(OG[:, h, :], og_rdy[h]) for h in range(8)], list(range(8)), 8, 1.0 / 128, EPS, 0.5, r8)
        y_rdy = []
        for h in range(8):
            ps, rd, pi = X.take()
            done = mm(ps[:, 0:T], selr[:, h, :], r8, rd, rk, count=True)
            tk = stt(OG[:, h, :], OG[:, h, :], V("a_onorm_g_2"), ps[:, 0:T], ALU.mult, ALU.mult, done)
            X.give(pi, tk)
            y_rdy.append(tt(pool, OG[:, h, :], OG[:, h, :], ZG[:, h, :], ALU.mult, tk, zg_rdy[h]))
        run(linear(a["a_out_w_2"], 0, D, OG, y_rdy, residual(mods[:, 88:96], mod_rdy[95])))

        n_rdy = normed(None, None, None, U, h_rdy, now(), 5)
        SK = B3(0)
        free = now()
        A2 = sm[:, 144:152]
        a2 = stt(A2, mods[:, 104:112], 1.0, V("norm_g_2")[:, 8:16], ALU.add, ALU.mult, mod_rdy[111])
        s_rdy, u_rdy = [], []
        for c in range(8):
            s_rdy.append(actv(SK[:, c, :], U[:, c, :], ACT.Copy, n_rdy[c], free, scale=V("kv_norm_g_2")[:, c:c + 1]))
            u_rdy.append(ts(dve, U[:, c, :], U[:, c, :], A2[:, c:c + 1], mods[:, 96 + c:97 + c], ALU.mult, ALU.add,
                            s_rdy[c], a2, mod_rdy[103]))

        BT = arena[:, 6 * UNIT:6 * UNIT + 4096].rearrange("p (h n) -> p h n", h=16)
        s_bt = sem("s_bt")
        skew = bass.AP(tensor=scratch.tensor, offset=127, ap=[[383, P], [P * 384, 16], [1, T]])
        sp.dma(lambda e: e.dma_start(BT, skew), s_bt, [(s, 16 * n) for s, n in zip(s_br, (8, 8))], free)
        bt_rdy = (s_bt, 16)

        KW = arena[:, 9 * UNIT:9 * UNIT + 1024].rearrange("p (b g t) -> p b g t", b=2, g=2)
        VW = arena[:, 9 * UNIT + 1024:9 * UNIT + 1536].rearrange("p (b i n) -> p b i n", b=2, i=2)
        BLK = arena[:, 8 * UNIT:8 * UNIT + 960].rearrange("p (s m g n) -> p s m g n", s=2, m=16, g=2)
        HK = arena[:, 8 * UNIT + 960:8 * UNIT + 1080].rearrange("p (s c n) -> p s c n", s=2, c=2)
        KC = arena[:, 8 * UNIT + 1080:8 * UNIT + 1110].rearrange("p (g n) -> p g n", g=2)
        VC = arena[0:15, 8 * UNIT + 1110:8 * UNIT + 1110 + 128]
        blk_rdy, kw_rdy, vw_rdy = [], [], []

        def kv_prep():
            (wv,), arrived, si = load((0, a["kv_w_2"][:, 0:512]))
            for j in range(4):
                if j == 3:
                    for i in range(2):
                        ps, done, pi = token_major(wv, 384, 128, SK, s_rdy, i, None, arrived=arrived)
                        tk = tt_copy(VW[:, 0, i, :], ps[:, 0:128], done, free)
                        L.give(pi, tk)
                        vw_rdy.append(tk)
                    yield
                    continue
                ps, rd, pi = L.take()
                done = group(ps[:, 0:T], [(wv[:, k, j * P:(j + 1) * P], SK[:, k, :]) for k in range(8)],
                             [[arrived, s_rdy[k]] for k in range(8)], rd, count=True)
                if j < 2:
                    pos = V(("cmp_pos_k_2", "cmp_pos_v_2")[j])
                    for g in range(2):
                        for par in range(2):
                            src = ps[64 * g:64 * g + 64, :]
                            src = bass.AP(tensor=src.tensor, offset=src.offset + par, ap=[list(src.ap[0]), [2, 16], [16, 15]])
                            tk = tt(dve, BLK[64 * par:64 * par + 64, j, :, g, :], src,
                                    pos[64 * par:64 * par + 64, :].unsqueeze(2).to_broadcast([64, 16, 15]), ALU.add, done, free)
                            blk_rdy.append(tk)
                    L.give(pi, tk)
                else:
                    yield from dup(ps, pi, done, 0)
                yield
            ring.give(si, done)
            (wv,), arrived, si = load((0, a["kv_w_2"][:, 512:768]))
            ps, rd, pi = L.take()
            done = group(ps[:, 0:T], [(wv[:, k, 0:P], SK[:, k, :]) for k in range(8)], [arrived] * 8, rd, count=True)
            yield from dup(ps, pi, done, 1)
            for i in range(2):
                ps, done, pi = token_major(wv, 128, 128, SK, s_rdy, i, None, arrived=arrived)
                tk = tt_copy(VW[:, 1, i, :], ps[:, 0:128], done, free)
                L.give(pi, tk)
                vw_rdy.append(tk)
            ring.give(si, done)
            yield
            for s in range(2):
                w1 = a[("cmp_k_w1_2", "cmp_v_w1_2")[s]]
                (wv,), arrived, si = load((0, w1))
                ps, rd, pi = L.take()
                done = group(ps[0:30, 0:T], [(BLK[:, s, m, :, :].rearrange("p g n -> p (g n)"), wv[:, m, :]) for m in range(16)],
                             [[arrived, blk_rdy]] * 16, rd, count=True)
                ring.give(si, done)
                tb, rd, bi = TC.take()
                th = actv(tb[0:30, 0:T], ps[0:30, 0:T], ACT.Tanh, done, rd, scale=0.5)
                tk = stt(tb[0:30, 0:T], tb[0:30, 0:T], 1.0, ps[0:30, 0:T], ALU.add, ALU.mult, th)
                L.give(pi, tk)
                yield
                ps, rd, pi = L.take()
                for c in range(2):
                    done = tr(ps[:, 30 * c:30 * c + 30], tb[0:30, c * P:(c + 1) * P], 30, rd if c == 0 else None, tk, count=c == 1)
                TC.give(bi, done)
                hk = ts(dve, HK[:, s, :, :], ps[:, 0:60].rearrange("p (c n) -> p c n", c=2), 0.5, None, ALU.mult, None, done)
                L.give(pi, hk)
                yield
                ps, rd, pi = X.take()
                if s == 0:
                    w2 = V("cmp_k_w2_2").rearrange("p (c n) -> p c n", c=2)
                    for half in range(2):
                        for c in range(2):
                            done = mm(ps[64 * half:64 * half + 64, 0:30], w2[:, c, :], HK[:, 0, c, :], rd if half + c == 0 else None, hk,
                                      start=c == 0, stop=c == 1, count=half + c == 2)
                    tk = tt_copy(KC, ps[:, 0:30].rearrange("p (g n) -> p g n", g=2), done)
                    cmp_rdy.append(tk)
                else:
                    w2 = V("cmp_v_w2_2").rearrange("p (c n) -> p c n", c=2)
                    for g in range(2):
                        for c in range(2):
                            done = mm(ps[0:15, 64 * g:64 * g + 64], HK[:, 1, c, 15 * g:15 * g + 15], w2[:, c, :], rd if g + c == 0 else None, hk,
                                      start=c == 0, stop=c == 1, count=g + c == 2)
                    tk = tt_copy(VC, ps[0:15, 0:128], done)
                    cmp_rdy.append(tk)
                X.give(pi, tk)
                yield

        cmp_rdy = []

        def dup(ps, pi, done, b):
            for g in range(2):
                for half in range(2):
                    tk = tt_copy(KW[64 * half:64 * half + 64, b, g, :], ps[64 * g:64 * g + 64, 0:T], done, free)
            kw_rdy.append(tk)
            L.give(pi, tk)
            yield

        QN, YN = B3(1), B3(5)
        ZS = [B3(2), B3(3), B3(4)]
        wb = a["b_in_w_2"]
        qn_rdy = [None] * 8
        zs_rdy = [[None] * 8 for _ in range(3)]

        def q_epi(pair, ps, done):
            tk = actv(QN[:, 2 * pair:2 * pair + 2, :], ps.rearrange("p (c t) -> p c t", t=T), ACT.Copy, done, free, scale=0.125)
            qn_rdy[2 * pair] = qn_rdy[2 * pair + 1] = tk
            return tk

        gates = sb("gates", [P, 2, 48])
        g3 = sb("g3", [P, 2, 16, 8])

        def zhalf(hf):
            for b in range(3):
                def epi(pair, ps, done, b=b):
                    return silu_epi(ZS[b], zs_rdy[b], free)(pair + 2 * hf, ps, done)
                yield from linear(wb, D * (1 + b) + 512 * hf, 512, U, u_rdy, epi)

        together(kv_prep(), seq(linear(wb, 0, D, U, u_rdy, q_epi), zhalf(0), zhalf(1)))
        (wv,), arrived, si = load((0, wb[:, 4096:4144]))
        ps, rd, pi = L.take()
        done = group(ps[0:48, 0:T], [(wv[:, k, :], U[:, k, :]) for k in range(8)], [[arrived, u_rdy[k]] for k in range(8)], rd, count=True)
        ring.give(si, done)
        tb, rd, bi = TC.take()
        tk = actv(tb[0:48, 0:T], ps[0:48, 0:T], ACT.Tanh, done, rd, scale=0.5)
        L.give(pi, tk)
        ps, rd, pi = L.take()
        for i in range(2):
            done = tr(ps[:, 48 * i:48 * i + 48], tb[0:48, i * P:(i + 1) * P], 48, rd if i == 0 else None, tk, count=i == 1)
        TC.give(bi, done)
        tk = tt_copy(gates[:, :, :], ps[:, 0:96].rearrange("p (i g) -> p i g", i=2), done)
        L.give(pi, tk)
        gt_rdy = ts(dve, gates[:, :, :], gates[:, :, :], 1.0, 0.25, ALU.add, ALU.mult, tk)

        CE = sb("CE", [P, 4, 24])
        CT = rows[:, 1:5, :]
        m15 = C("m15")
        y_rdy = [None] * 8

        def nsa(s, j):
            g = j // 4
            PS, PO, EE, EA, EC, ET, ES = streams[s]
            for b in (1, 2, 0):
                op_, ord_, oi = PO.take()
                for half in range(2):
                    h = 2 * j + half
                    lo = 64 * half
                    q = QN[lo:lo + 64, j, :]
                    gcl = [gates[:, i, 16 * b + h:16 * b + h + 1] for i in range(2)]
                    s_, srd, s_i = ES.take()
                    ps, rd, pi = PS.take()
                    if b:
                        k = KW[lo:lo + 64, b - 1, g, :]
                        mm(ps[:, 0:128], q[:, 0:128], k[:, 0:128], rd, qn_rdy[j], kw_rdy)
                        done = mm(ps[:, 128:384], q[:, 128:256], k[:, 0:256], count=True)
                        ev, erd, ei = EE.take()
                        E = ev
                        tiles = [(0, 0, 128, BT[:, h, 128:256]), (1, 128, 384, BT[:, h, :])]
                    else:
                        k = KC[lo:lo + 64, g, :]
                        mm(ps[:, 0:7], q[:, 0:128], k[:, 0:7], rd, qn_rdy[j], cmp_rdy)
                        done = mm(ps[:, 7:22], q[:, 128:256], k[:, 0:15], count=True)
                        ev, erd, ei = EC.take()
                        E = ev
                        tiles = [(0, 0, 7, BT[:, h, 159:256:16]), (1, 7, 22, BT[:, h, 31:256:16])]
                    for i, a0, a1, bias in tiles:
                        mk = dve(lambda e, E=E, a0=a0, a1=a1, ps=ps, bias=bias, s_=s_, i=i: e.tensor_tensor_reduce(
                            E[:, a0:a1], ps[:, a0:a1], bias, 1.0, -3e38, ALU.add, ALU.max, s_[:, i:i + 1]), done, erd, srd, bt_rdy)
                    PS.give(pi, mk)
                    nm = ts(dve, s_[:, 2:4], s_[:, 0:2], -1.0, None, ALU.mult, None, mk)
                    yield
                    for i, a0, a1, bias in tiles:
                        kw = {"accum_out": s_[:, 4 + i:5 + i]} if b else {}
                        ex = actv(E[:, a0:a1], E[:, a0:a1], ACT.Exp, nm, bias=s_[:, 2 + i:3 + i], **kw)
                    if b == 0:
                        for i, a0, a1, bias in tiles:
                            ex = dve(lambda e, E=E, a0=a0, a1=a1, s_=s_, i=i: e.tensor_tensor_reduce(
                                E[:, a0:a1], E[:, a0:a1], m15[:, a0:a1], 1.0, 0.0, ALU.mult, ALU.add, s_[:, 4 + i:5 + i]), ex)
                        ex = ts(dve, s_[:, 4:6], s_[:, 4:6], 1e-30, None, ALU.max, None, ex)
                    rk = dve(lambda e, s_=s_: e.reciprocal(s_[:, 6:8], s_[:, 4:6]), ex)
                    for i, a0, a1, bias in tiles:
                        pk = ts(dve, E[:, a0:a1], E[:, a0:a1], s_[:, 6 + i:7 + i], gcl[i], ALU.mult, ALU.mult, rk, gt_rdy)
                    ES.give(s_i, pk)
                    yield
                    if b:
                        aT, tk, ti, trd = transposed3(E, pk, PS, EA)
                        EE.give(ei, trd)
                        o_ = op_[lo:lo + 64, 0:T]
                        mm(o_, VW[:, b - 1, 0, 64 * g:64 * g + 64], aT[:, 0:T], ord_ if half == 0 else None, tk, vw_rdy, stop=False)
                        od = mm(op_[lo:lo + 64, P:T], VW[:, b - 1, 1, 64 * g:64 * g + 64], aT[:, T:384], start=False, count=True)
                        EA.give(ti, od)
                    else:
                        tp, rd, ti = PS.take()
                        tr(tp[0:7, 0:128], E[:, 0:7], P, rd, pk)
                        done = tr(tp[0:15, 128:256], E[:, 7:22], P, count=True)
                        EC.give(ei, done)
                        ct, crd, ci = ET.take()
                        c1 = actv(ct[0:7, 0:128], tp[0:7, 0:128], ACT.Copy, done, crd)
                        c1 = actv(ct[0:15, 128:256], tp[0:15, 128:256], ACT.Copy)
                        PS.give(ti, c1)
                        mm(op_[lo:lo + 64, 0:128], VC[0:7, 64 * g:64 * g + 64], ct[0:7, 0:128], ord_ if half == 0 else None, c1, cmp_rdy)
                        od = mm(op_[lo:lo + 64, 128:256], VC[0:15, 64 * g:64 * g + 64], ct[0:15, 128:256], count=True)
                        ET.give(ci, od)
                    yield
                zr = zs_rdy[b][j]
                if b == 1:
                    yk = tt(dve, YN[:, j, :], op_[:, 0:T], ZS[b][:, j, :], ALU.mult, od, zr, free)
                    PO.give(oi, yk)
                else:
                    tb, rd, bi = TB.take()
                    tk = tt(dve, tb[:, 0:T], op_[:, 0:T], ZS[b][:, j, :], ALU.mult, od, zr, rd)
                    PO.give(oi, tk)
                    yk = tt(pool, YN[:, j, :], YN[:, j, :], tb[:, 0:T], ALU.add, tk, yk)
                    TB.give(bi, yk)
            y_rdy[j] = yk

        U2 = U[:, :, :].rearrange("p c t -> p (c t)")
        after = now()
        streams = []
        for s in range(4):
            r = [Ring([banks[2 * s][:, :]]), Ring([banks[2 * s + 1][:, :]]), Ring([B(0)[:, s * 384:(s + 1) * 384]]),
                 Ring([U2[:, s * 384:(s + 1) * 384]]), Ring([CE[:, s, :]]), Ring([CT[:, s, :]]), Ring([st[:, s, :]])]
            for x in r:
                x.readers = [after]
            streams.append(r)
        together(*[seq(nsa(s, s), nsa(s, s + 4)) for s in range(4)])
        after = now()
        for r in (L, S, X):
            r.readers = [after] * len(r.bufs)
        run(linear(a["b_out_w_2"], 0, D, YN, y_rdy, residual(mods[:, 112:120], mod_rdy[119])))

        n_rdy = normed(None, None, None, U, h_rdy, now(), 6)
        s_out = sem("s_out")
        for c in range(8):
            tk = ts(dve, U[:, c, :], U[:, c, :], V("final_g_2")[:, c:c + 1], None, ALU.mult, None, n_rdy[c])
            sp.dma(lambda e, c=c: e.dma_start(out[c * P:(c + 1) * P, :], U[:, c, :]), s_out, tk)
        sp.items.append(([(s_out, 128)] + [(s, 128) for s in s_br], None, None))

        block = ctx.enter_context(nc.Block())
        block.sync(lambda e: sp.emit(e))
        block.tensor(lambda e: pe.emit(e))
        block.vector(lambda e: dve.emit(e))
        block.scalar(lambda e: act.emit(e))
        block.gpsimd(lambda e: pool.emit(e))


def kernel(**inputs):
    import concourse.bacc as _bacc
    from concourse.bass_utils import run_bass_kernel_spmd as _run

    nc = _bacc.Bacc("TRN2", target_bir_lowering=False, num_devices=1)
    x = {k: np.asarray(v) for k, v in inputs.items()}
    cst, lvls, oh, rope = constants()
    vec, lam = vectors(x)
    arrays = {"vec": vec, "lam": lam, "cst": cst, "lvls": lvls, "oh": oh, "rope": rope, "xT": np.ascontiguousarray(x["x"][0].T),
              "ada_w1": x["ada_w_2"][0], "ada_w2": x["ada_w_2"][1]}
    for n in ("w_ada", "w1_gate", "w1_up", "w1_down", "w_in", "w_proj_a", "w_proj_b", "w_out", "w2_gate", "w2_up",
              "w2_down", "a_in_w_2", "a_out_w_2", "b_in_w_2", "b_out_w_2"):
        arrays[n] = x[n][0]
    for n in ("w_mq", "w_mk", "w_mv"):
        arrays[n] = x[n][0].reshape(1024, 256)
    for n in ("kv_w_2", "cmp_k_w1_2", "cmp_v_w1_2"):
        arrays[n] = x[n]
    feed, aps = {}, {}
    for n, v in arrays.items():
        v = np.ascontiguousarray(v)
        feed[f"in_{n}"] = v
        aps[n] = nc.dram_tensor(f"in_{n}", v.shape, F32, kind="ExternalInput").ap()
    out = nc.dram_tensor("out_T", (D, T), F32, kind="ExternalOutput").ap()
    scratch = nc.dram_tensor("bias_rows", (16, P, 384), F32, kind="Internal").ap()
    build(nc, aps, out, scratch)
    r = _run(nc, [feed], core_ids=[0])
    return np.ascontiguousarray(r.results[0]["out_T"].T)[None]
```

```python
import itertools
from contextlib import ExitStack

import numpy as np

import concourse.bass as bass
from concourse import mybir

P = 128
T = 256
D = 1024
DFF = 2816
F32 = mybir.dt.float32
ALU = mybir.AluOpType
ACT = mybir.ActivationFunctionType
AX = mybir.AxisListType
NEG = -1e30
EPS = 1e-6
UNIT = 2080
SLOT = 4096
NSLOT = 4

VEC = [("c", 8), ("b_ada", 72), ("g_ff1", 8), ("g_mix", 8), ("g_subln", 1), ("conv_w", 32), ("conv_b", 8),
       ("ml_skip", 8), ("g_mlnorm", 8), ("g_ff2", 8), ("g_final", 8), ("c_2", 8), ("ada_b_2", 48),
       ("norm_g_2", 16), ("a_conv_w_2", 96), ("a_onorm_g_2", 1), ("kv_norm_g_2", 8), ("final_g_2", 8),
       ("cmp_pos_k_2", 16), ("cmp_pos_v_2", 16), ("w_if", 192), ("cmp_k_w2_2", 128), ("cmp_v_w2_2", 128),
       ("b_i", 1), ("b_f", 1), ("a_dt_bias_2", 1), ("a_A_log_2", 1), ("rel_bias_2", 16)]
CST = [("ident", 128), ("ones", 128), ("mblk", 256),
       ("mtri", 384), ("selc", 64), ("selr", 8 * 128), ("m15", 22)]


def offsets(table):
    out, at = {}, 0
    for name, n in table:
        out[name] = (at, n)
        at += n
    return out, at


VO, VN = offsets(VEC)
CO, CN = offsets(CST)


def constants():
    c = np.zeros((P, CN), np.float32)

    def put(name, a):
        o, n = CO[name]
        a = np.asarray(a, np.float32).reshape(a.shape[0], -1)
        assert a.shape[1] == n, (name, a.shape)
        c[:a.shape[0], o:o + n] = a

    i = np.arange(P)
    put("ident", np.eye(P))
    put("ones", np.ones((P, P)))
    rot = np.zeros((P, P))
    for p in range(P):
        d = p % 64
        if d < 32:
            rot[p + 32, p] = -1.0
        else:
            rot[p - 32, p] = 1.0
    inv = np.float32(10000.0) ** (-np.arange(0, 64, 2, dtype=np.float32) / np.float32(64))
    ang = np.arange(T, dtype=np.float32)[:, None] * inv.astype(np.float32)[None, :]
    rope = np.concatenate([rot, np.cos(ang).T[i % 32], np.sin(ang).T[i % 32]], 1).astype(np.float32)
    mblk = np.zeros((P, 256))
    mblk[0:64, 192:256] = NEG
    put("mblk", mblk)
    tri = np.where(i[None, :] >= i[:, None], 0.0, NEG)
    put("mtri", np.concatenate([tri, np.zeros((P, P)), tri], 1))
    lv = np.zeros((P, 7, P))
    for n in range(7):
        b = 1 << n
        bi, bj = i[None, :] // b, i[:, None] // b
        lv[:, n, :] = (bj % 2 == 0) & (bi == bj + 1)
    sc = np.zeros((P, 8, 8))
    sr = np.zeros((8, 8, P))
    for h in range(8):
        sc[:, h, h] = 1.0
        sr[h, h, :] = 1.0
    put("selc", sc)
    put("selr", sr)
    delta = 255 - np.arange(384)
    n = np.maximum(delta, 0)
    nf = np.maximum(n, 1).astype(np.float32)
    large = 16 + (np.log(nf / np.float32(16)) / np.float32(np.log(128 / 16)) * np.float32(16)).astype(np.int32)
    bucket = np.where(n < 16, n, np.minimum(large, 31))
    oh = np.zeros((33, 384))
    for j in range(384):
        if delta[j] >= 0:
            oh[bucket[j], j] = 1.0
        else:
            oh[32, j] = NEG
    m = np.zeros((P, 22))
    for q in range(7):
        m[:, q] = i - 16 * q - 31 >= 0
    for q in range(15):
        m[:, 7 + q] = i + 128 - 16 * q - 31 >= 0
    put("m15", m)
    lvls = np.concatenate([lv[:, 0:1], lv.transpose(2, 1, 0)], 1).reshape(P, -1).astype(np.float32)
    return c, lvls, oh.astype(np.float32), rope


def vectors(x):
    v = np.zeros((P, VN), np.float32)

    def put(name, a):
        o, n = VO[name]
        a = a.reshape(a.shape[0], -1)
        assert a.shape[1] == n, (name, a.shape)
        v[:a.shape[0], o:o + n] = a

    def cols(a):
        return np.asarray(a).reshape(-1, P).T

    for name in ("c", "b_ada", "g_ff1", "g_mix", "g_subln", "conv_w", "conv_b", "ml_skip", "g_mlnorm", "g_ff2",
                 "g_final", "c_2", "ada_b_2", "norm_g_2", "a_conv_w_2", "a_onorm_g_2", "kv_norm_g_2", "final_g_2",
                 "cmp_pos_k_2", "cmp_pos_v_2"):
        put(name, cols(x[name]))
    for name in ("w_if", "cmp_k_w2_2", "cmp_v_w2_2"):
        a = np.asarray(x[name])
        put(name, a.reshape(-1, P, a.shape[-1]).transpose(1, 0, 2))
    b = np.asarray(x["b_if"]).reshape(8, 1)
    put("b_i", b[0:4])
    put("b_f", b[4:8])
    put("a_dt_bias_2", np.asarray(x["a_dt_bias_2"]).reshape(8, 1))
    put("a_A_log_2", np.asarray(x["a_A_log_2"]).reshape(8, 1))
    lam = np.concatenate([np.asarray(x[k]).reshape(1, 64) for k in ("lambda_q1", "lambda_q2", "lambda_k1", "lambda_k2")], 1)
    put("rel_bias_2", np.concatenate([np.asarray(x["rel_bias_2"]), np.ones((1, 16), np.float32)], 0))
    return v, lam


class Queue:

    def __init__(self, sem):
        self.sem, self.n, self.items = sem, 0, []

    def __call__(self, fn, *waits, count=True):
        if count:
            self.n += 1
        self.items.append((flat(waits), fn, (self.sem, 1) if count else None))
        return (self.sem, self.n)

    def dma(self, fn, sem, *waits):
        self.items.append((flat(waits), fn, (sem, 16)))

    def emit(self, eng):
        seen = {}
        for waits, fn, inc in self.items:
            need = {}
            for s, v in waits:
                if v > max(seen.get(id(s), 0), need.get(id(s), (s, 0))[1]):
                    need[id(s)] = (s, v)
            for k, (s, v) in need.items():
                eng.wait_ge(s, v)
                seen[k] = v
            ins = fn(eng) if fn is not None else None
            if inc is not None:
                ins.then_inc(*inc)


def flat(x):
    if x is None:
        return []
    if isinstance(x, list) or (isinstance(x, tuple) and not (len(x) == 2 and isinstance(x[1], int))):
        return [y for e in x for y in flat(e)]
    return [x]


class Ring:

    def __init__(self, bufs):
        self.bufs, self.i, self.readers = bufs, -1, [[] for _ in bufs]

    def take(self):
        self.i = (self.i + 1) % len(self.bufs)
        assert self.readers[self.i] is not None, "still in use"
        r, self.readers[self.i] = self.readers[self.i], None
        return self.bufs[self.i], r, self.i

    def give(self, i, *toks):
        self.readers[i] = flat(toks)


def together(*gens):
    gens = list(gens)
    while gens:
        for g in list(gens):
            try:
                next(g)
            except StopIteration:
                gens.remove(g)


def rounds(*gens):
    gens = list(gens)
    while gens:
        for g in list(gens):
            if next(g, gens) is gens:
                gens.remove(g)
        yield


def seq(*gens):
    for g in gens:
        yield from g


def beside(main, side, every=1):
    n = 0
    for _ in main:
        n += 1
        if n % every == 0:
            next(side, None)


def run(gen):
    for _ in gen:
        pass


def build(nc, a, out, scratch):
    ctx = ExitStack()
    with ctx:
        def sb(name, shape):
            return ctx.enter_context(nc.sbuf_tensor(name, shape, F32))

        def sem(name):
            return ctx.enter_context(nc.semaphore(name))

        pe, dve, act, pool, sp = (Queue(sem("s_" + n)) for n in ("pe", "dve", "act", "pool", "sp"))

        vec = sb("vec", [P, VN])
        cst = sb("cst", [P, CN])
        H = sb("H", [P, 8, T])
        U = sb("U", [P, 8, T])
        arena = sb("arena", [P, 10 * UNIT])
        slots = sb("slots", [P, NSLOT, SLOT])
        mods = sb("mods", [P, 72 + 48])
        sm = sb("sm", [P, 192])
        rstd = sb("rstd", [P, T])
        tmpA = sb("tmpA", [P, 3, 512])
        tmpB = sb("tmpB", [P, 3, 512])
        tmpC = sb("tmpC", [P, 2, 512])
        banks = [ctx.enter_context(nc.psum_tensor(f"ps{i}", [P, 512], F32)) for i in range(8)]
        L = Ring([b[:, :] for b in banks[0:3]])
        S = Ring([b[:, :] for b in banks[3:5]])
        X = Ring([b[:, :] for b in banks[5:8]])
        TA = Ring([tmpA[:, i, :] for i in range(3)])
        TB = Ring([tmpB[:, i, :] for i in range(3)])
        TC = Ring([tmpC[:, i, :] for i in range(2)])

        def V(name, r=P):
            o, n = VO[name]
            return vec[0:r, o:o + n]

        def C(name, r=P):
            o, n = CO[name]
            return cst[0:r, o:o + n]

        def B(i, n=2048):
            return arena[:, i * UNIT:i * UNIT + n]

        def B3(i):
            return B(i).rearrange("p (c t) -> p c t", t=T)

        def now():
            return [(q.sem, q.n) for q in (pe, dve, act, pool)]

        ident = C("ident")
        selc = C("selc").rearrange("p (h m) -> p h m", h=8)
        selr = C("selr", 8).rearrange("p (h m) -> p h m", h=8)
        mtri = C("mtri")
        mblk = C("mblk")

        s_vec, s_cst = sem("s_vec"), sem("s_cst")
        s_x = sem("s_x")
        sp.dma(lambda e: e.dma_start(vec[:, :], a["vec"]), s_vec)
        act.dma(lambda e: e.dma_start(cst[:, :], a["cst"]), s_cst)
        s_oh, s_lvl, s_rope, s_lam = sem("s_oh"), sem("s_lvl"), sem("s_rope"), sem("s_lam")
        rope = arena[:, 9 * UNIT + 384:9 * UNIT + 1024]
        lamv = arena[0:1, 9 * UNIT + 1024:9 * UNIT + 1280]
        act.dma(lambda e: e.dma_start(rope, a["rope"]), s_rope)
        act.dma(lambda e: e.dma_start(lamv, a["lam"]), s_lam)
        oneh = arena[0:33, 9 * UNIT:9 * UNIT + 384]
        act.dma(lambda e: e.dma_start(oneh, a["oh"]), s_oh)
        vec_in, cst_in = (s_vec, 16), (s_cst, 16)
        act.dma(lambda e: e.dma_start(H[:, :, :], a["xT"].rearrange("(c p) t -> p c t", p=P)), s_x)
        x_in = (s_x, 16)

        s_slot = [sem(f"s_slot{i}") for i in range(NSLOT)]
        slot_n = [0] * NSLOT
        ring = Ring([slots[:, i, :] for i in range(NSLOT)])

        def load(*parts):
            buf, readers, i = ring.take()
            views = []
            for off, src in parts:
                kc, n = src.shape[0] // P, src.shape[1]
                v = buf[:, off:off + kc * n].rearrange("p (k n) -> p k n", n=n)
                s = src.rearrange("(k p) n -> p k n", p=P)
                sp.dma(lambda e, v=v, s=s: e.dma_start(v, s), s_slot[i], readers)
                slot_n[i] += 16
                views.append(v)
            return views, (s_slot[i], slot_n[i]), i

        def mm(out_, lhsT, rhs, *waits, start=True, stop=True, count=False):
            return pe(lambda e: e.matmul(out_, lhsT, rhs, start=start, stop=stop), *waits, count=count)

        def tr(out_, in_, n, *waits, count=False):
            return pe(lambda e: e.transpose(out_, in_, ident[0:n, 0:n]), *waits, count=count)

        def actv(out_, in_, f, *waits, **kw):
            return act(lambda e: e.activation(out_, in_, f, **kw), *waits)

        def tt(q, out_, i0, i1, op, *waits):
            return q(lambda e: e.tensor_tensor(out_, i0, i1, op), *waits)

        def ts(q, out_, i0, s1, s2, op0, op1, *waits):
            if op1 is None:
                return q(lambda e: e.tensor_scalar(out_, i0, s1, None, op0), *waits)
            return q(lambda e: e.tensor_scalar(out_, i0, s1, s2, op0, op1), *waits)

        def stt(out_, i0, s, i1, op0, op1, *waits):
            return dve(lambda e: e.scalar_tensor_tensor(out=out_, in0=i0, scalar=s, in1=i1, op0=op0, op1=op1), *waits)

        def group(out_, pairs, rdy, waits, count=False):
            tok = None
            for n, (l, r) in enumerate(pairs):
                tok = mm(out_, l, r, rdy[n] if rdy else None, waits if n == 0 else None,
                         start=n == 0, stop=n == len(pairs) - 1, count=count and n == len(pairs) - 1)
            return tok

        cs = sm[:, 0:16]
        t_c = actv(sm[:, 16:24], V("c"), ACT.Tanh, vec_in, scale=0.5)
        t_c = actv(sm[:, 24:32], V("c_2"), ACT.Tanh, scale=0.5)
        t = stt(cs[:, 0:8], sm[:, 16:24], 1.0, V("c"), ALU.add, ALU.mult, t_c)
        t = stt(cs[:, 8:16], sm[:, 24:32], 1.0, V("c_2"), ALU.add, ALU.mult, t_c)
        cs_rdy = ts(dve, cs, cs, 0.5, None, ALU.mult, None, t)
        mod_rdy = {}

        def ada(w, first, blocks, vec0, bias, share=0):
            for b0 in range(blocks[0], blocks[1], 4):
                (wv,), arrived, si = load((0, w[:, b0 * P:(b0 + 4) * P]))
                acc, rd, ai = TA.take()
                if share:
                    pr, prd, pri = X.take()
                    part = group(pr[0:1, :], [(cs[:, vec0 + k:vec0 + k + 1], wv[:, k, :]) for k in range(share)],
                                 None, [prd, arrived, cs_rdy], count=True)
                tok = ts(dve, acc, wv[:, share, :], cs[:, vec0 + share:vec0 + share + 1], None, ALU.mult, None, rd, arrived, cs_rdy)
                for k in range(share + 1, 8):
                    tok = stt(acc, wv[:, k, :], cs[:, vec0 + k:vec0 + k + 1], acc, ALU.mult, ALU.add, tok)
                if share:
                    tok = tt(dve, acc[0:1, :], acc[0:1, :], pr[0:1, :], ALU.add, tok, part)
                    X.give(pri, tok)
                ring.give(si, tok)
                yield
                ps, rd, pi = L.take()
                for j in range(4):
                    done = tr(ps[:, j * P:(j + 1) * P], acc[:, j * P:(j + 1) * P], P, rd if j == 0 else None, tok, cst_in,
                              count=j == 3)
                TA.give(ai, done)
                c0 = first + b0
                mc = mods[:, c0:c0 + 4]
                tok = dve(lambda e, mc=mc, ps=ps: e.tensor_reduce(mc, ps.rearrange("p (j n) -> p j n", j=4), AX.X, ALU.add), done)
                L.give(pi, tok)
                tok = tt(dve, mc, mc, bias[:, b0:b0 + 4], ALU.add, tok, vec_in)
                for j in range(4):
                    mod_rdy[c0 + j] = tok

        def ada_both():
            yield from ada(a["ada_w1"], 72, (0, 24), 8, V("ada_b_2")[:, 0:24])
            yield from ada(a["ada_w2"], 96, (0, 24), 8, V("ada_b_2")[:, 24:48])

        def root(src_rdy):
            actv(sm[:, 30:31], eps, ACT.Sqrt, eps_rdy)
            for c2 in range(4):
                tb, rd, bi = TA.take()
                sq = actv(tb[:, :].rearrange("p (c t) -> p c t", t=T), H[:, 2 * c2:2 * c2 + 2, :], ACT.Square, rd,
                          src_rdy[2 * c2:2 * c2 + 2])
                if c2 == 0:
                    ps, rd, pi = X.take()
                for j in range(2):
                    last = mm(ps[:, 0:T], C("ones"), tb[:, j * T:(j + 1) * T], rd if c2 + j == 0 else None, sq, cst_in,
                              start=c2 + j == 0, stop=c2 == 3 and j == 1, count=j == 1)
                TA.give(bi, last)
            sq = actv(rstd[:, :], ps[:, 0:T], ACT.Sqrt, last, eps_rdy, now(), bias=eps, scale=1.0 / D)
            X.give(pi, sq)
            return dve(lambda e: e.reciprocal(rstd[:, :], rstd[:, :]), sq)

        def normed(gcol, sc0, sh0, dst, src_rdy, dst_free, tag):
            A = sm[:, 32 + 8 * tag:40 + 8 * tag]
            if sc0 is not None:
                a_rdy = stt(A, mods[:, sc0:sc0 + 8], 1.0, gcol, ALU.add, ALU.mult, mod_rdy[sc0 + 7], now())
            r = root(src_rdy)
            toks = []
            for c in range(8):
                tk = tt(dve, dst[:, c, :], H[:, c, :], rstd[:, :], ALU.mult, r, dst_free if c == 0 else None)
                if sc0 is not None:
                    tk = actv(dst[:, c, :], dst[:, c, :], ACT.Identity, tk, a_rdy, mod_rdy[sh0 + 7],
                              scale=A[:, c:c + 1], bias=mods[:, sh0 + c:sh0 + c + 1])
                toks.append(tk)
            return toks

        eps = sm[:, 31:32]
        eps_rdy = dve(lambda e: e.memset(eps, EPS), t)

        def linear(w, c0, cols, rhs, rdy, epi, width=512):
            kc = w.shape[0] // P
            for b in range(0, cols, width):
                if kc * width <= SLOT:
                    (wv,), arrived, si = load((0, w[:, c0 + b:c0 + b + width]))
                    pieces = [(wv, arrived, si, 0, kc)]
                else:
                    hk = kc // 2
                    pieces = []
                    for n in range(2):
                        (wv,), arrived, si = load((0, w[n * hk * P:(n + 1) * hk * P, c0 + b:c0 + b + width]))
                        pieces.append((wv, arrived, si, n * hk, hk))
                for j2 in range(width // 256):
                    ps, rd, pi = L.take()
                    for j in range(2):
                        o = j2 * 256 + j * 128
                        prs, rr = [], []
                        for wv, arrived, si, k0, n in pieces:
                            for k in range(n):
                                prs.append((wv[:, k, o:o + P], rhs[:, k0 + k, :]))
                                rr.append([arrived, rdy[k0 + k]])
                        done = group(ps[:, j * T:(j + 1) * T], prs, rr, rd, count=j == 1)
                    if j2 == width // 256 - 1:
                        for p in pieces:
                            ring.give(p[2], done)
                    L.give(pi, epi((b + j2 * 256) // 256, ps, done))
                    yield

        def ffn(wg, wu, wd, u_rdy, gate0, h_rdy):
            free = now()
            actT = arena[:, 0:22 * T].rearrange("p (c t) -> p c t", t=T)
            rdy = []
            for b in range(11):
                (g_, u_), arrived, si = load((0, wg[:, b * 256:(b + 1) * 256]), (2048, wu[:, b * 256:(b + 1) * 256]))
                for j in range(2):
                    ps, rd, pi = L.take()
                    group(ps[:, 0:T], [(g_[:, k, j * P:(j + 1) * P], U[:, k, :]) for k in range(8)],
                          [[arrived, u_rdy[k]] for k in range(8)], rd)
                    done = group(ps[:, T:2 * T], [(u_[:, k, j * P:(j + 1) * P], U[:, k, :]) for k in range(8)],
                                 None, None, count=True)
                    tb, rd, bi = TB.take()
                    tk = actv(tb[:, 0:T], ps[:, 0:T], ACT.Tanh, done, rd, scale=0.5)
                    tk = stt(tb[:, T:512], tb[:, 0:T], 1.0, ps[:, 0:T], ALU.add, ALU.mult, tk)
                    tk = tt(dve, actT[:, 2 * b + j, :], tb[:, T:512], ps[:, T:512], ALU.mult, tk, free)
                    TB.give(bi, tk)
                    L.give(pi, tk)
                    rdy.append(tk)
                ring.give(si, done)
                yield
            gq = ts(dve, sm[:, 96:104], mods[:, gate0:gate0 + 8], 0.25, None, ALU.mult, None, mod_rdy[gate0 + 7], now())

            def epi(pair, ps, done):
                for j in range(2):
                    c = 2 * pair + j
                    h_rdy[c] = stt(H[:, c, :], ps[:, j * T:(j + 1) * T], sm[:, 96 + c:97 + c], H[:, c, :],
                                   ALU.mult, ALU.add, done, gq, h_rdy[c])
                return h_rdy[c]
            yield from linear(wd, 0, D, actT, rdy, epi, width=256)

        def rows_rsqrt(srcs, rowof, nrow, scale, e, post, dst8, sq_to=None):
            ps, rd, pi = X.take()
            for n, (s, tk) in enumerate(srcs):
                tb, trd, bi = TC.take()
                sq = actv(tb[:, 0:T], s, ACT.Square, trd, tk)
                last = mm(ps[0:8, 0:T], selc[:, rowof[n], :], tb[:, 0:T], rd if n == 0 else None, sq,
                          start=n == 0, stop=n == len(srcs) - 1, count=True)
                TC.give(bi, last)
            tk = ts(dve, dst8, ps[0:8, 0:T], scale / post ** 2, e / post ** 2, ALU.mult, ALU.add, last, now())
            X.give(pi, tk)
            tk = actv(dst8, dst8, ACT.Sqrt, tk)
            return dve(lambda en: en.reciprocal(dst8, dst8), tk)

        s_br = [sem("s_br0"), sem("s_br1")]

        def bias_rows():
            for h in range(16):
                ps, rd, pi = X.take()
                rb = V("rel_bias_2", 33)[:, h:h + 1].to_broadcast([33, P])
                done = mm(ps[:, 0:384], rb, oneh, rd, vec_in, (s_oh, 16), count=True)
                tb, rd, bi = TC.take()
                tk = dve(lambda e, tb=tb, ps=ps: e.tensor_copy(tb[:, 0:384], ps[:, 0:384]), done, rd)
                X.give(pi, tk)
                pool.dma(lambda e, h=h, tb=tb: e.dma_start(scratch[h, :, :], tb[:, 0:384]), s_br[h % 2], tk)
                TC.give(bi, (s_br[h % 2], 16 * (h // 2 + 1)))
                yield

        nlam = sm[:, 109:110]
        lam_tok = []

        def lambdas():
            tb, rd, bi = TC.take()
            lv = tb[0:1, 0:128]
            l1 = tt(dve, lv, lamv[:, 0:128], lamv[:, 128:256], ALU.mult, rd, (s_lam, 16))
            l2 = dve(lambda e: e.tensor_reduce(sm[0:1, 106:108], lv.rearrange("p (a n) -> p a n", a=2), AX.X, ALU.add), l1)
            TC.give(bi, l2)
            l2 = actv(sm[0:1, 106:108], sm[0:1, 106:108], ACT.Exp, l2)
            l2 = stt(sm[0:1, 108:109], sm[0:1, 106:107], -1.0, sm[0:1, 107:108], ALU.mult, ALU.add, l2)
            l2 = ts(dve, sm[0:1, 108:109], sm[0:1, 108:109], -(0.8 - 0.6), None, ALU.add, None, l2)
            yield
            ps, rd, pi = X.take()
            l2 = mm(ps[:, 0:1], C("ones", 1), sm[0:1, 108:109], rd, l2, count=True)
            tk = actv(nlam, ps[:, 0:1], ACT.Copy, l2)
            lam_tok.append(tk)
            X.give(pi, tk)

        run(ada(a["w_ada"], 0, (0, 16), 0, V("b_ada"), share=4))
        h_rdy = [x_in] * 8
        u_rdy = normed(V("g_ff1"), 8, 0, U, h_rdy, None, 0)
        ada1 = ada(a["w_ada"], 0, (16, 72), 0, V("b_ada"))
        lam = lambdas()
        next(lam)
        side = seq(lam, ada1, bias_rows())
        beside(ffn(a["w1_gate"], a["w1_up"], a["w1_down"], u_rdy, 16, h_rdy), side)
        while 71 not in mod_rdy:
            next(side)
        u_rdy = normed(V("g_mix"), 32, 24, U, h_rdy, now(), 1)

        w_in = a["w_in"]
        QR, KR, YA = B3(0), B3(1), B3(3)
        VA = B(2).rearrange("p (i n) -> p i n", i=2)
        qk_rdy = {}
        free0 = now()

        turning = []

        def rope_epi(dst, key):
            def epi(pair, ps, done):
                tb, rd, bi = TA.take()
                raw = actv(tb, ps, ACT.Copy, done, rd)
                if turning:
                    turning.pop()()
                turning.append(lambda: turn(pair, tb, bi, raw))
                return raw

            def turn(pair, tb, bi, raw):
                p2, rd2, pi2 = X.take()
                rt = mm(p2, rope[:, 0:128], tb, raw, rd2, (s_rope, 16), count=True)
                tb2, rd3, bi2 = TB.take()
                cosb = rope[:, 128:384].unsqueeze(1).to_broadcast([P, 2, T])
                sinb = rope[:, 384:640].unsqueeze(1).to_broadcast([P, 2, T])
                d3 = dst[:, 2 * pair:2 * pair + 2, :]
                a1 = tt(pool, d3, tb.rearrange("p (c t) -> p c t", t=T), cosb, ALU.mult, raw, free0, (s_rope, 16))
                b1 = tt(dve, tb2.rearrange("p (c t) -> p c t", t=T), p2.rearrange("p (c t) -> p c t", t=T), sinb, ALU.mult, rt, rd3)
                X.give(pi2, b1)
                TA.give(bi, rt, a1)
                s = tt(dve, d3, d3, tb2.rearrange("p (c t) -> p c t", t=T), ALU.add, a1, b1)
                TB.give(bi2, s)
                qk_rdy[(key, 2 * pair)] = qk_rdy[(key, 2 * pair + 1)] = s
            return epi

        beside(linear(w_in, 0, D, U, u_rdy, rope_epi(QR, "q")), side)
        beside(linear(w_in, D, D, U, u_rdy, rope_epi(KR, "k")), side)

        def token_major(w, c0, n, src, rdy, i, waits, view=None, arrived=None):
            ps, rd, pi = L.take()
            done = group(ps[:, 0:n], [(src[:, k, i * P:(i + 1) * P], w[:, k, c0:c0 + n]) for k in range(8)],
                         [[arrived, rdy[k]] for k in range(8)], rd, count=True)
            return ps, done, pi

        va_rdy = []
        for b in range(2):
            (wv,), arrived, si = load((0, w_in[:, 2 * D + b * 512:2 * D + (b + 1) * 512]))
            for i in range(2):
                ps, done, pi = token_major(wv, 0, 512, U, u_rdy, i, None, arrived=arrived)
                if turning:
                    turning.pop()()
                tk = actv(VA[:, i, b * 512:(b + 1) * 512], ps, ACT.Copy, done, free0)
                L.give(pi, tk)
                va_rdy.append(tk)
            ring.give(si, done)

        EB = arena[:, 7 * UNIT:7 * UNIT + 3072].rearrange("p (n c k) -> p n c k", n=4, c=2)
        ABT = sb("ABT", [P, 4, 384])
        AB, AT = ABT[:, 0:2, :], ABT[:, 2:4, :]
        eb = Ring([EB[:, i, :, :] for i in range(4)])
        ab = Ring([AB[:, i, :] for i in range(2)])
        at = Ring([AT[:, i, :] for i in range(2)])
        st = sb("st", [P, 4, 24])
        stR = Ring([st[:, i, :] for i in range(2)])
        TILES = [(0, 0, 128, 128), (1, 128, 384, 0)]

        def transposed3(src, waits, PT, PA):
            ps, rd, pi = PT.take()
            for n in range(3):
                done = tr(ps[:, n * P:(n + 1) * P], src[:, n * P:(n + 1) * P], P, rd if n == 0 else None, waits, count=n == 2)
            t_, rd, ti = PA.take()
            tk = actv(t_, ps[:, 0:384], ACT.Copy, done, rd)
            PT.give(pi, tk)
            return t_, tk, ti, done

        ya_rdy = [None] * 8

        def diff_attention(h0):
            for h in range(h0, 8, 2):
                ev, erd, ei = eb.take()
                s_, srd, s_i = stR.take()
                mx = []
                for c in range(2):
                    ps, rd, pi = S.take()
                    q = QR[64 * c:64 * c + 64, h, :]
                    k = KR[64 * c:64 * c + 64, h, :]
                    mm(ps[:, 0:128], q[:, 0:128], k[:, 0:128], rd, qk_rdy[("q", h)], qk_rdy[("k", h)])
                    done = mm(ps[:, 128:384], q[:, 128:256], k[:, 0:256], count=True)
                    for i, a0, a1, m0 in TILES:
                        tk = dve(lambda e, ps=ps, a0=a0, a1=a1, m0=m0, c=c, i=i, ev=ev, s_=s_: e.tensor_tensor_reduce(
                            ev[:, c, a0:a1], ps[:, a0:a1], mblk[:, m0:256], 0.125, NEG, ALU.add, ALU.max,
                            s_[:, 2 * c + i:2 * c + i + 1]), done, erd, srd)
                    S.give(pi, tk)
                    mx.append(tk)
                nm = ts(dve, s_[:, 4:8], s_[:, 0:4], -1.0, None, ALU.mult, None, mx)
                yield
                for c in range(2):
                    for i, a0, a1, m0 in TILES:
                        n = 2 * c + i
                        ex = actv(ev[:, c, a0:a1], ev[:, c, a0:a1], ACT.Exp, nm, bias=s_[:, 4 + n:5 + n],
                                  accum_out=s_[:, 8 + n:9 + n])
                r = dve(lambda e, s_=s_: e.reciprocal(s_[:, 12:16], s_[:, 8:12]), ex)
                r = ts(dve, s_[:, 14:16], s_[:, 14:16], nlam, None, ALU.mult, None, r, lam_tok)
                a_, ard, ai = ab.take()
                for i, a0, a1, m0 in TILES:
                    tk = ts(dve, a_[:, a0:a1], ev[:, 0, a0:a1], s_[:, 12 + i:13 + i], None, ALU.mult, None, r, ard)
                    tk = stt(a_[:, a0:a1], ev[:, 1, a0:a1], s_[:, 14 + i:15 + i], a_[:, a0:a1], ALU.mult, ALU.add, tk)
                eb.give(ei, tk)
                stR.give(s_i, tk)
                yield
                aT, tk, ti, trd = transposed3(a_, tk, X, at)
                ab.give(ai, trd)
                ps, rd, pi = S.take()
                mm(ps[:, 0:T], VA[:, 0, h * P:(h + 1) * P], aT[:, 0:T], rd, tk, va_rdy, start=True, stop=False)
                done = mm(ps[:, 128:T], VA[:, 1, h * P:(h + 1) * P], aT[:, 256:384], start=False, stop=True, count=True)
                at.give(ti, done)
                tk = actv(YA[:, h, :], ps[:, 0:T], ACT.Copy, done, free0)
                S.give(pi, tk)
                ya_rdy[h] = tk
                yield

        def diff_norm():
            r8 = rows[0:8, 0, :]
            rk = rows_rsqrt([(YA[:, h, :], ya_rdy[h]) for h in range(8)], list(range(8)), 8, 1.0 / 128, EPS, 0.8, r8)
            yield
            for h in range(8):
                ps, rd, pi = X.take()
                done = mm(ps[:, 0:T], selr[:, h, :], r8, rd, rk, count=True)
                tk = stt(YA[:, h, :], YA[:, h, :], V("g_subln"), ps[:, 0:T], ALU.mult, ALU.mult, done)
                X.give(pi, tk)
                out_rdy["ya", h] = tk
                if h % 2:
                    yield

        rows = sb("rows", [16, 8, T])
        out_rdy = {}
        XM = arena[:, 4 * UNIT:5 * UNIT].rearrange("p (c t) -> p c t", t=260)
        XC, OP = B3(5), B3(6)
        hw = sb("hw", [P, 40 + 96])
        hw1 = ts(dve, hw[:, 0:40], vec[:, VO["conv_w"][0]:VO["conv_w"][0] + 40], 0.5, None, ALU.mult, None)
        hw2 = ts(dve, hw[:, 40:136], V("a_conv_w_2"), 0.5, None, ALU.mult, None)
        z1 = dve(lambda e: e.memset(XM[:, :, 0:3], 0.0), free0)
        xm_rdy, xc_rdy, op_rdy = [None] * 8, [None] * 8, [None] * 8

        def conv_silu(pad, pad_rdy, w, dst, bias, dwait):
            tb, rd, bi = TB.take()
            y = tb[:, 0:T]
            if bias is None:
                tk = ts(dve, y, pad[:, 0:T], w(0), None, ALU.mult, None, pad_rdy, rd)
            else:
                tk = ts(dve, y, pad[:, 0:T], w(0), bias, ALU.mult, ALU.add, pad_rdy, rd)
            for k in range(1, 4):
                tk = stt(y, pad[:, k:k + T], w(k), y, ALU.mult, ALU.add, tk)
            th = actv(tb[:, T:512], y, ACT.Tanh, tk)
            tk = stt(dst, tb[:, T:512], 1.0, y, ALU.add, ALU.mult, th, dwait)
            TB.give(bi, tk)
            return tk

        def xm_epi(pair, ps, done):
            if pair:
                conv_pair(pair - 1)
            tk = actv(XM[:, 2 * pair:2 * pair + 2, 3:259], ps.rearrange("p (c t) -> p c t", t=T), ACT.Copy, done, free0)
            xm_rdy[2 * pair] = xm_rdy[2 * pair + 1] = tk
            return tk

        def conv_pair(pair):
            for c in (2 * pair, 2 * pair + 1):
                xc_rdy[c] = conv_silu(XM[:, c, :], [xm_rdy[c], z1], lambda k, c=c: hw[:, 8 * k + c:8 * k + c + 1], XC[:, c, :],
                                      hw[:, 32 + c:33 + c], hw1)

        def op_epi(pair, ps, done):
            if pair == 0:
                conv_pair(3)
            return tanh_epi(OP, op_rdy)(pair, ps, done)

        def tanh_epi(dst, rdy):
            def epi(pair, ps, done):
                tk = actv(dst[:, 2 * pair:2 * pair + 2, :], ps.rearrange("p (c t) -> p c t", t=T), ACT.Tanh, done, scale=0.5)
                rdy[2 * pair] = rdy[2 * pair + 1] = tk
                return tk
            return epi

        together(seq(rounds(diff_attention(0), diff_attention(1)), diff_norm()), seq(side, linear(w_in, 3 * D, D, U, u_rdy, xm_epi),
                                       linear(w_in, 4 * D, D, U, u_rdy, op_epi)))

        MQ, MK, MVT, HC = B3(0), B3(1), B3(2), B3(2)
        MV = B(7).rearrange("p (i n) -> p i n", i=2)
        GA, GB = B3(8), B3(9)
        ga_rdy, gb_rdy = [None] * 8, [None] * 8
        YB = HC
        wif = V("w_if").rearrange("p (t h c g) -> p t h c g", t=3, h=4, c=2)
        gcol = sb("gcol", [P, 2, 20])
        xmv = XM[:, :, 3:259]

        def mlstm():
            free = now()
            (wq, wk), arrived, si = load((0, a["w_mq"]), (2048, a["w_mk"]))
            (wv,), arrived2, si2 = load((0, a["w_mv"]))
            q_r, k_r, vt_r, v_r = {}, {}, {}, {}

            def turned(h):
                ps, rd, pi = L.take()
                for n in range(4):
                    e2, i = n // 2, n % 2
                    done = tr(ps[:, n * P:(n + 1) * P], MV[:, i, h * T + e2 * P:h * T + (e2 + 1) * P], P,
                              [rd, v_r[h]] if n == 0 else None, count=n == 3)
                tk = actv(MVT[:, 2 * h:2 * h + 2, :], ps.rearrange("p (c t) -> p c t", t=T), ACT.Copy, done, free)
                L.give(pi, tk)
                vt_r[h] = tk

            for h in range(4):
                for w, arr, src, rdy, dst, rr in ((wq, arrived, XC, xc_rdy, MQ, q_r), (wk, arrived, XC, xc_rdy, MK, k_r)):
                    ps, rd, pi = L.take()
                    for e2 in range(2):
                        done = group(ps[:, e2 * T:(e2 + 1) * T],
                                     [(w[:, 2 * h + k, e2 * P:(e2 + 1) * P], src[:, 2 * h + k, :]) for k in range(2)],
                                     [[arr, rdy[2 * h + k]] for k in range(2)], rd, count=e2 == 1)
                    tk = actv(dst[:, 2 * h:2 * h + 2, :], ps.rearrange("p (c t) -> p c t", t=T), ACT.Copy, done, free)
                    L.give(pi, tk)
                    rr[h] = tk
                ps, rd, pi = L.take()
                for i in range(2):
                    done = group(ps[:, i * T:(i + 1) * T],
                                 [(xmv[:, 2 * h + k, i * P:(i + 1) * P], wv[:, 2 * h + k, :]) for k in range(2)],
                                 [[arrived2, xm_rdy[2 * h + k]] for k in range(2)], rd, count=i == 1)
                tk = tt_copy(MV[:, :, h * T:(h + 1) * T], ps.rearrange("p (i n) -> p i n", i=2), done, free)
                L.give(pi, tk)
                pdone = done
                v_r[h] = tk
                if h:
                    turned(h - 1)
            yield
            turned(3)
            ring.give(si, pdone)
            ring.give(si2, pdone)
            yield
            R = rows
            ps, rd, pi = X.take()
            prs, rr = [], []
            for t3, (buf, r_) in enumerate(((MQ, q_r), (MK, k_r), (MVT, vt_r))):
                for h in range(4):
                    for c2 in range(2):
                        prs.append((wif[:, t3, h, c2, :], buf[:, 2 * h + c2, :]))
                        rr.append(r_[h])
            gates_done = group(ps[0:8, 0:T], prs, rr, rd, count=True)
            tk = tt_copy(R[0:8, 6, :], ps[0:8, 0:T], gates_done, free)
            X.give(pi, tk)
            yield
            ps, rd, pi = X.take()
            for i in range(2):
                done = tr(ps[:, 8 * i:8 * i + 8], R[0:8, 6, i * P:(i + 1) * P], 8, rd if i == 0 else None, tk, count=i == 1)
            tk = tt_copy(gcol[:, :, 0:8], ps[:, 0:16].rearrange("p (i g) -> p i g", i=2), done, free)
            X.give(pi, tk)
            yield
            ps, rd, pi = X.take()
            for i in range(2):
                tr(ps[0:4, i * P:(i + 1) * P], gcol[:, i, 0:4], P, rd if i == 0 else None, tk)
            for i in range(2):
                done = tr(ps[0:4, T + i * P:T + (i + 1) * P], gcol[:, i, 4:8], P, count=i == 1)
            ig = ts(dve, R[0:4, 1, :], ps[0:4, 0:T], V("b_i", 4), None, ALU.add, None, done, free)
            fg = ts(dve, R[0:4, 2, :], ps[0:4, T:512], V("b_f", 4), None, ALU.add, None)
            X.give(pi, fg)
            tk = actv(R[0:4, 3, :], R[0:4, 2, :], ACT.Abs, fg)
            tk = actv(R[0:4, 3, :], R[0:4, 3, :], ACT.Exp, tk, scale=-1.0)
            tk = actv(R[0:4, 3, :], R[0:4, 3, :], ACT.Ln, tk, bias=1.0)
            tk = stt(R[0:4, 2, :], R[0:4, 2, :], 0.0, R[0:4, 3, :], ALU.min, ALU.subtract, tk)
            tk = dve(lambda e: e.tensor_tensor_scan(R[0:4, 3, :], one_row[0:4, :], R[0:4, 2, :], 0.0, ALU.mult, ALU.add), tk, one_rdy)
            tk = tt(dve, R[0:4, 1, :], R[0:4, 1, :], R[0:4, 3, :], ALU.subtract, tk, ig)
            tk = dve(lambda e: e.tensor_tensor_scan(R[0:4, 2, :], R[0:4, 1, :], R[0:4, 1, :], 0.0, ALU.max, ALU.max), tk)
            tk2 = stt(R[0:4, 5, :], R[0:4, 3, :], -1.0, R[0:4, 2, :], ALU.mult, ALU.subtract, tk)
            tk2 = actv(R[0:4, 5, :], R[0:4, 5, :], ACT.Exp, tk2)
            tk3 = ts(dve, R[0:4, 4, :], R[0:4, 2, :], -1.0, None, ALU.mult, None, tk)
            yield
            ps, rd, pi = X.take()
            for i in range(2):
                done = tr(ps[:, 4 * i:4 * i + 4], R[0:4, 1, i * P:(i + 1) * P], 4, rd if i == 0 else None, tk, count=i == 1)
            gs = tt_copy(gcol[:, :, 8:12], ps[:, 0:8].rearrange("p (i g) -> p i g", i=2), done)
            X.give(pi, gs)
            yield
            hc_rdy = [None] * 8
            for h in range(4):
                ps, rd, pi = X.take()
                bc = mm(ps, selr[0:4, h, :], R[0:4, 4:6, :], rd, tk2, tk3, count=True)
                w_, wrd, wi = TA.take()
                xs = tt(dve, w_[:, 0:T], ps[:, 0:T], mtri[:, 0:T], ALU.add, bc, wrd)
                xs = tt(dve, w_[:, T:384], ps[:, 128:T], mtri[:, 256:384], ALU.add)
                em, emrd, emi = TB.take()
                emr = actv(em[:, 0:T], ps[:, T:512], ACT.Copy, bc, xs, emrd)
                X.give(pi, xs, emr)
                actv(w_[:, 0:T], w_[:, 0:T], ACT.Exp, xs, gs, bias=gcol[:, 0, 8 + h:9 + h])
                wr = actv(w_[:, T:384], w_[:, T:384], ACT.Exp, bias=gcol[:, 1, 8 + h:9 + h])
                sp_, rd, si_ = S.take()
                group(sp_[:, 0:T], [(MK[:, 2 * h + c, 0:P], MQ[:, 2 * h + c, :]) for c in range(2)], [[q_r[h], k_r[h]]] * 2, rd)
                done = group(sp_[:, T:384], [(MK[:, 2 * h + c, P:T], MQ[:, 2 * h + c, P:T]) for c in range(2)], None, None, count=True)
                sc_, srd, sci = ab.take()
                sc = stt(sc_, sp_[:, 0:384], 0.0625, w_[:, 0:384], ALU.mult, ALU.mult, wr, done, srd)
                TA.give(wi, sc)
                S.give(si_, sc)
                yield
                np_, rd, ni = S.take()
                for e2 in range(2):
                    o = h * T + e2 * P
                    mm(np_[:, e2 * T:(e2 + 1) * T], MV[:, 0, o:o + P], sc_[:, 0:T], rd if e2 == 0 else None, sc, v_r[h], stop=False)
                    num = mm(np_[:, e2 * T + P:(e2 + 1) * T], MV[:, 1, o:o + P], sc_[:, T:384], start=False, count=e2 == 1)
                dp, rd, di = X.take()
                mm(dp[:, 0:T], C("ones"), sc_[:, 0:T], rd, stop=False)
                den = mm(dp[:, P:T], C("ones"), sc_[:, T:384], start=False, count=True)
                ab.give(sci, den)
                dk = actv(em[:, T:512], dp[:, 0:T], ACT.Abs, den)
                X.give(di, dk)
                dk = tt(dve, em[:, 0:T], em[:, 0:T], em[:, T:512], ALU.max, dk, emr)
                dk = dve(lambda e, em=em: e.reciprocal(em[:, 0:T], em[:, 0:T]), dk)
                for e2 in range(2):
                    hk = tt(dve, HC[:, 2 * h + e2, :], np_[:, e2 * T:(e2 + 1) * T], em[:, 0:T], ALU.mult, dk, num, gates_done)
                    hc_rdy[2 * h + e2] = hk
                S.give(ni, hk)
                TB.give(emi, hk)
                yield
            r8 = rows[0:8, 0, :]
            rk = rows_rsqrt([(HC[:, c, :], hc_rdy[c]) for c in range(8)], [c // 2 for c in range(8)], 4, 1.0 / 256, EPS, 1.0, r8)
            hg = ts(dve, sm[:, 112:120], V("g_mlnorm"), 0.5, None, ALU.mult, None)
            hg = ts(dve, sm[:, 120:128], V("ml_skip"), 0.5, None, ALU.mult, None)
            yield
            for h in range(4):
                ps, rd, pi = X.take()
                done = mm(ps[:, 0:T], selr[:, h, :], r8, rd, rk, count=True)
                for e2 in range(2):
                    c = 2 * h + e2
                    tk = stt(HC[:, c, :], HC[:, c, :], sm[:, 112 + c:113 + c], ps[:, 0:T], ALU.mult, ALU.mult, done, hg)
                    tk2 = stt(HC[:, c, :], XC[:, c, :], sm[:, 120 + c:121 + c], HC[:, c, :], ALU.mult, ALU.add, tk, hg)
                    tk3 = stt(HC[:, c, :], OP[:, c, :], 1.0, HC[:, c, :], ALU.add, ALU.mult, tk2, op_rdy[c])
                    out_rdy["yb", c] = tk3
                X.give(pi, tk)
                yield

        def tt_copy(o, i, *waits):
            return dve(lambda e: e.tensor_copy(o, i), *waits)

        one_row = rows[0:8, 7, :]
        one_rdy = dve(lambda e: e.memset(one_row, 1.0))

        MG = GA

        def epi_a(pair, ps, done):
            for j in range(2):
                c = 2 * pair + j
                tk = stt(GA[:, c, :], GA[:, c, :], 1.0, ps[:, j * T:(j + 1) * T], ALU.add, ALU.mult, done, ga_rdy[c])
                ga_rdy[c] = tk
            return tk

        together(mlstm(), seq(linear(w_in, 5 * D, D, U, u_rdy, tanh_epi(GA, ga_rdy)),
                              linear(w_in, 6 * D, D, U, u_rdy, tanh_epi(GB, gb_rdy)),
                              linear(a["w_proj_a"], 0, D, YA, [out_rdy["ya", c] for c in range(8)], epi_a)))

        mg_rdy = ga_rdy

        def epi_b(pair, ps, done):
            tb, rd, bi = TB.take()
            for j in range(2):
                c = 2 * pair + j
                tk = stt(tb[:, j * T:(j + 1) * T], GB[:, c, :], 1.0, ps[:, j * T:(j + 1) * T], ALU.add, ALU.mult, done, gb_rdy[c], rd)
            s = tt(pool, MG[:, 2 * pair:2 * pair + 2, :], MG[:, 2 * pair:2 * pair + 2, :], tb.rearrange("p (c t) -> p c t", t=T),
                   ALU.add, tk, mg_rdy[2 * pair + 1])
            TB.give(bi, s)
            mg_rdy[2 * pair] = mg_rdy[2 * pair + 1] = s
            return tk

        run(linear(a["w_proj_b"], 0, D, YB, [out_rdy["yb", c] for c in range(8)], epi_b))

        def residual(scale_cols, scale_rdy):
            def epi(pair, ps, done):
                for j in range(2):
                    c = 2 * pair + j
                    h_rdy[c] = stt(H[:, c, :], ps[:, j * T:(j + 1) * T], scale_cols[:, c:c + 1], H[:, c, :],
                                   ALU.mult, ALU.add, done, scale_rdy, h_rdy[c])
                return h_rdy[c]
            return epi

        g2 = ts(dve, sm[:, 128:136], mods[:, 40:48], 0.5, None, ALU.mult, None, mod_rdy[47])
        run(linear(a["w_out"], 0, D, MG, mg_rdy, residual(sm[:, 128:136], g2)))

        u_rdy = normed(V("g_ff2"), 56, 48, U, h_rdy, now(), 2)
        ada2 = ada_both()
        beside(ffn(a["w2_gate"], a["w2_up"], a["w2_down"], u_rdy, 64, h_rdy), ada2)
        run(ada2)

        r_ = root(h_rdy)
        h_rdy = [stt(H[:, c, :], H[:, c, :], V("g_final")[:, c:c + 1], rstd[:, :], ALU.mult, ALU.mult, r_) for c in range(8)]

        u_rdy = normed(V("norm_g_2")[:, 0:8], 80, 72, U, h_rdy, now(), 4)
        free = now()
        wa = a["a_in_w_2"]
        lvls = ABT[:, :, :].rearrange("p i n -> p (i n)")[:, 0:1024]
        act.dma(lambda e: e.dma_start(lvls, a["lvls"]), s_lvl, free)
        lvls = lvls.rearrange("p (n i) -> p n i", n=8)
        lvl, lvlN = lvls[:, 0:1, :], lvls[:, 1:8, :]
        R = rows
        gb_ = sb("gb_", [P, 2, 32])
        (wv,), arrived, si = load((0, wa[:, 4096:4112]))
        ps, rd, pi = L.take()
        done = group(ps[0:16, 0:T], [(wv[:, k, :], U[:, k, :]) for k in range(8)], [[arrived, u_rdy[k]] for k in range(8)], rd, count=True)
        ring.give(si, done)
        tk = dve(lambda e, ps=ps: e.tensor_copy(rows[0:16, 5, :], ps[0:16, 0:T]), done, free)
        L.give(pi, tk)
        ps, rd, pi = L.take()
        for i in range(2):
            done = tr(ps[:, 16 * i:16 * i + 16], rows[0:16, 5, i * P:(i + 1) * P], 16, rd if i == 0 else None, tk, count=i == 1)
        gtok = dve(lambda e, ps=ps: e.tensor_copy(gb_[:, :, 0:16], ps[:, 0:32].rearrange("p (i g) -> p i g", i=2)), done)
        L.give(pi, gtok)
        QG, KG, VG, ZG = B3(0), B3(1), B3(2), B3(3)
        cv_rdy = {}
        pads = B(9, 1040).rearrange("p (a b n) -> p a b n", a=2, b=2)
        padr = Ring([pads[:, i, :, :] for i in range(2)])
        z2 = dve(lambda e: e.memset(pads[:, :, :, 0:3], 0.0), free)

        r8q, r8k = rows[0:8, 0, :], rows[0:8, 4, :]
        squares, sums = [], {}

        def add_squares(pair, tb, bi, sq):
            key, part = pair // 4, pair % 4
            if part == 0:
                sums[key] = X.take()
            ps, rd, pi = sums[key]
            for j in range(2):
                last = mm(ps[0:8, 0:T], selc[:, 2 * part + j, :], tb[:, j * T:(j + 1) * T], rd if part + j == 0 else None, sq,
                          start=part + j == 0, stop=part + j == 4, count=j == 1)
            TC.give(bi, last)
            if part == 3:
                k2 = (128.0, 1.0)[key]
                dst8 = (r8q, r8k)[key]
                tk = ts(dve, dst8, ps[0:8, 0:T], k2, EPS * k2, ALU.mult, ALU.add, last, free)
                X.give(pi, tk)
                tk = actv(dst8, dst8, ACT.Sqrt, tk)
                g_tok[key] = dve(lambda e: e.reciprocal(dst8, dst8), tk)

        def conv_epi(pair, ps, done):
            if len(squares) > 1 or pair > 8 and squares:
                add_squares(*squares.pop(0))
            pd, rd, di = padr.take()
            cp = actv(pd[:, :, 3:259], ps.rearrange("p (c t) -> p c t", t=T), ACT.Copy, done, rd)
            for j in range(2):
                c = 2 * pair + j
                dst = (QG, KG, VG)[c // 8][:, c % 8, :]
                cv_rdy[c] = conv_silu(pd[:, j, :], [cp, z2], lambda k, c=c: hw[:, 40 + 24 * k + c:41 + 24 * k + c], dst,
                                      None, [free, hw2])
            padr.give(di, cv_rdy[c])
            if pair < 8:
                tb, rd, bi = TC.take()
                src = (QG, KG)[pair // 4][:, 2 * (pair % 4):2 * (pair % 4) + 2, :]
                sq = actv(tb.rearrange("p (c t) -> p c t", t=T), src, ACT.Square, rd, cv_rdy[c])
                squares.append((pair, tb, bi, sq))
            return cp

        g_tok = {}

        def delta_gates():
            yield
            ps, rd, pi = X.take()
            for i in range(2):
                tr(ps[0:8, i * P:(i + 1) * P], gb_[:, i, 0:8], P, rd if i == 0 else None, gtok)
            for i in range(2):
                done = tr(ps[0:8, T + i * P:T + (i + 1) * P], gb_[:, i, 8:16], P, count=i == 1)
            bt0 = actv(R[0:8, 1, :], ps[0:8, 0:T], ACT.Tanh, done, free, scale=0.5)
            bt = ts(dve, R[0:8, 1, :], R[0:8, 1, :], 1.0, 0.5, ALU.add, ALU.mult, bt0)
            ak = ts(dve, R[0:8, 2, :], ps[0:8, T:512], V("a_dt_bias_2", 8), None, ALU.add, None, done, bt0)
            X.give(pi, ak)
            tk = actv(R[0:8, 3, :], R[0:8, 2, :], ACT.Abs, ak)
            tk = actv(R[0:8, 3, :], R[0:8, 3, :], ACT.Exp, tk, scale=-1.0)
            tk = actv(R[0:8, 3, :], R[0:8, 3, :], ACT.Ln, tk, bias=1.0)
            el = actv(sm[0:8, 136:137], V("a_A_log_2", 8), ACT.Exp)
            tk = stt(R[0:8, 2, :], R[0:8, 2, :], 0.0, R[0:8, 3, :], ALU.max, ALU.add, tk)
            tk = ts(dve, R[0:8, 2, :], R[0:8, 2, :], sm[0:8, 136:137], -1.0, ALU.mult, ALU.mult, tk, el)
            gc = dve(lambda e: e.tensor_tensor_scan(R[0:8, 3, :], one_row[0:8, :], R[0:8, 2, :], 0.0, ALU.mult, ALU.add), tk)
            yield
            yield
            ps, rd, pi = X.take()
            for i in range(2):
                tr(ps[:, 16 * i:16 * i + 8], R[0:8, 1, i * P:(i + 1) * P], 8, rd if i == 0 else None, bt, gc)
                done = tr(ps[:, 16 * i + 8:16 * i + 16], R[0:8, 3, i * P:(i + 1) * P], 8, count=i == 1)
            pv = ps[:, 0:32].rearrange("p (i g) -> p i g", i=2)
            tk = tt_copy(gb_[:, :, 16:24], pv[:, :, 0:8], done)
            tk = ts(dve, gb_[:, :, 24:32], pv[:, :, 8:16], -1.0, None, ALU.mult, None, done)
            X.give(pi, tk)
            g_tok["tok"] = tk
            g_tok["beta"], g_tok["gc"] = bt, gc
            yield

        MT = arena[:, 6 * UNIT:6 * UNIT + 3072].rearrange("p (h n) -> p h n", h=8)
        ATT = arena[:, 6 * UNIT + 3072:6 * UNIT + 6144].rearrange("p (h n) -> p h n", h=8)
        VB = B(4).rearrange("p (h i n) -> p h i n", h=8, i=2)
        DM = B(5).rearrange("p (u n) -> p u n", u=16)
        DT = B(9).rearrange("p (u n) -> p u n", u=16)
        P1 = B(2).rearrange("p (u n) -> p u n", u=16)
        UU = B(1).rearrange("p (h i n) -> p h i n", h=8, i=2)
        OG = B3(0)

        def delta(h0):
            rq, rk = g_tok[0], g_tok[1]
            for h in range(h0, 8, 2):
                ps, rd, pi = X.take()
                mm(ps[:, 0:T], selr[:, h, :], r8q, rd, rq)
                done = mm(ps[:, T:512], selr[:, h, :], r8k, rk, count=True)
                qn = tt(dve, QG[:, h, :], QG[:, h, :], ps[:, 0:T], ALU.mult, done)
                kn = tt(dve, KG[:, h, :], KG[:, h, :], ps[:, T:512], ALU.mult, done)
                X.give(pi, kn)
                ps, rd, pi = X.take()
                mm(ps[:, 0:T], selr[:, h, :], R[0:8, 1, :], rd, g_tok["beta"])
                done = mm(ps[:, T:512], selr[:, h, :], R[0:8, 3, :], g_tok["gc"], count=True)
                kb, kbrd, kbi = TA.take()
                kbt = tt(dve, kb[:, 0:T], KG[:, h, :], ps[:, 0:T], ALU.mult, done, kn, kbrd)
                dc, dcrd, dci = TB.take()
                dk = tt(dve, dc[:, 0:T], ps[:, T:512], mtri[:, 0:T], ALU.add, dcrd)
                dk = tt(dve, dc[:, T:384], ps[:, T + P:512], mtri[:, 256:384], ALU.add)
                X.give(pi, dk)
                actv(dc[:, 0:T], dc[:, 0:T], ACT.Exp, dk, g_tok["tok"], bias=gb_[:, 0, 24 + h:25 + h])
                dk = actv(dc[:, T:384], dc[:, T:384], ACT.Exp, bias=gb_[:, 1, 24 + h:25 + h])
                ps, rd, pi = X.take()
                for i in range(2):
                    done = tr(ps[:, i * P:(i + 1) * P], VG[:, h, i * P:(i + 1) * P], P, rd if i == 0 else None,
                              cv_rdy[16 + h], count=i == 1)
                for i in range(2):
                    vb = actv(VB[:, h, i, :], ps[:, i * P:(i + 1) * P], ACT.Copy, done, g_tok["tok"], scale=gb_[:, i, 16 + h:17 + h])
                X.give(pi, vb)
                vb_rdy[h] = vb
                yield
                p1, rd, i1 = S.take()
                mm(p1[:, 0:T], KG[:, h, 0:P], kb[:, 0:T], rd, kbt)
                done = mm(p1[:, T:384], KG[:, h, P:T], kb[:, P:T], count=True)
                TA.give(kbi, done)
                p2, rd, i2 = S.take()
                mm(p2[:, 0:T], KG[:, h, 0:P], QG[:, h, :], rd, qn)
                done2 = mm(p2[:, T:384], KG[:, h, P:T], QG[:, h, P:T], count=True)
                mt = tt(dve, MT[:, h, :], p1[:, 0:384], dc[:, 0:384], ALU.mult, done, dk, free)
                S.give(i1, mt)
                att = tt(dve, ATT[:, h, :], p2[:, 0:384], dc[:, 0:384], ALU.mult, done2)
                S.give(i2, att)
                TB.give(dci, att)
                mt_rdy[h] = att
                yield

        vb_rdy, mt_rdy = {}, {}
        beside(linear(wa, 0, 3 * D, U, u_rdy, conv_epi), delta_gates())
        zg_rdy = [None] * 8

        def silu_epi(dst, rdy, w):
            def epi(pair, ps, done):
                tb, rd, bi = TC.take()
                th = actv(tb, ps, ACT.Tanh, done, rd, scale=0.5)
                tk = stt(dst[:, 2 * pair:2 * pair + 2, :], tb.rearrange("p (c t) -> p c t", t=T), 1.0,
                         ps.rearrange("p (c t) -> p c t", t=T), ALU.add, ALU.mult, th, w)
                TC.give(bi, tk)
                rdy[2 * pair] = rdy[2 * pair + 1] = tk
                return tk
            return epi
        zg = linear(wa, 3 * D, D, U, u_rdy, silu_epi(ZG, zg_rdy, free))
        next(zg)
        together(delta(0), delta(1))

        d_rdy = {}

        def inverse(g):
            def mt(u):
                h, i = u // 2, u % 2
                return MT[:, h, 256:384] if i else MT[:, h, 0:128]
            us = list(range(4 * g, 4 * g + 4))
            sl = slice(4 * g, 4 * g + 4)
            rdy = [mt_rdy[2 * g], mt_rdy[2 * g + 1]]
            idb = ident.unsqueeze(1).to_broadcast([P, 4, P])
            mtv = MT[:, 2 * g:2 * g + 2, :].rearrange("p h (k n) -> p h k n", k=3)[:, :, 0:3:2, :]
            X2 = XX[g]

            def four(ps):
                return ps.rearrange("p (u n) -> p u n", u=4)

            def mask(m):
                return m.unsqueeze(1).to_broadcast([P, 4, P])

            ps, rd, pi = X2.take()
            for j, u in enumerate(us):
                done = tr(ps[:, j * P:(j + 1) * P], mt(u), P, rd if j == 0 else None, rdy, count=j == 3)
            pk = tt(dve, P1[:, sl, :], four(ps), mask(lvlN[:, 0, :]), ALU.mult, done, freei)
            X2.give(pi, pk)
            dk = tt(dve, DM[:, sl, :], idb, P1[:, sl, :], ALU.subtract, pk, freei)
            yield
            ek = None
            for h in range(2):
                ek = tt(pool, DT[:, 4 * g + 2 * h:4 * g + 2 * h + 2, :], mtv[:, h, :, :],
                        lvl[:, 0, :].unsqueeze(1).to_broadcast([P, 2, P]), ALU.mult, rdy, freei)
            ek = tt(pool, DT[:, sl, :], idb, DT[:, sl, :], ALU.subtract, ek)
            for n in range(1, 7):
                ps, rd, pi = X2.take()
                for j, u in enumerate(us):
                    done = mm(ps[:, j * P:(j + 1) * P], mt(u), DM[:, u, :], rd if j == 0 else None, dk, count=j == 3)
                pk = tt(dve, P1[:, sl, :], four(ps), mask(lvlN[:, n, :]), ALU.mult, done)
                X2.give(pi, pk)
                yield
                ps, rd, pi = X2.take()
                for j, u in enumerate(us):
                    done = mm(ps[:, j * P:(j + 1) * P], DT[:, u, :], P1[:, u, :], rd if j == 0 else None, pk, ek, count=j == 3)
                dk = tt(dve, DM[:, sl, :], DM[:, sl, :], four(ps), ALU.subtract, done, dk)
                X2.give(pi, dk)
                yield
                ps, rd, pi = X2.take()
                for j, u in enumerate(us):
                    done = tr(ps[:, j * P:(j + 1) * P], DM[:, u, :], P, rd if j == 0 else None, dk, count=j == 3)
                ek = actv(DT[:, sl, :], four(ps), ACT.Copy, done)
                X2.give(pi, ek)
            d_rdy[g] = [dk, ek]

        freei = [now(), (s_lvl, 16)]
        XX = [Ring([b[:, :] for b in banks[2 * g:2 * g + 2]]) for g in range(4)]
        for r in XX:
            r.readers = [freei] * 2
        together(*[inverse(g) for g in range(4)])
        after = now()
        for r in (L, S, X):
            r.readers = [after] * len(r.bufs)

        og_rdy = [None] * 8

        def delta_out(h0):
            for h in range(h0, 8, 2):
                u = 2 * h
                ps, rd, pi = X.take()
                done = mm(ps[:, 0:P], DT[:, u, :], VB[:, h, 0, :], rd, vb_rdy[h], after, count=True)
                uk = actv(UU[:, h, 0, :], ps[:, 0:P], ACT.Copy, done, after)
                X.give(pi, uk)
                yield
                ps, rd, pi = X.take()
                done = mm(ps[:, 0:P], MT[:, h, P:T], UU[:, h, 0, :], rd, uk, count=True)
                rk = tt(dve, VB[:, h, 1, :], VB[:, h, 1, :], ps[:, 0:P], ALU.subtract, done)
                X.give(pi, rk)
                yield
                ps, rd, pi = X.take()
                done = mm(ps[:, 0:P], DT[:, u + 1, :], VB[:, h, 1, :], rd, rk, count=True)
                uk = actv(UU[:, h, 1, :], ps[:, 0:P], ACT.Copy, done, after)
                X.give(pi, uk)
                yield
                ps, rd, pi = S.take()
                mm(ps[:, 0:T], UU[:, h, 0, :], ATT[:, h, 0:T], rd, uk, stop=False)
                done = mm(ps[:, P:T], UU[:, h, 1, :], ATT[:, h, T:384], start=False, count=True)
                ok = actv(OG[:, h, :], ps[:, 0:T], ACT.Copy, done, after)
                S.give(pi, ok)
                og_rdy[h] = ok
                yield
        beside(rounds(delta_out(0), delta_out(1)), zg, 5)
        r8 = rows[0:8, 0, :]
        rk = rows_rsqrt([(OG[:, h, :], og_rdy[h]) for h in range(8)], list(range(8)), 8, 1.0 / 128, EPS, 0.5, r8)
        run(zg)
        y_rdy = []
        for h in range(8):
            ps, rd, pi = X.take()
            done = mm(ps[:, 0:T], selr[:, h, :], r8, rd, rk, count=True)
            tk = stt(OG[:, h, :], OG[:, h, :], V("a_onorm_g_2"), ps[:, 0:T], ALU.mult, ALU.mult, done)
            X.give(pi, tk)
            y_rdy.append(tt(dve, OG[:, h, :], OG[:, h, :], ZG[:, h, :], ALU.mult, tk, zg_rdy[h]))
        after_delta = [og_rdy, now()]
        BT = arena[:, 6 * UNIT:6 * UNIT + 4096].rearrange("p (h n) -> p h n", h=16)
        s_bt = sem("s_bt")
        skew = bass.AP(tensor=scratch.tensor, offset=127, ap=[[383, P], [P * 384, 16], [1, T]])
        act.dma(lambda e: e.dma_start(BT, skew), s_bt, [(s, 16 * n) for s, n in zip(s_br, (8, 8))], after_delta)
        bt_rdy = (s_bt, 16)

        run(linear(a["a_out_w_2"], 0, D, OG, y_rdy, residual(mods[:, 88:96], mod_rdy[95])))

        freeu = now()
        r_ = root(h_rdy)
        SK = B3(0)
        free = now()
        A2 = sm[:, 144:152]
        a2 = stt(A2, mods[:, 104:112], 1.0, V("norm_g_2")[:, 8:16], ALU.add, ALU.mult, mod_rdy[111])
        s_rdy, u_rdy = [], []
        for c in range(8):
            tk = stt(SK[:, c, :], H[:, c, :], V("kv_norm_g_2")[:, c:c + 1], rstd[:, :], ALU.mult, ALU.mult, r_, free)
            s_rdy.append(tk)
        for c in range(8):
            tk = stt(U[:, c, :], H[:, c, :], A2[:, c:c + 1], rstd[:, :], ALU.mult, ALU.mult, a2, freeu)
            u_rdy.append(actv(U[:, c, :], U[:, c, :], ACT.Identity, tk, mod_rdy[103], bias=mods[:, 96 + c:97 + c]))

        KX = arena[:, 9 * UNIT:9 * UNIT + 1088].rearrange("p (g n) -> p g n", g=2)
        VW = arena[:, 9 * UNIT + 1088:9 * UNIT + 1600].rearrange("p (b i n) -> p b i n", b=2, i=2)
        BLK = arena[:, 8 * UNIT:8 * UNIT + 960].rearrange("p (s m g n) -> p s m g n", s=2, m=16, g=2)
        HK = arena[:, 8 * UNIT + 960:8 * UNIT + 1080].rearrange("p (s c n) -> p s c n", s=2, c=2)
        VC = arena[0:15, 8 * UNIT + 1110:8 * UNIT + 1110 + 128]
        blk_rdy, kw_rdy, vw_rdy = [], [], []

        def kv_prep():
            (wv,), arrived, si = load((0, a["kv_w_2"][:, 0:512]))
            for j in range(4):
                if j == 3:
                    for i in range(2):
                        ps, done, pi = token_major(wv, 384, 128, SK, s_rdy, i, None, arrived=arrived)
                        tk = tt_copy(VW[:, 0, i, :], ps[:, 0:128], done, free)
                        L.give(pi, tk)
                        vw_rdy.append(tk)
                    yield
                    continue
                ps, rd, pi = L.take()
                done = group(ps[:, 0:T], [(wv[:, k, j * P:(j + 1) * P], SK[:, k, :]) for k in range(8)],
                             [[arrived, s_rdy[k]] for k in range(8)], rd, count=True)
                if j < 2:
                    pos = V(("cmp_pos_k_2", "cmp_pos_v_2")[j])
                    for g in range(2):
                        for par in range(2):
                            src = ps[64 * g:64 * g + 64, :]
                            src = bass.AP(tensor=src.tensor, offset=src.offset + par, ap=[list(src.ap[0]), [2, 16], [16, 15]])
                            tk = tt(dve, BLK[64 * par:64 * par + 64, j, :, g, :], src,
                                    pos[64 * par:64 * par + 64, :].unsqueeze(2).to_broadcast([64, 16, 15]), ALU.add, done, free)
                            blk_rdy.append(tk)
                    L.give(pi, tk)
                else:
                    yield from dup(ps, pi, done, 0)
                yield
            ring.give(si, done)
            (wv,), arrived, si = load((0, a["kv_w_2"][:, 512:768]))
            ps, rd, pi = L.take()
            done = group(ps[:, 0:T], [(wv[:, k, 0:P], SK[:, k, :]) for k in range(8)], [arrived] * 8, rd, count=True)
            yield from dup(ps, pi, done, 1)
            for i in range(2):
                ps, done, pi = token_major(wv, 128, 128, SK, s_rdy, i, None, arrived=arrived)
                tk = tt_copy(VW[:, 1, i, :], ps[:, 0:128], done, free)
                L.give(pi, tk)
                vw_rdy.append(tk)
            ring.give(si, done)
            yield
            for s in range(2):
                w1 = a[("cmp_k_w1_2", "cmp_v_w1_2")[s]]
                (wv,), arrived, si = load((0, w1))
                ps, rd, pi = L.take()
                done = group(ps[0:30, 0:T], [(BLK[:, s, m, :, :].rearrange("p g n -> p (g n)"), wv[:, m, :]) for m in range(16)],
                             [[arrived, blk_rdy]] * 16, rd, count=True)
                ring.give(si, done)
                tb, rd, bi = TC.take()
                th = actv(tb[0:30, 0:T], ps[0:30, 0:T], ACT.Tanh, done, rd, scale=0.5)
                tk = stt(tb[0:30, 0:T], tb[0:30, 0:T], 1.0, ps[0:30, 0:T], ALU.add, ALU.mult, th)
                L.give(pi, tk)
                yield
                ps, rd, pi = L.take()
                for c in range(2):
                    done = tr(ps[:, 30 * c:30 * c + 30], tb[0:30, c * P:(c + 1) * P], 30, rd if c == 0 else None, tk, count=c == 1)
                TC.give(bi, done)
                hk = ts(dve, HK[:, s, :, :], ps[:, 0:60].rearrange("p (c n) -> p c n", c=2), 0.5, None, ALU.mult, None, done)
                L.give(pi, hk)
                yield
                ps, rd, pi = X.take()
                if s == 0:
                    w2 = V("cmp_k_w2_2").rearrange("p (c n) -> p c n", c=2)
                    for half in range(2):
                        for c in range(2):
                            done = mm(ps[64 * half:64 * half + 64, 0:30], w2[:, c, :], HK[:, 0, c, :], rd if half + c == 0 else None, hk,
                                      start=c == 0, stop=c == 1, count=half + c == 2)
                    tk = tt_copy(KX[:, :, 256:271], ps[:, 0:30].rearrange("p (g n) -> p g n", g=2), done, free)
                    cmp_rdy.append(tk)
                else:
                    w2 = V("cmp_v_w2_2").rearrange("p (c n) -> p c n", c=2)
                    for g in range(2):
                        for c in range(2):
                            done = mm(ps[0:15, 64 * g:64 * g + 64], HK[:, 1, c, 15 * g:15 * g + 15], w2[:, c, :], rd if g + c == 0 else None, hk,
                                      start=c == 0, stop=c == 1, count=g + c == 2)
                    tk = tt_copy(VC, ps[0:15, 0:128], done)
                    cmp_rdy.append(tk)
                X.give(pi, tk)
                yield

        cmp_rdy = []

        def dup(ps, pi, done, b):
            for g in range(2):
                for half in range(2):
                    tk = tt_copy(KX[64 * half:64 * half + 64, g, 271 * b:271 * b + 256], ps[64 * g:64 * g + 64, 0:T], done, free)
            kw_rdy.append(tk)
            L.give(pi, tk)
            yield

        QN, YN = B3(1), B3(5)
        ZS = [B3(2), B3(3), B3(4)]
        wb = a["b_in_w_2"]
        qn_rdy = [None] * 8
        zs_rdy = [[None] * 8 for _ in range(3)]

        def q_epi(pair, ps, done):
            tk = actv(QN[:, 2 * pair:2 * pair + 2, :], ps.rearrange("p (c t) -> p c t", t=T), ACT.Copy, done, free, scale=0.125)
            qn_rdy[2 * pair] = qn_rdy[2 * pair + 1] = tk
            return tk

        gates = sb("gates", [P, 2, 48])
        g3 = sb("g3", [P, 2, 16, 8])

        def z_linears():
            for m in range(4):
                for b in range(3):
                    def epi(pair, ps, done, b=b, m=m):
                        return silu_epi(ZS[b], zs_rdy[b], free)(pair + m, ps, done)
                    yield from linear(wb, D * (1 + b) + 256 * m, 256, U, u_rdy, epi, width=256)

        zl = z_linears()
        together(kv_prep(), seq(linear(wb, 0, D, U, u_rdy, q_epi), itertools.islice(zl, 3)))
        (wv,), arrived, si = load((0, wb[:, 4096:4144]))
        ps, rd, pi = L.take()
        done = group(ps[0:48, 0:T], [(wv[:, k, :], U[:, k, :]) for k in range(8)], [[arrived, u_rdy[k]] for k in range(8)], rd, count=True)
        ring.give(si, done)
        tb, rd, bi = TC.take()
        tk = actv(tb[0:48, 0:T], ps[0:48, 0:T], ACT.Tanh, done, rd, scale=0.5)
        L.give(pi, tk)
        ps, rd, pi = L.take()
        for i in range(2):
            done = tr(ps[:, 48 * i:48 * i + 48], tb[0:48, i * P:(i + 1) * P], 48, rd if i == 0 else None, tk, count=i == 1)
        TC.give(bi, done)
        tk = tt_copy(gates[:, :, :], ps[:, 0:96].rearrange("p (i g) -> p i g", i=2), done)
        L.give(pi, tk)
        gt_rdy = ts(dve, gates[:, :, :], gates[:, :, :], 1.0, 0.25, ALU.add, ALU.mult, tk)

        m15 = C("m15")
        y_rdy = [None] * 8
        after = now()
        L.bufs, L.i = [b[:, :] for b in banks[0:2]], -1
        PS = Ring([b[:, :] for b in banks[2:6]])
        PO = Ring([(banks[6][:, :], banks[7][:, :])])
        EE = Ring([B(0)[:, 0:798], B(0)[:, 798:1596], arena[:, 8 * UNIT + 1240:8 * UNIT + 2038]])
        EA = Ring([tmpA[:, :, :].rearrange("p i n -> p (i n)")[:, 0:1024],
                   ABT[:, :, :].rearrange("p i n -> p (i n)")[:, 0:1024]])
        ES = Ring([st[:, i, :] for i in range(4)])
        for r in (L, PS, PO, EE, EA, ES):
            r.readers = [after] * len(r.bufs)
        for e_ in EE.bufs:
            e_zero = dve(lambda e, e_=e_: e.memset(e_[:, 775:783], 0.0), after)
        TILE6 = [(0, 128), (128, 384), (384, 512), (512, 768), (768, 775), (783, 798)]
        heads = {}

        def scores(h):
            j, lo, g = h // 2, 64 * (h % 2), h // 8
            q = QN[lo:lo + 64, j, :]
            kx = KX[lo:lo + 64, g, :]
            s_, srd, s_i = ES.take()
            E, erd, ei = EE.take()
            pa, rda, ia = PS.take()
            mm(pa[:, 0:256], q[:, 0:128], kx[:, 0:542].rearrange("p (b t) -> p b t", b=2)[:, :, 0:128], rda, qn_rdy[j], kw_rdy)
            da = mm(pa[:, 256:512], q[:, 128:256], kx[:, 0:256], count=True)
            pb, rdb, ib = PS.take()
            mm(pb[:, 0:7], q[:, 0:128], kx[:, 256:263], rdb, cmp_rdy)
            db = mm(pb[:, 15:286], q[:, 128:256], kx[:, 256:527], count=True)
            b0, b1 = BT[:, h, 128:256], BT[:, h, :]
            for n, src, bias, done in ((0, pa[:, 0:128], b0, da), (2, pa[:, 128:256], b0, da), (1, pa[:, 256:512], b1, da),
                                       (4, pb[:, 0:7], BT[:, h, 159:256:16], db), (5, pb[:, 15:30], BT[:, h, 31:256:16], db),
                                       (3, pb[:, 30:286], b1, db)):
                a0, a1 = TILE6[n]
                mk = dve(lambda e, E=E, a0=a0, a1=a1, src=src, bias=bias, s_=s_, n=n: e.tensor_tensor_reduce(
                    E[:, a0:a1], src, bias, 1.0, -3e38, ALU.add, ALU.max, s_[:, n:n + 1]), done, erd, srd, bt_rdy)
                if n == 1:
                    PS.give(ia, mk)
            PS.give(ib, mk)
            nm = ts(dve, s_[:, 6:12], s_[:, 0:6], -1.0, None, ALU.mult, None, mk)
            heads[h] = [E, ei, s_, s_i, nm]

        def weights(h):
            E, ei, s_, s_i, nm = heads[h]
            for n in (4, 5, 0, 1, 2, 3):
                a0, a1 = TILE6[n]
                kw = {"accum_out": s_[:, 12 + n:13 + n]} if n < 4 else {}
                ex = actv(E[:, a0:a1], E[:, a0:a1], ACT.Exp, nm, bias=s_[:, 6 + n:7 + n], **kw)
                if n == 5:
                    cx = ex
            for n, m0, m1 in ((4, 0, 7), (5, 7, 22)):
                a0, a1 = TILE6[n]
                sx = dve(lambda e, E=E, a0=a0, a1=a1, s_=s_, n=n, m0=m0, m1=m1: e.tensor_tensor_reduce(
                    E[:, a0:a1], E[:, a0:a1], m15[:, m0:m1], 1.0, 0.0, ALU.mult, ALU.add, s_[:, 12 + n:13 + n]), cx)
            sx = ts(dve, s_[:, 16:18], s_[:, 16:18], 1e-30, None, ALU.max, None, sx)
            rk = dve(lambda e, s_=s_: e.reciprocal(s_[:, 18:24], s_[:, 12:18]), sx, ex)
            pk = []
            for n in range(6):
                a0, a1 = TILE6[n]
                b = (1, 1, 2, 2, 0, 0)[n]
                pk.append(ts(dve, E[:, a0:a1], E[:, a0:a1], s_[:, 18 + n:19 + n], gates[:, n % 2, 16 * b + h:16 * b + h + 1],
                             ALU.mult, ALU.mult, rk, gt_rdy))
            ES.give(s_i, pk[5])
            heads[h][4] = pk

        def turned_weights(h):
            E, ei, s_, s_i, pk = heads[h]
            A_, rd, ai = EA.take()
            cks = []
            for b in range(2):
                ps, prd, pi = PS.take()
                for n in range(3):
                    o = 384 * b + n * P
                    tr(ps[:, n * P:(n + 1) * P], E[:, o:o + P], P, prd if n == 0 else None, pk[2 * b + 1])
                done = tr(ps[0:15, 384:512], E[:, 768 + 15 * b:783 + 15 * b], P, pk[5], e_zero, count=True)
                actv(A_[:, 384 * b:384 * b + 384], ps[:, 0:384], ACT.Copy, done, rd)
                ck = actv(A_[0:15, 768 + P * b:768 + P * (b + 1)], ps[0:15, 384:512], ACT.Copy)
                PS.give(pi, ck)
                cks.append(ck)
            EE.give(ei, done)
            heads[h] = [A_, ai, cks]

        def mixed(h):
            j, half, g = h // 2, h % 2, h // 8
            lo = 64 * half
            A_, ai, cks = heads.pop(h)
            if half == 0:
                heads["out"] = PO.take()
            (p1, p2), rd, oi = heads["out"]
            for b in range(2):
                v = VW[:, b, :, 64 * g:64 * g + 64]
                mm(p1[lo:lo + 64, T * b:T * b + T], v[:, 0, :], A_[:, 384 * b:384 * b + T],
                   rd if half + b == 0 else None, cks[b], vw_rdy, stop=False)
                done1 = mm(p1[lo:lo + 64, T * b + P:T * b + T], v[:, 1, :], A_[:, 384 * b + T:384 * b + 384], start=False, count=True)
            done = mm(p2[lo:lo + 64, 0:T], VC[:, 64 * g:64 * g + 64], A_[0:15, 768:1024], cmp_rdy, count=True)
            EA.give(ai, done)
            if half == 0:
                return
            z12 = arena[:, 3 * UNIT:5 * UNIT].rearrange("p (b n) -> p b n", b=2)[:, :, j * T:(j + 1) * T]
            tb, rd, bi = TB.take()
            tk = tt(dve, tb.rearrange("p (b t) -> p b t", b=2), p1.rearrange("p (b t) -> p b t", b=2), z12, ALU.mult,
                    done1, zs_rdy[1][j], zs_rdy[2][j], rd)
            tb2, rd2, bi2 = TC.take()
            tk2 = tt(dve, tb2[:, 0:T], p2[:, 0:T], ZS[0][:, j, :], ALU.mult, done, zs_rdy[0][j], rd2)
            PO.give(oi, tk2)
            yk = tt(pool, YN[:, j, :], tb[:, 0:T], tb[:, T:512], ALU.add, tk, free)
            TB.give(bi, yk)
            yk = tt(pool, YN[:, j, :], YN[:, j, :], tb2[:, 0:T], ALU.add, tk2, yk)
            TC.give(bi2, yk)
            y_rdy[j] = yk

        for t_ in range(19):
            if t_ % 2 == 0:
                next(zl, None)
            if t_ < 16:
                scores(t_)
            if t_ >= 3:
                mixed(t_ - 3)
            if 1 <= t_ < 17:
                weights(t_ - 1)
            if 2 <= t_ < 18:
                turned_weights(t_ - 2)
        assert next(zl, None) is None
        after = now()
        L.bufs, L.i = [b[:, :] for b in banks[0:3]], -1
        for r in (L, S, X, TA):
            r.readers = [after] * len(r.bufs)
        run(linear(a["b_out_w_2"], 0, D, YN, y_rdy, residual(mods[:, 112:120], mod_rdy[119])))

        free = now()
        r_ = root(h_rdy)
        s_out = sem("s_out")
        for c in range(8):
            tk = stt(U[:, c, :], H[:, c, :], V("final_g_2")[:, c:c + 1], rstd[:, :], ALU.mult, ALU.mult, r_, free)
            sp.dma(lambda e, c=c: e.dma_start(out[c * P:(c + 1) * P, :], U[:, c, :]), s_out, tk)
        sp.items.append(([(s_out, 128)] + [(s, 128) for s in s_br], None, None))

        block = ctx.enter_context(nc.Block())
        block.sync(lambda e: sp.emit(e))
        block.tensor(lambda e: pe.emit(e))
        block.vector(lambda e: dve.emit(e))
        block.scalar(lambda e: act.emit(e))
        block.gpsimd(lambda e: pool.emit(e))


def kernel(**inputs):
    import concourse.bacc as _bacc
    from concourse.bass_utils import run_bass_kernel_spmd as _run

    nc = _bacc.Bacc("TRN2", target_bir_lowering=False, num_devices=1)
    x = {k: np.asarray(v) for k, v in inputs.items()}
    cst, lvls, oh, rope = constants()
    vec, lam = vectors(x)
    arrays = {"vec": vec, "lam": lam, "cst": cst, "lvls": lvls, "oh": oh, "rope": rope, "xT": np.ascontiguousarray(x["x"][0].T),
              "ada_w1": x["ada_w_2"][0], "ada_w2": x["ada_w_2"][1]}
    for n in ("w_ada", "w1_gate", "w1_up", "w1_down", "w_in", "w_proj_a", "w_proj_b", "w_out", "w2_gate", "w2_up",
              "w2_down", "a_in_w_2", "a_out_w_2", "b_in_w_2", "b_out_w_2"):
        arrays[n] = x[n][0]
    for n in ("w_mq", "w_mk", "w_mv"):
        arrays[n] = x[n][0].reshape(1024, 256)
    for n in ("kv_w_2", "cmp_k_w1_2", "cmp_v_w1_2"):
        arrays[n] = x[n]
    feed, aps = {}, {}
    for n, v in arrays.items():
        v = np.ascontiguousarray(v)
        feed[f"in_{n}"] = v
        aps[n] = nc.dram_tensor(f"in_{n}", v.shape, F32, kind="ExternalInput").ap()
    out = nc.dram_tensor("out_T", (D, T), F32, kind="ExternalOutput").ap()
    scratch = nc.dram_tensor("bias_rows", (16, P, 384), F32, kind="Internal").ap()
    build(nc, aps, out, scratch)
    r = _run(nc, [feed], core_ids=[0])
    return np.ascontiguousarray(r.results[0]["out_T"].T)[None]
```
